# Optimizing a Trainium2 kernel written in Bass

```python
import math
import jax, jax.numpy as jnp
from jax import lax
import numpy as np

D_MODEL = 1024
BATCH = 1
SEQ = 512
DEPTH = 1

D_MIX = 2 * D_MODEL
D_CONV = D_MIX // 2
D_LRU = D_MIX - D_CONV
CONV_GROUPS = 8
LRU_HEADS = 8
LRU_HEAD_DIM = D_LRU // LRU_HEADS
CONV_KERNEL = 31
SHORT_CONV = 4
LRU_C = 8.0
D_IN = 3 * D_CONV + 2 * D_LRU
EPS = 1e-6


def rmsnorm(x, g):
    xf = x.astype(jnp.float32)
    y = xf * lax.rsqrt(jnp.mean(xf * xf, axis=-1, keepdims=True) + EPS)
    return (y * g.astype(jnp.float32)).astype(x.dtype)

def layernorm(x, g, b):
    xf = x.astype(jnp.float32)
    mu = jnp.mean(xf, axis=-1, keepdims=True)
    var = jnp.mean(jnp.square(xf - mu), axis=-1, keepdims=True)
    y = (xf - mu) * lax.rsqrt(var + EPS)
    return (y * g.astype(jnp.float32) + b.astype(jnp.float32)).astype(x.dtype)

def causal_depthwise_conv(v, w, b):
    k, ch = w.shape
    y = lax.conv_general_dilated(
        v, w.astype(v.dtype)[:, None, :], window_strides=(1,),
        padding=[(k - 1, 0)], dimension_numbers=("NWC", "WIO", "NWC"),
        feature_group_count=ch)
    return y + b.astype(v.dtype)

def linear_scan(a, bx):
    def step(h, inp):
        a_t, b_t = inp
        h = a_t * h + b_t
        return h, h
    h0 = jnp.zeros((a.shape[0], a.shape[2]), jnp.float32)
    _, hs = lax.scan(step, h0, (jnp.swapaxes(a, 0, 1), jnp.swapaxes(bx, 0, 1)))
    return jnp.swapaxes(hs, 0, 1)

def first_inputs(seed: int = 0) -> dict:
    key = jax.random.key(seed)
    ks = jax.random.split(key, 24)
    f32 = jnp.float32
    nrm = lambda k, s, sc: (jax.random.normal(k, s, f32) * sc)
    x = jax.random.normal(ks[0], (BATCH, SEQ, D_MODEL), f32)
    c = jax.random.normal(ks[1], (BATCH, D_MODEL), f32)
    norm_g = 1.0 + nrm(ks[2], (DEPTH, D_MODEL), 0.05)
    mod_w = nrm(ks[3], (DEPTH, D_MODEL, 3 * D_MODEL), 0.5 * D_MODEL ** -0.5)
    mod_b = nrm(ks[4], (DEPTH, 3 * D_MODEL), 0.02)
    w_in = nrm(ks[5], (DEPTH, D_MODEL, D_IN), D_MODEL ** -0.5)
    dw_w = nrm(ks[6], (DEPTH, CONV_KERNEL, D_CONV), CONV_KERNEL ** -0.5)
    dw_b = nrm(ks[7], (DEPTH, D_CONV), 0.02)
    cln_g = 1.0 + nrm(ks[8], (DEPTH, D_CONV), 0.05)
    cln_b = nrm(ks[9], (DEPTH, D_CONV), 0.02)
    pw2_w = nrm(ks[10], (DEPTH, D_CONV, D_CONV), D_CONV ** -0.5)
    pw2_b = nrm(ks[11], (DEPTH, D_CONV), 0.02)
    sc_w = nrm(ks[12], (DEPTH, SHORT_CONV, D_LRU), SHORT_CONV ** -0.5)
    sc_b = nrm(ks[13], (DEPTH, D_LRU), 0.02)
    wr = nrm(ks[14], (DEPTH, LRU_HEADS, LRU_HEAD_DIM, LRU_HEAD_DIM), LRU_HEAD_DIM ** -0.5)
    br = nrm(ks[15], (DEPTH, D_LRU), 0.02)
    wi = nrm(ks[16], (DEPTH, LRU_HEADS, LRU_HEAD_DIM, LRU_HEAD_DIM), LRU_HEAD_DIM ** -0.5)
    bi = nrm(ks[17], (DEPTH, D_LRU), 0.02)
    a0 = jax.random.uniform(ks[18], (DEPTH, D_LRU), f32, 0.9, 0.999)
    s = a0 ** (1.0 / LRU_C)
    lam = jnp.log(s) - jnp.log1p(-s)
    w_out = nrm(ks[19], (DEPTH, D_MIX, D_MODEL), D_MIX ** -0.5)
    final_g = 1.0 + nrm(ks[20], (D_MODEL,), 0.05)
    return {"x": x, "c": c, "norm_g": norm_g, "mod_w": mod_w, "mod_b": mod_b,
            "w_in": w_in, "dw_w": dw_w, "dw_b": dw_b, "cln_g": cln_g, "cln_b": cln_b,
            "pw2_w": pw2_w, "pw2_b": pw2_b, "sc_w": sc_w, "sc_b": sc_b,
            "wr": wr, "br": br, "wi": wi, "bi": bi, "lam": lam,
            "w_out": w_out, "final_g": final_g}

def first_block(x, c, norm_g, mod_w, mod_b, w_in, dw_w, dw_b, cln_g, cln_b,
              pw2_w, pw2_b, sc_w, sc_b, wr, br, wi, bi, lam, w_out, final_g):
    bsz, seq, _ = x.shape
    c_act = jax.nn.silu(c)
    for l in range(DEPTH):
        mod = c_act @ mod_w[l] + mod_b[l]
        shift, scale, gate = jnp.split(mod, 3, axis=-1)
        h = rmsnorm(x, norm_g[l]) * (1.0 + scale[:, None, :]) + shift[:, None, :]

        u = h @ w_in[l]
        cv, cg, cs, lx, ls = jnp.split(
            u, [D_CONV, 2 * D_CONV, 3 * D_CONV, 3 * D_CONV + D_LRU], axis=-1)

        v = cv * jax.nn.sigmoid(cg)
        v = causal_depthwise_conv(v, dw_w[l], dw_b[l])
        v = jax.nn.silu(layernorm(v, cln_g[l], cln_b[l]))
        v = v @ pw2_w[l] + pw2_b[l]
        y_conv = v * jax.nn.silu(cs)

        xs = causal_depthwise_conv(lx, sc_w[l], sc_b[l])
        xh = xs.reshape(bsz, seq, LRU_HEADS, LRU_HEAD_DIM)
        r = jax.nn.sigmoid(jnp.einsum("bshd,hde->bshe", xh, wr[l]).reshape(bsz, seq, D_LRU) + br[l])
        i = jax.nn.sigmoid(jnp.einsum("bshd,hde->bshe", xh, wi[l]).reshape(bsz, seq, D_LRU) + bi[l])
        log_a = (-LRU_C * r.astype(jnp.float32)
                 * jax.nn.softplus(-lam[l].astype(jnp.float32)))
        a = jnp.exp(log_a)
        mult = jnp.sqrt(-jnp.expm1(2.0 * log_a))
        bx = mult * (i * xs).astype(jnp.float32)
        hs = linear_scan(a, bx).astype(x.dtype)
        y_lru = hs * jax.nn.silu(ls)

        y = jnp.concatenate([y_conv, y_lru], axis=-1) @ w_out[l]
        x = x + (1.0 + gate[:, None, :]) * y
    return rmsnorm(x, final_g)


N_META = 16
GRID_W = 64
Q_BLOCK = 128
ROPE_THETA = 10000.0

MLA_HEADS = 4
Q_LORA = 256
KV_LORA = 128
NOPE_DIM = 128
ROPE_DIM = 64
V_DIM = 128
QK_DIM = NOPE_DIM + ROPE_DIM

GQA_HEADS = 4
GQA_KV_HEADS = 2
GQA_DIM = 128
AXIAL_HALF = GQA_DIM // 2

MLA_WIDTH = MLA_HEADS * V_DIM
GQA_WIDTH = GQA_HEADS * GQA_DIM
MIX_WIDTH = MLA_WIDTH + GQA_WIDTH

IN_SPLITS = (Q_LORA, KV_LORA, ROPE_DIM, GQA_HEADS * GQA_DIM, GQA_KV_HEADS * GQA_DIM, GQA_KV_HEADS * GQA_DIM)
IN_COLS = sum(IN_SPLITS)
IN_OFFSETS = tuple(int(o) for o in np.cumsum(IN_SPLITS)[:-1])

N_EXPERTS = 32
TOP_K = 4
D_FF = D_MODEL
SWIGLU_LIMIT = 7.0
SWIGLU_ALPHA = 1.702

RMS_EPS = 1e-6
LN_EPS = 1e-5
DEEPNORM_ALPHA = (2.0 * DEPTH) ** 0.25
DEEPNORM_BETA = (8.0 * DEPTH) ** -0.25


def _rmsnorm(x, g):
    xf = x.astype(jnp.float32)
    y = xf * lax.rsqrt(jnp.mean(xf * xf, axis=-1, keepdims=True) + RMS_EPS)
    return (y * g.astype(jnp.float32)).astype(x.dtype)

def _layernorm(x, g, b):
    xf = x.astype(jnp.float32)
    mu = jnp.mean(xf, axis=-1, keepdims=True)
    var = jnp.mean(jnp.square(xf - mu), axis=-1, keepdims=True)
    y = (xf - mu) * lax.rsqrt(var + LN_EPS)
    return (y * g.astype(jnp.float32) + b.astype(jnp.float32)).astype(x.dtype)

def _rope_cos_sin(pos, dim):
    inv = ROPE_THETA ** (-jnp.arange(0, dim, 2, dtype=jnp.float32) / dim)
    ang = pos.astype(jnp.float32)[:, None] * inv[None, :]
    return jnp.cos(ang)[:, None, :], jnp.sin(ang)[:, None, :]

def _rotate(x, cos, sin):
    xf = x.astype(jnp.float32)
    x1, x2 = jnp.split(xf, 2, axis=-1)
    return jnp.concatenate([x1 * cos - x2 * sin, x1 * sin + x2 * cos], axis=-1).astype(x.dtype)

def _attend(q, k, v, scale):
    s = jnp.einsum('bqkgd,bskd->bkgqs', q, k).astype(jnp.float32) * scale
    p = jax.nn.softmax(s, axis=-1).astype(v.dtype)
    return jnp.einsum('bkgqs,bskd->bqkgd', p, v)

def _blocked_attention(q, k, v, scale):
    B, L, H, Dq = q.shape
    Hk = k.shape[2]
    G = H // Hk
    Dv = v.shape[-1]
    q = q.reshape(B, L, Hk, G, Dq)
    o_meta = _attend(q[:, :N_META], k, v, scale)
    n_blk = (L - N_META) // Q_BLOCK
    qb = q[:, N_META:].reshape(B, n_blk, Q_BLOCK, Hk, G, Dq).transpose(1, 0, 2, 3, 4, 5)
    ob = lax.map(lambda qi: _attend(qi, k, v, scale), qb)
    ob = ob.transpose(1, 0, 2, 3, 4, 5).reshape(B, L - N_META, Hk, G, Dv)
    return jnp.concatenate([o_meta, ob], axis=1).reshape(B, L, H, Dv)

def _mixer(h, pos_1d, row, col, w_in, g_q_a, w_q_b, g_kv_a, w_kv_b, g_q_gqa, g_k_gqa, g_o_mla, g_o_gqa, w_o):
    B, L, _ = h.shape
    z = jnp.einsum('bld,dc->blc', h, w_in)
    q_a, kv_a, k_pe, q_g, k_g, v_g = jnp.split(z, IN_OFFSETS, axis=-1)

    cos1, sin1 = _rope_cos_sin(pos_1d, ROPE_DIM)
    q = jnp.einsum('blr,rc->blc', _rmsnorm(q_a, g_q_a), w_q_b).reshape(B, L, MLA_HEADS, QK_DIM)
    q_m = jnp.concatenate([q[..., :NOPE_DIM], _rotate(q[..., NOPE_DIM:], cos1, sin1)], axis=-1)
    kv = jnp.einsum('blr,rc->blc', _rmsnorm(kv_a, g_kv_a), w_kv_b).reshape(B, L, MLA_HEADS, NOPE_DIM + V_DIM)
    k_rot = _rotate(k_pe[:, :, None, :], cos1, sin1)
    k_m = jnp.concatenate([kv[..., :NOPE_DIM], jnp.broadcast_to(k_rot, (B, L, MLA_HEADS, ROPE_DIM))], axis=-1)
    v_m = kv[..., NOPE_DIM:]
    o_mla = _blocked_attention(q_m, k_m, v_m, QK_DIM ** -0.5).reshape(B, L, MLA_WIDTH)

    cos_r, sin_r = _rope_cos_sin(row, AXIAL_HALF)
    cos_c, sin_c = _rope_cos_sin(col, AXIAL_HALF)

    def axial(t):
        return jnp.concatenate([_rotate(t[..., :AXIAL_HALF], cos_r, sin_r),
                                _rotate(t[..., AXIAL_HALF:], cos_c, sin_c)], axis=-1)

    qg = axial(_rmsnorm(q_g.reshape(B, L, GQA_HEADS, GQA_DIM), g_q_gqa))
    kg = axial(_rmsnorm(k_g.reshape(B, L, GQA_KV_HEADS, GQA_DIM), g_k_gqa))
    vg = v_g.reshape(B, L, GQA_KV_HEADS, GQA_DIM)
    o_gqa = _blocked_attention(qg, kg, vg, GQA_DIM ** -0.5).reshape(B, L, GQA_WIDTH)

    o = jnp.concatenate([_rmsnorm(o_mla, g_o_mla), _rmsnorm(o_gqa, g_o_gqa)], axis=-1)
    return jnp.einsum('blc,cd->bld', o, w_o)

def _clamped_swiglu(hgu):
    x_glu = jnp.minimum(hgu[..., ::2], SWIGLU_LIMIT)
    x_lin = jnp.clip(hgu[..., 1::2], -SWIGLU_LIMIT, SWIGLU_LIMIT)
    return x_glu * jax.nn.sigmoid(SWIGLU_ALPHA * x_glu) * (x_lin + 1.0)

def _moe_sequence(h, w_router, b_router, w_gate_up, b_gate_up, w_down, b_down):
    L = h.shape[0]
    logits = (jnp.einsum('ld,de->le', h, w_router) + b_router).astype(jnp.float32)
    top_val, top_idx = lax.top_k(logits, TOP_K)
    gates = jax.nn.softmax(top_val, axis=-1).astype(h.dtype)
    flat_e = top_idx.reshape(-1)
    order = jnp.argsort(flat_e)
    tok = order // TOP_K
    e_sorted = flat_e[order]
    group_sizes = jnp.bincount(flat_e, length=N_EXPERTS).astype(jnp.int32)
    xs = h[tok]
    hgu = lax.ragged_dot(xs, w_gate_up, group_sizes) + b_gate_up[e_sorted]
    act = _clamped_swiglu(hgu)
    out = lax.ragged_dot(act, w_down, group_sizes) + b_down[e_sorted]
    out = out * gates.reshape(-1)[order][:, None]
    return jax.ops.segment_sum(out, tok, num_segments=L)

def second_inputs(seed: int = 0) -> dict:
    key = jax.random.key(seed)
    ks = jax.random.split(key, 28)
    f32 = jnp.float32

    def nrm(k, shape, scale):
        return jax.random.normal(k, shape, f32) * scale

    def gain(k, shape):
        return 1.0 + 0.05 * jax.random.normal(k, shape, f32)

    Dp = DEPTH
    return {
        'x': jax.random.normal(ks[0], (BATCH, SEQ, D_MODEL), f32),
        'meta_tokens': nrm(ks[1], (N_META, D_MODEL), 1.0),
        'ln_emb_g': gain(ks[2], (D_MODEL,)),
        'ln_emb_b': nrm(ks[3], (D_MODEL,), 0.02),
        'w_in': nrm(ks[4], (Dp, D_MODEL, IN_COLS), D_MODEL ** -0.5),
        'g_q_a': gain(ks[5], (Dp, Q_LORA)),
        'w_q_b': nrm(ks[6], (Dp, Q_LORA, MLA_HEADS * QK_DIM), Q_LORA ** -0.5),
        'g_kv_a': gain(ks[7], (Dp, KV_LORA)),
        'w_kv_b': nrm(ks[8], (Dp, KV_LORA, MLA_HEADS * (NOPE_DIM + V_DIM)), KV_LORA ** -0.5),
        'g_q_gqa': gain(ks[9], (Dp, GQA_DIM)),
        'g_k_gqa': gain(ks[10], (Dp, GQA_DIM)),
        'g_o_mla': gain(ks[11], (Dp, MLA_WIDTH)),
        'g_o_gqa': gain(ks[12], (Dp, GQA_WIDTH)),
        'w_o': nrm(ks[13], (Dp, MIX_WIDTH, D_MODEL), DEEPNORM_BETA * MIX_WIDTH ** -0.5),
        'ln1_g': gain(ks[14], (Dp, D_MODEL)),
        'ln1_b': nrm(ks[15], (Dp, D_MODEL), 0.02),
        'w_router': nrm(ks[16], (Dp, D_MODEL, N_EXPERTS), D_MODEL ** -0.5),
        'b_router': nrm(ks[17], (Dp, N_EXPERTS), 0.01),
        'w_gate_up': nrm(ks[18], (Dp, N_EXPERTS, D_MODEL, 2 * D_FF), D_MODEL ** -0.5),
        'b_gate_up': nrm(ks[19], (Dp, N_EXPERTS, 2 * D_FF), 0.02),
        'w_down': nrm(ks[20], (Dp, N_EXPERTS, D_FF, D_MODEL), DEEPNORM_BETA * D_FF ** -0.5),
        'b_down': nrm(ks[21], (Dp, N_EXPERTS, D_MODEL), 0.02),
        'ln2_g': gain(ks[22], (Dp, D_MODEL)),
        'ln2_b': nrm(ks[23], (Dp, D_MODEL), 0.02),
    }

def second_block(x, meta_tokens, ln_emb_g, ln_emb_b, w_in, g_q_a, w_q_b, g_kv_a, w_kv_b,
              g_q_gqa, g_k_gqa, g_o_mla, g_o_gqa, w_o, ln1_g, ln1_b,
              w_router, b_router, w_gate_up, b_gate_up, w_down, b_down, ln2_g, ln2_b):
    B, S, D = x.shape
    meta = jnp.broadcast_to(meta_tokens.astype(x.dtype)[None], (B, N_META, D))
    h = _layernorm(jnp.concatenate([meta, x], axis=1), ln_emb_g, ln_emb_b)
    L = S + N_META

    rows = S // GRID_W
    pos_1d = jnp.arange(L, dtype=jnp.int32)
    row = jnp.concatenate([jnp.full((N_META,), -1, jnp.int32), jnp.repeat(jnp.arange(rows, dtype=jnp.int32), GRID_W)])
    col = jnp.concatenate([jnp.arange(N_META, dtype=jnp.int32), jnp.tile(jnp.arange(GRID_W, dtype=jnp.int32), rows)])

    for i in range(DEPTH):
        mix = _mixer(h, pos_1d, row, col, w_in[i], g_q_a[i], w_q_b[i], g_kv_a[i], w_kv_b[i],
                     g_q_gqa[i], g_k_gqa[i], g_o_mla[i], g_o_gqa[i], w_o[i])
        h = _layernorm(DEEPNORM_ALPHA * h + mix, ln1_g[i], ln1_b[i])
        moe = lax.map(lambda hs: _moe_sequence(hs, w_router[i], b_router[i], w_gate_up[i],
                                               b_gate_up[i], w_down[i], b_down[i]), h)
        h = _layernorm(DEEPNORM_ALPHA * h + moe, ln2_g[i], ln2_b[i])

    return h[:, N_META:]


def setup_inputs(seed=0):
    out = dict(first_inputs(seed))
    for name, value in second_inputs(seed + 1).items():
        if name != "x":
            out[name + "_2"] = value
    return out


def reference(
    x, c, norm_g, mod_w, mod_b, w_in, dw_w, dw_b, cln_g, cln_b, pw2_w, pw2_b, sc_w, sc_b, wr,
    br, wi, bi, lam, w_out, final_g, meta_tokens_2, ln_emb_g_2, ln_emb_b_2, w_in_2, g_q_a_2,
    w_q_b_2, g_kv_a_2, w_kv_b_2, g_q_gqa_2, g_k_gqa_2, g_o_mla_2, g_o_gqa_2, w_o_2, ln1_g_2,
    ln1_b_2, w_router_2, b_router_2, w_gate_up_2, b_gate_up_2, w_down_2, b_down_2, ln2_g_2,
    ln2_b_2,
):
    x = first_block(
        x, c, norm_g, mod_w, mod_b, w_in, dw_w, dw_b, cln_g, cln_b, pw2_w, pw2_b, sc_w, sc_b,
        wr, br, wi, bi, lam, w_out, final_g,
    )
    return second_block(
        x, meta_tokens_2, ln_emb_g_2, ln_emb_b_2, w_in_2, g_q_a_2, w_q_b_2, g_kv_a_2, w_kv_b_2,
        g_q_gqa_2, g_k_gqa_2, g_o_mla_2, g_o_gqa_2, w_o_2, ln1_g_2, ln1_b_2, w_router_2,
        b_router_2, w_gate_up_2, b_gate_up_2, w_down_2, b_down_2, ln2_g_2, ln2_b_2,
    )


_drawn_inputs = setup_inputs


def setup_inputs(seed=0):
    import zlib

    import numpy as np

    out = dict(_drawn_inputs(seed))
    spreads = {}
    factors = {'dw_b': 4.444,
     'cln_b': 6.888,
     'pw2_b': 3.803,
     'br': 8.0,
     'bi': 4.67,
     'g_q_a_2': 4.67,
     'g_q_gqa_2': 5.606,
     'g_k_gqa_2': 5.089,
     'b_router_2': 3.538,
     'b_gate_up_2': 8.0,
     'b_down_2': 6.41,
     'ln2_b_2': 2.853}
    for name, (base, spread) in spreads.items():
        noise = np.random.default_rng([zlib.crc32(name.encode()), seed]).standard_normal(out[name].shape)
        drawn = base * np.exp(spread * noise) if base else spread * noise
        out[name] = __import__('jax').numpy.asarray(drawn.astype(out[name].dtype))
    for name, factor in factors.items():
        out[name] = (out[name] * factor).astype(out[name].dtype)
    return out
```

```python
from contextlib import ExitStack
import math

import concourse.bass as bass
from concourse import mybir

F32 = mybir.dt.float32
I32 = mybir.dt.int32
U32 = mybir.dt.uint32
ALU = mybir.AluOpType
ACT = mybir.ActivationFunctionType
AX = mybir.AxisListType

P = 128
D = 1024
KD = D // P
T = 512
TC = T // P
META = 16
L = T + META
LC = TC + 1
TAPS = 31
STAPS = 4
EPS_RMS = 1e-6
EPS_LN1 = 1e-6
EPS_LN2 = 1e-5
ALPHA = 2.0 ** 0.25
E = 32
TOPK = 4
HM = 4
NOPE, ROPE = 128, 64
LIMIT = 7.0
SWALPHA = 1.702
NONE = 4096.0
ITEMS = 64

CHAN = {}
_at = 0
for _name, _n in (("c", 8), ("norm_g", 8), ("mod_b", 16), ("cln_g", 8), ("cln_b", 8), ("pw2_b", 8), ("sc_b", 8),
                  ("br", 8), ("bi", 8), ("lam", 8), ("dw_b", 8), ("sc_w", 8 * STAPS), ("dw_w", 8 * TAPS),
                  ("g_q_a", 2), ("g_kv_a", 1), ("g_o", 8)):
    CHAN[_name] = (_at, _n)
    _at += _n
NCHAN = _at

CONST = {}
_at = 0
for _name, _n in (("ident", P), ("ones", P), ("mean", P), ("before", P), ("iota", P), ("over_e", 96), ("over_t", 96),
                  ("dst", 16), ("part1", 1), ("tok", TC), ("eps6", 1), ("eps5", 1), ("hln2", 1), ("tiny", 1), ("one", 1)):
    CONST[_name] = (_at, _n)
    _at += _n
NCONST = _at

ROWS = {"gate_b": 0, "final_g": 1024, "ln_emb_g": 2048, "ln_emb_b": 3072, "ln1_g": 4096, "ln1_b": 5120, "g_qk": 6144,
        "b_router": 6400, "ln2_g": 6432, "ln2_b": 7456}
NROWS = 8480

RING1 = 6
TILE = 2048
N_MOD, N_IN, N_GATE, N_PW2, N_OUT, N_IN2, N_Q, N_KV, N_O = 8, 20, 4, 4, 8, 6, 1, 1, 4
T_IN = N_MOD
T_GATE = T_IN + N_IN
T_PW2 = T_GATE + N_GATE
T_OUT = T_PW2 + N_PW2
T_IN2 = T_OUT + N_OUT
T_Q = T_IN2 + N_IN2
T_KV = T_Q + N_Q
T_O = T_KV + N_KV
N_PHASE1 = T_O + N_O
EXPERT_TILES = 12


class Steps:

    def __init__(self, eng, sem):
        self.eng, self.sem, self.n = eng, sem, 0

    def go(self, ins):
        self.n += 1
        ins.then_inc(self.sem, 1)

    def wait(self):
        self.eng.wait_ge(self.sem, self.n)

    def link(self, ins):
        self.go(ins)
        self.wait()


def program(nc, a, out, h1_dram, y_dram):
    with ExitStack() as ctx:
        sems = {}

        def sig(name):
            if name not in sems:
                sems[name] = ctx.enter_context(nc.semaphore(name))
            return sems[name]

        def sb(name, shape, dt=F32):
            return ctx.enter_context(nc.sbuf_tensor(name, shape, dt))

        ps = ctx.enter_context(nc.psum_tensor("ps", [P, 8, 512], F32))
        ring = sb("ring", [P, RING1, TILE])
        chan = sb("chan", [P, NCHAN])
        const = sb("const", [P, NCONST])
        rows = sb("rows", [P, 3, D])
        small = sb("small", [P, 512])
        ARENA = 35904
        arena = sb("arena", [P, ARENA])

        def ch(name, k=0, n=1):
            o = CHAN[name][0] + k
            return chan[:, o:o + n]

        def cst(name, lo=0, hi=None, p=P):
            o, n = CONST[name]
            return const[0:p, o + lo:o + (n if hi is None else hi)]

        class Area:
            def __init__(self, at=0):
                self.at = at

            def take(self, *shape):
                n = math.prod(shape)
                assert self.at + n <= ARENA, (self.at, n)
                v = arena[:, self.at:self.at + n]
                self.at += n
                if len(shape) == 2:
                    v = v.rearrange("p (a b) -> p a b", b=shape[1])
                if len(shape) == 3:
                    v = v.rearrange("p (a b c) -> p a b c", b=shape[1], c=shape[2])
                return v

        m1 = Area()
        hT = m1.take(KD, T)
        xtok = m1.take(TC, D)
        v = m1.take(KD, T + TAPS - 1)
        vc = m1.take(KD, T)
        ylru = m1.take(KD, T)
        sgt = m1.take(2, T)
        lxb = m1.take(2, T + STAPS - 1)
        xs = m1.take(2, T)
        lsil = m1.take(2, T)
        lru = m1.take(4, T)
        gates_w = m1.take(2 * KD, P)
        crep = m1.take(KD, P)
        gate1 = m1.take(D)
        rep = m1.take(2, T)
        scs = Area(2 * KD * T).take(KD, T)
        m2 = Area(0)
        qnT = m2.take(HM, T)
        rtmp = m2.take(2, 384)
        tab = m2.take(LC, 192)
        assert m2.at <= KD * T
        x2 = xtok
        m2 = Area(KD * T)
        qanT = m2.take(2, T)
        kvanT = m2.take(L)
        krT = m2.take(L)
        qpT = m2.take(2, T)
        assert m2.at <= KD * T + TC * D
        m2 = Area(KD * T + TC * D)
        h = m2.take(LC, D)
        after_h = m2.at
        hT2 = m2.take(KD, L)
        zA = m2.take(LC, 448)
        zB = m2.take(TC, 512)
        zC = m2.take(LC, 512)
        after_z = m2.at
        vm = m2.take(LC, 512)
        knT = m2.take(HM, L)
        qgT = m2.take(4, T)
        kgT = m2.take(2, L)
        junk = m2.take(D)
        m2.at -= D
        pr = m2.take(2, L)
        pT = m2.take(2, LC * P)
        rot = m2.take(6 * P)
        pe_rot = m2.take(4 * ROPE + P)
        wrouter = m2.take(KD, E)
        o_tok = Area(after_h).take(TC, D)
        oT = Area(0).take(KD, T)
        h1 = h
        h1T = hT2
        m3 = Area(0)
        xe = m3.take(D)
        ysb = m3.take(D)
        actv = m3.take(D)
        xT = m3.take(KD, P)
        aT = m3.take(KD, P)
        glu = m3.take(2, T)
        gsig = m3.take(2, T)
        oh = m3.take(TC, P)
        eo = m3.take(P)
        posm = m3.take(TC, E)
        dst = m3.take(TC, E)
        assert m3.at <= KD * T + TC * D
        ext = Area(after_h).take(6, TILE)
        m3 = Area(after_h + 6 * TILE)
        bgu = m3.take(2 * D)
        assert m3.at <= ARENA
        bdown = m3.take(D)
        mk = m3.take(TC * TOPK, E)
        mkt = m3.take(TC * TOPK, E)
        routed = m3.take(TC, E)
        gmat = m3.take(TC, E)
        logit = m3.take(TC, E)
        gT = m3.take(T)
        flags = m3.take(E, 3)
        fsum = m3.take(96)
        feq = m3.take(96)
        ftmp = m3.take(96)
        evb = m3.take(2, P)
        elist = m3.take(ITEMS)
        tlist = m3.take(ITEMS)
        v8 = m3.take(TC, 8)
        if4 = m3.take(TC * TOPK)
        gates = m3.take(TC, TOPK)
        cur = m3.take(TC)
        dcur = m3.take(TC, 2)
        assert m3.at <= m2.at - KD * E, (m3.at, m2.at)
        ybuf = [ext[:, q // 2, (q % 2) * D:(q % 2 + 1) * D] for q in range(12)]
        ybuf += [ring[:, q // 2, (q % 2) * D:(q % 2 + 1) * D] for q in range(4)]

        cols = {}
        used = [0]

        def col(name, n=None):
            if name not in cols:
                cols[name] = (used[0], n)
                used[0] += n
                assert used[0] <= 512
            o, n = cols[name]
            return small[:, o:o + n]

        c_act, c_sig, lam_abs, lam_e, lam_neg = (col(n, 8) for n in ("c_act", "c_sig", "lam_abs", "lam_e", "lam_neg"))
        rate, nrate, lam_z, shift, gain = (col(n, 8) for n in ("rate", "nrate", "lam_z", "shift", "gain"))
        x2_ss, x2_ln, x2_rstd = (col(n, TC) for n in ("x2_ss", "x2_ln", "x2_rstd"))
        emb_mean, emb_var, emb_ln, emb_rstd = (col(n, LC) for n in ("emb_mean", "emb_var", "emb_ln", "emb_rstd"))
        bn_part = col("bn_part", 12 * LC).rearrange("p (t s) -> p t s", t=LC)
        bn_mv = col("bn_mv", 2 * LC).rearrange("p (t s) -> p t s", t=LC)
        z_ss, z_ln = col("z_ss", 9 * LC), col("z_ln", 9 * LC)
        nmaxs, psums = col("nmax", 32), col("psum", 32)
        o_ss, o_ln, o_rstd = (col(n, 2 * TC) for n in ("o_ss", "o_ln", "o_rstd"))
        ln_var, ln_ln, ln_rstd = (col(n, TC) for n in ("ln_var", "ln_ln", "ln_rstd"))
        nv0, gsum = col("nv0", TC), col("gsum", TC)
        ev, tv = col("ev", 1), col("tv", 1)
        i8 = sb("i8", [P, TC, 8], U32)
        idx_g = sb("idx_g", [P, 1], I32)
        idx_2 = sb("idx_2", [P, 1], I32)
        idx_s = sb("idx_s", [P, 1], I32)
        eint = sb("eint", [1, ITEMS], I32)
        nint = sb("nint", [1, 1], I32)

        def rows_of(t):
            return P if t < TC else META

        ONE = cst("one")
        IDENT = cst("ident")

        tile_ready = [sig(f"tile{s}_ready") for s in range(EXPERT_TILES)]

        def wait_tile(eng, n):
            eng.wait_ge(tile_ready[n % RING1], 16 * (n // RING1 + 1))

        def tile(n):
            return ring[:, n % RING1, :]

        def last_use(n):
            if n < T_IN:
                return sig("mod_used"), n + 1
            if n < T_GATE:
                return sig("u_ready"), 2 * (n - T_IN) + 2
            if n < T_PW2:
                return sig("gate_used"), n - T_GATE + 1
            if n < T_OUT:
                return sig("pw2_ready"), 2 * (n - T_PW2) + 2
            if n < T_IN2:
                return sig("out_used"), n - T_OUT + 1
            if n < T_Q:
                return sig("z_ready"), (LC, LC + TC, 2 * LC + TC)[(n - T_IN2) // 2]
            if n == T_Q:
                return sig("qp_ps"), TC
            if n == T_KV:
                return sig("vm_ps"), LC
            return sig("o_used"), n - T_O + 1

        UNITS = [(hh, qt) for hh in range(8) for qt in range(TC)]
        loads_before = [len([n for n in range(N_PHASE1) if n % RING1 == s]) for s in range(RING1)] + [0] * 6

        def wait_alone(eng, sem, value):
            eng.wait_ge(sig("list_ready"), 1)
            eng.wait_ge(sem, value)
            eng.wait_ge(sig("list_ready"), 2)

        block = ctx.enter_context(nc.Block())

        @block.sync
        def _(sp):
            sp.dma_start(chan[:], a["chan"]).then_inc(sig("chan_in"), 16)
            sp.dma_start(const[:], a["const"]).then_inc(sig("const_in"), 16)

            def load(n, dst, src):
                if n >= RING1:
                    sp.wait_ge(*last_use(n - RING1))
                sp.dma_start(dst, src).then_inc(tile_ready[n % RING1], 16)

            for k in range(N_MOD):
                load(k, tile(k), a["mod_w"][k * P:(k + 1) * P, 0:2 * D])
            for n in range(N_IN):
                load(T_IN + n, tile(T_IN + n), a["w_in"][n])
            for n in range(N_GATE):
                load(T_GATE + n, tile(T_GATE + n).rearrange("p (k n) -> p k n", k=2),
                     a["mod_w"][n * 2 * P:(n + 1) * 2 * P, 2 * D:].rearrange("(k p) n -> p k n", p=P))
            for n in range(N_PW2):
                load(T_PW2 + n, tile(T_PW2 + n).rearrange("p (k n) -> p k n", k=KD),
                     a["pw2_w"][:, n * 256:(n + 1) * 256].rearrange("(k p) n -> p k n", p=P))
            for n in range(N_OUT):
                half, g = n // 4, n % 4
                load(T_OUT + n, tile(T_OUT + n).rearrange("p (k n) -> p k n", k=4),
                     a["w_out"][g * 512:(g + 1) * 512, half * 512:(half + 1) * 512].rearrange("(k p) n -> p k n", p=P))
            for n in range(N_IN2):
                g, kk = n // 2, n % 2
                lo, w = ((0, 448), (448, 512), (960, 512))[g]
                load(T_IN2 + n, tile(T_IN2 + n)[:, 0:4 * w].rearrange("p (k n) -> p k n", k=4),
                     a["w_in_2"][kk * 512:(kk + 1) * 512, lo:lo + w].rearrange("(k p) n -> p k n", p=P))
            load(T_Q, tile(T_Q)[:, 0:1536].rearrange("p (k n) -> p k n", k=2), a["w_q_b_2"].rearrange("(k p) n -> p k n", p=P))
            load(T_KV, tile(T_KV)[:, 0:D], a["w_kv_b_2"][:, :])
            for n in range(N_O):
                half, g = n // 2, n % 2
                load(T_O + n, tile(T_O + n).rearrange("p (k n) -> p k n", k=4),
                     a["w_o_2"][g * 512:(g + 1) * 512, half * 512:(half + 1) * 512].rearrange("(k p) n -> p k n", p=P))
            def slot(j):
                return (ring[:, j, :] if j < RING1 else ext[:, j - RING1, :]).rearrange("p (k n) -> p k n", k=2)

            def expert_tile(j, e):
                if j < 8:
                    half, g = j // 4, j % 4
                    src = a["w_gate_up_2"][bass.ds(e, 1), g * 256:(g + 1) * 256, half * D:(half + 1) * D]
                else:
                    src = a["w_down_2"][bass.ds(e, 1), (j - 8) * 256:(j - 7) * 256, :]
                return src.rearrange("o (k p) n -> p (o k) n", p=P)

            for j in range(EXPERT_TILES):
                if j < RING1:
                    sp.wait_ge(*last_use(max(n for n in range(N_PHASE1) if n % RING1 == j)))
                elif j == RING1:
                    sp.wait_ge(sig("logits_ps"), 1)
                sp.dma_start(slot(j), expert_tile(j, 0)).then_inc(tile_ready[j], 16)
            sp.wait_ge(sig("list_ready"), 3)
            n_items = sp.value_load(nint[0:1, 0:1], min_val=E, max_val=E + 16)
            with sp.Fori(1, n_items) as i:
                e = sp.value_load(eint[0:1, bass.ds(i, 1)], min_val=0, max_val=E - 1)
                for j in range(EXPERT_TILES):
                    wait_alone(sp, sig("moe_used"), (i - 1) * EXPERT_TILES + (j + 1))
                    sp.dma_start(slot(j), expert_tile(j, e)).then_inc(tile_ready[j], 16)
            wait_alone(sp, sig("scattered"), n_items * 16)
            for t in range(TC):
                for k in range(TOPK):
                    sp.dma_start(ybuf[t * TOPK + k], y_dram[k * T + t * P:k * T + (t + 1) * P, :]).then_inc(sig(f"y{t}_in"), 16)
            for t in range(TC):
                sp.wait_ge(sig("out_ready"), t + 1)
                sp.dma_start(out[t * P:(t + 1) * P, :], h1[:, t, :]).then_inc(sig("out_written"), 16)
            sp.wait_ge(sig("out_written"), 16 * TC)

        @block.gpsimd
        def _(pool):
            nc.gpsimd.memset(v[:, :, 0:TAPS - 1], 0.0).then_inc(sig("pads_zero"), 1)
            nc.gpsimd.memset(lxb[:, :, 0:STAPS - 1], 0.0).then_inc(sig("pads_zero"), 1)
            pool.dma_start(wrouter, a["w_router_2"].rearrange("(k p) e -> p k e", p=P)).then_inc(sig("router_in"), 16)
            pool.wait_ge(sig("u_ready"), 2 * N_IN)
            pool.dma_start(tab[:, 0:TC, :], a["tab"][0:T, :].rearrange("(t p) n -> p t n", p=P)).then_inc(sig("tab_in"), 16)
            pool.dma_start(tab[0:META, TC, :], a["tab"][T:L, :]).then_inc(sig("tab_in"), 16)
            pool.wait_ge(sig("out_used"), N_OUT)
            pool.dma_start(h[0:META, TC, :], a["meta_tokens_2"][:, :]).then_inc(sig("meta_in"), 16)

            def load_rows(dst, name, n, signal):
                pool.dma_start(dst, a["rows"][:, ROWS[name]:ROWS[name] + n].partition_broadcast(P)).then_inc(signal, 16)

            pool.wait_ge(sig("h_ready"), LC)
            load_rows(rows[:, 2, 0:2 * P + E], "g_qk", 2 * P + E, sig("rows2_in"))
            load_rows(rows[:, 0, :], "ln1_g", D, sig("rows2_in"))
            load_rows(rows[:, 1, :], "ln1_b", D, sig("rows2_in"))
            pool.wait_ge(sig("o_taken"), 8 * TC)
            pool.dma_start(bgu[0:E, :], a["b_gate_up_2"][:, :]).then_inc(sig("bias_in"), 16)
            pool.dma_start(bdown[0:E, :], a["b_down_2"][:, :]).then_inc(sig("bias_in"), 16)
            for t in range(TC):
                pool.wait_ge(sig("h1_ready"), t + 1)
                pool.dma_start(h1_dram[t * P:(t + 1) * P, :], h1[:, t, :]).then_inc(sig("h1_stored"), 16)
            load_rows(rows[:, 0, :], "ln2_g", D, sig("rows3_in"))
            load_rows(rows[:, 1, :], "ln2_b", D, sig("rows3_in"))
            pool.wait_ge(sig("h1T_ps"), TC)
            pool.wait_ge(sig("o_used"), N_O)
            nc.gpsimd.memset(xe, 0.0).then_inc(sig("xe_zero"), 1)
            pool.wait_ge(sig("xe_zero"), 1)
            pool.wait_ge(sig("h1_stored"), 16 * TC)
            last_token = pool.to_reg(T - 1)
            last_row = pool.to_reg(TOPK * T - 1)

            def gather():
                nc.gpsimd.indirect_dma_start(out=xe, out_offset=None, in_=h1_dram, in_offset=bass.IndirectOffsetOnAxis(idx_g[:, 0:1], 0),
                                             bounds_check=last_token, oob_is_err=False).then_inc(sig("gathered"), 16)

            pool.wait_ge(sig("idx0_ready"), 1)
            gather()
            pool.wait_ge(sig("list_ready"), 3)
            n_items = pool.value_load(nint[0:1, 0:1], min_val=E, max_val=E + 16)
            with pool.Fori(1, n_items + 1) as m:
                wait_alone(pool, sig("idx_ready"), m)
                gather()
                wait_alone(pool, sig("y_ready"), m)
                nc.gpsimd.indirect_dma_start(out=y_dram, out_offset=bass.IndirectOffsetOnAxis(idx_s[:, 0:1], 0), in_=ysb, in_offset=None,
                                             bounds_check=last_row, oob_is_err=False).then_inc(sig("scattered"), 16)
            wait_alone(pool, sig("gathered"), n_items * 16 + 16)

        @block.tensor
        def _(pe):
            mm = nc.tensor.matmul

            def lru_gates(pe, j):
                b = 4 + 2 * (j % 2)
                pe.wait_ge(sig("xs"), j + 1)
                if j >= 2:
                    pe.wait_ge(sig("gates_taken"), 2 * (j - 1))
                if j == 0:
                    pe.wait_ge(sig("gates_in"), 32)
                nc.tensor.matmul(ps[:, b, :], gates_w[:, j, :], xs[:, j % 2, :], start=True, stop=True)
                nc.tensor.matmul(ps[:, b + 1, :], gates_w[:, KD + j, :], xs[:, j % 2, :], start=True, stop=True).then_inc(sig("gates_ps"), 1)

            def channel_mean(pe):
                pe.wait_ge(sig("gates_taken"), 16)
                for k in range(KD):
                    pe.wait_ge(sig("conv"), k + 1)
                    i = nc.tensor.matmul(ps[:, 4, :], cst("mean"), vc[:, k, :], start=(k == 0), stop=(k == KD - 1))
                i.then_inc(sig("mean_ps"), 1)

            def channel_var(pe):
                for k in range(KD):
                    pe.wait_ge(sig("vsq"), k + 1)
                    nc.tensor.matmul(ps[:, 5, :], cst("mean"), rep[:, k % 2, :], start=(k == 0), stop=(k == KD - 1)).then_inc(sig("vsq_summed"), 1)

            def attention(pe):
                mm = nc.tensor.matmul

                def scores(u):
                    hh, qt = UNITS[u]
                    b = 2 * (u % 2)
                    q = slice(qt * P, (qt + 1) * P)
                    if u >= 2:
                        pe.wait_ge(sig("prob"), u - 1)
                    for lo, hi, bb in ((0, T, b), (T, L, b + 1)):
                        dst = ps[:, bb, 0:hi - lo]
                        if hh < HM:
                            pb = ROPE * (hh % 2)
                            mm(dst, qnT[:, hh, q], knT[:, hh, lo:hi], start=True, stop=False)
                            i = mm(dst, qpT[pb:pb + ROPE, hh // 2, q], krT[pb:pb + ROPE, lo:hi], start=False, stop=True)
                        else:
                            i = mm(dst, qgT[:, hh - HM, q], kgT[:, (hh - HM) // 2, lo:hi], start=True, stop=True)
                    i.then_inc(sig("scores_ps"), 1)

                def turn(u):
                    if u >= 1:
                        pe.wait_ge(sig("probT"), 2 * u)
                    pe.wait_ge(sig("prob"), u + 1)
                    for c in range(TC):
                        i = nc.tensor.transpose(ps[:, 4, c * P:(c + 1) * P], pr[:, u % 2, c * P:(c + 1) * P], IDENT)
                    i = nc.tensor.transpose(ps[0:META, 5, 0:P], pr[:, u % 2, T:L], IDENT)
                    i.then_inc(sig("probT_ps"), 1)

                def weigh(u):
                    hh, qt = UNITS[u]
                    pe.wait_ge(sig("probT"), 2 * (u + 1))
                    if u >= 2:
                        pe.wait_ge(sig("o_taken"), u - 1)
                    for c in range(LC):
                        r = rows_of(c)
                        if hh < HM:
                            val = vm[0:r, c, hh * P:(hh + 1) * P]
                        else:
                            val = zC[0:r, c, 256 + (hh - HM) // 2 * P:256 + ((hh - HM) // 2 + 1) * P]
                        i = mm(ps[:, 6 + u % 2, 0:P], pT[0:r, u % 2, c * P:(c + 1) * P], val, start=(c == 0), stop=(c == LC - 1))
                    i.then_inc(sig("o_ps"), 1)

                pe.wait_ge(sig("kn"), HM + 1)
                pe.wait_ge(sig("qpT"), TC)
                scores(0)
                scores(1)
                for u in range(len(UNITS)):
                    turn(u)
                    if u + 2 < len(UNITS):
                        scores(u + 2)
                    weigh(u)

            def slot(j):
                return (ring[:, j, :] if j < RING1 else ext[:, j - RING1, :]).rearrange("p (k n) -> p k n", k=2)

            def item_index():
                for c in range(TC):
                    i = mm(ps[:, 4, 0:2], oh[:, c, :], dcur[:, c, :], start=(c == 0), stop=(c == TC - 1))
                i.then_inc(sig("idx_ps"), 1)

            def turn_tokens():
                for q in range(2):
                    for k in range(4):
                        i = nc.tensor.transpose(ps[:, 6 + q, k * P:(k + 1) * P], xe[:, (4 * q + k) * P:(4 * q + k + 1) * P], IDENT)
                    i.then_inc(sig("xt_ps"), 1)

            def experts(pe):
                pe.wait_ge(sig("routed"), 1)
                for c in range(TC):
                    for cc in range(c + 1):
                        mm(ps[:, 3, c * E:(c + 1) * E], cst("before") if cc == c else cst("ones"), routed[:, cc, :],
                           start=(cc == 0), stop=(cc == c))
                for c in range(TC):
                    i = mm(ps[:, 3, TC * E:(TC + 1) * E], cst("ones"), routed[:, c, :], start=(c == 0), stop=(c == TC - 1))
                i.then_inc(sig("places_ps"), 1)
                pe.wait_ge(sig("over_ready"), 2)
                for q in range(2):
                    i = mm(ps[:, 3, q * E:(q + 1) * E], evb[0:E, q, :], cst("ident", 0, E, E), start=True, stop=True)
                i.then_inc(sig("list_ps"), 1)
                pe.wait_ge(sig("gmat"), 1)
                for c in range(TC):
                    i = nc.tensor.transpose(ps[0:E, 4, c * P:(c + 1) * P], gmat[:, c, :], IDENT)
                i.then_inc(sig("gT_ps"), 1)
                pe.wait_ge(sig("gT"), 1)
                pe.wait_ge(sig("bias_in"), 32)
                for c in range(TC):
                    if c >= 2:
                        pe.wait_ge(sig("acc"), 2 * (c - 1))
                    for q in range(2):
                        mm(ps[:, 4 + 2 * (c % 2) + q, :], gT[0:E, c * P:(c + 1) * P], bdown[0:E, q * 512:(q + 1) * 512],
                           start=True, stop=True).then_inc(sig("bdown_ps"), 1)
                pe.wait_ge(sig("acc"), 2 * TC)
                pe.wait_ge(sig("oh_ready"), 1)
                item_index()
                pe.wait_ge(sig("gathered"), 16)
                turn_tokens()
                pe.wait_ge(sig("idx0_ready"), 1)
                pe.wait_ge(sig("list_ready"), 3)
                n_items = pe.value_load(nint[0:1, 0:1], min_val=E, max_val=E + 16)
                with pe.Fori(0, n_items) as i:
                    pe.wait_ge(sig("oh_ready"), i + 2)
                    pe.wait_ge(sig("y_ready"), i)
                    pe.wait_ge(sig("idx_ready"), i)
                    item_index()
                    pe.wait_ge(sig("eo_ready"), i + 1)
                    pe.wait_ge(sig("xt_sb"), i * 2 + 2)
                    for half in range(2):
                        pe.wait_ge(sig("lin_ready"), i * 2 + half)
                        for q in range(2):
                            mm(ps[:, 2 * half + q, :], eo[0:E, :], bgu[0:E, half * D + q * 512:half * D + (q + 1) * 512], start=True, stop=False)
                        for g in range(4):
                            j = 4 * half + g
                            pe.wait_ge(tile_ready[j], i * 16 + 16 * (loads_before[j] + 1))
                            for kk in range(2):
                                k = 2 * g + kk
                                for q in range(2):
                                    m = mm(ps[:, 2 * half + q, :], xT[:, k, :], slot(j)[:, kk, q * 512:(q + 1) * 512],
                                           start=False, stop=(k == KD - 1))
                            m.then_inc(sig("moe_used"), 1)
                    pe.wait_ge(sig("gathered"), i * 16 + 32)
                    pe.wait_ge(sig("at_sb"), i * 2)
                    turn_tokens()
                    pe.wait_ge(sig("idx_ready"), i + 1)
                    for half in range(2):
                        pe.wait_ge(sig("act_ready"), i * 2 + (half + 1))
                        pe.wait_ge(sig("xt_sb"), i * 2 + 4)
                        for k in range(4):
                            m = nc.tensor.transpose(ps[:, 6 + half, k * P:(k + 1) * P], actv[:, (4 * half + k) * P:(4 * half + k + 1) * P], IDENT)
                        m.then_inc(sig("at_ps"), 1)
                        pe.wait_ge(sig("at_sb"), i * 2 + (half + 1))
                        for g in range(2):
                            j = 8 + 2 * half + g
                            pe.wait_ge(tile_ready[j], i * 16 + 16)
                            for kk in range(2):
                                k = 4 * half + 2 * g + kk
                                for q in range(2):
                                    m = mm(ps[:, 4 + q, :], aT[:, k, :], slot(j)[:, kk, q * 512:(q + 1) * 512],
                                           start=(k == 0), stop=(k == KD - 1))
                            m.then_inc(sig("moe_used"), 1)

            pe.wait_ge(sig("c_act"), 1)
            for k in range(KD):
                wait_tile(pe, k)
                for m in range(16):
                    i = mm(ps[:, 0, m:m + 1], tile(k)[:, m * P:(m + 1) * P], c_act[:, k:k + 1],
                           start=(k == 0 and m == 0), stop=(k == KD - 1), skip_group_check=True)
                i.then_inc(sig("mod_used"), 1)
            pe.wait_ge(sig("const_in"), 16)
            for k in range(KD):
                pe.wait_ge(sig("xsq"), k + 1)
                mm(ps[:, 1, :], cst("mean"), rep[:, k % 2, :], start=(k == 0), stop=(k == KD - 1)).then_inc(sig("xsq_summed"), 1)
            for n in range(N_IN):
                wait_tile(pe, T_IN + n)
                if n == 0:
                    pe.wait_ge(sig("hT"), KD)
                if n >= 2:
                    pe.wait_ge(sig("u_taken"), n - 1)
                w = tile(T_IN + n).rearrange("p (k n) -> p k n", k=KD)
                for half in range(2):
                    for k in range(KD):
                        i = mm(ps[:, 2 * (n % 2) + half, :], w[:, k, half * P:(half + 1) * P], hT[:, k, :],
                               start=(k == 0), stop=(k == KD - 1))
                    i.then_inc(sig("u_ready"), 1)
                if 9 <= n <= 16:
                    lru_gates(pe, n - 9)
                if n == 17:
                    channel_mean(pe)
            channel_var(pe)
            pe.wait_ge(sig("crep"), KD)
            for n in range(N_GATE):
                wait_tile(pe, T_GATE + n)
                w = tile(T_GATE + n).rearrange("p (k n) -> p k n", k=2)
                for kk in range(2):
                    k = 2 * n + kk
                    for half in range(2):
                        i = mm(ps[:, 6 + half, :], crep[:, k, :], w[:, kk, half * 512:(half + 1) * 512],
                               start=(k == 0), stop=(k == KD - 1))
                i.then_inc(sig("gate_used"), 1)
            pe.wait_ge(sig("u_taken"), N_IN)
            for n in range(N_PW2):
                wait_tile(pe, T_PW2 + n)
                w = tile(T_PW2 + n).rearrange("p (k n) -> p k n", k=KD)
                for half in range(2):
                    m = 2 * n + half
                    if m >= 4:
                        pe.wait_ge(sig("yconv"), m - 3)
                    for k in range(KD):
                        if m == 0:
                            pe.wait_ge(sig("vln"), k + 1)
                        i = mm(ps[:, m % 4, :], w[:, k, half * P:(half + 1) * P], vc[:, k, :],
                               start=(k == 0), stop=(k == KD - 1))
                    i.then_inc(sig("pw2_ready"), 1)
            pe.wait_ge(sig("yconv"), KD)
            pe.wait_ge(sig("ylru"), KD)
            pe.wait_ge(sig("gate1"), 2)
            for n in range(N_OUT):
                half, g = n // 4, n % 4
                wait_tile(pe, T_OUT + n)
                w = tile(T_OUT + n).rearrange("p (k n) -> p k n", k=4)
                for kk in range(4):
                    k = 4 * g + kk
                    src = scs[:, k, :] if k < KD else ylru[:, k - KD, :]
                    for t in range(TC):
                        i = mm(ps[:, 4 * half + t, :], src[:, t * P:(t + 1) * P], w[:, kk, :],
                               start=(k == 0), stop=(k == 2 * KD - 1))
                i.then_inc(sig("out_used"), 1)
            for t in range(LC):
                r = rows_of(t)
                b = 2 * (t % 2)
                if t < 2:
                    pe.wait_ge(sig("x2"), 2 * TC)
                pe.wait_ge(sig("h_ready"), t + 1)
                if t >= 2:
                    pe.wait_ge(sig("hT2"), 2 * (t - 1))
                for k in range(KD):
                    i = nc.tensor.transpose(ps[:, b + k // 4, (k % 4) * P:(k % 4) * P + r], h[0:r, t, k * P:(k + 1) * P],
                                            cst("ident", 0, r, r))
                    if k % 4 == 3:
                        i.then_inc(sig("hT2_ps"), 1)
            unit = 0
            for g in range(3):
                wd = (448, 512, 512)[g]
                for t in range(LC):
                    if g == 1 and t == TC:
                        continue
                    r = rows_of(t)
                    b = 4 + unit % 4
                    if unit >= 4:
                        pe.wait_ge(sig("z"), unit - 3)
                    for k in range(KD):
                        if t == 0 and k % 4 == 0:
                            wait_tile(pe, T_IN2 + 2 * g + k // 4)
                        if unit == 0 and k == 0:
                            pe.wait_ge(sig("hT2"), 2 * LC)
                        w = tile(T_IN2 + 2 * g + k // 4)[:, 0:4 * wd].rearrange("p (k n) -> p k n", k=4)
                        i = mm(ps[0:r, b, 0:wd], hT2[:, k, t * P:t * P + r], w[:, k % 4, :],
                               start=(k == 0), stop=(k == KD - 1))
                    i.then_inc(sig("z_ready"), 1)
                    unit += 1
            for t in range(LC):
                r = rows_of(t)
                pe.wait_ge(sig("small_qk"), t + 1)
                if t >= 1:
                    pe.wait_ge(sig("turned"), 3 * t)
                ident = cst("ident", 0, r, r)
                for j in range(4):
                    if j < 2 and t == TC:
                        continue
                    src = zA[0:r, t, j * P:(j + 1) * P] if j < 3 else pe_rot[0:r, 4 * ROPE:4 * ROPE + P]
                    i = nc.tensor.transpose(ps[:, 0, j * P:j * P + r], src, ident)
                i.then_inc(sig("turned_ps"), 1)
                for j in range(4):
                    if t < TC:
                        i = nc.tensor.transpose(ps[:, 1, j * P:j * P + r], rot[0:r, j * P:(j + 1) * P], ident)
                if t < TC:
                    i.then_inc(sig("turned_ps"), 1)
                for j in range(2):
                    i = nc.tensor.transpose(ps[:, 2, j * P:j * P + r], rot[0:r, (4 + j) * P:(5 + j) * P], ident)
                i.then_inc(sig("turned_ps"), 1)
            pe.wait_ge(sig("turned"), 3 * LC - 1)
            wait_tile(pe, T_Q)
            wq = tile(T_Q)[:, 0:1536].rearrange("p (k n) -> p k n", k=2)
            for j in range(HM):
                for k in range(2):
                    i = mm(ps[:, 4 + j, :], wq[:, k, j * 192:j * 192 + P], qanT[:, k, :], start=(k == 0), stop=(k == 1))
                i.then_inc(sig("qn_ps"), 1)
            for t in range(TC):
                for k in range(2):
                    i = mm(ps[:, 0, 0:256], qanT[:, k, t * P:(t + 1) * P],
                           wq[:, k, :].rearrange("p (h n) -> p h n", h=HM)[:, :, P:192], start=(k == 0), stop=(k == 1))
                i.then_inc(sig("qp_ps"), 1)
                pe.wait_ge(sig("qp_rot"), t + 1)
                for j in range(2):
                    i = nc.tensor.transpose(ps[:, 1, j * P:(j + 1) * P], pe_rot[:, j * P:(j + 1) * P], IDENT)
                i.then_inc(sig("qpT_ps"), 1)
                pe.wait_ge(sig("qpT"), t + 1)
            wait_tile(pe, T_KV)
            wkv = tile(T_KV)[:, 0:D]
            for j in range(HM):
                pe.wait_ge(sig("qn"), j + 1)
                mm(ps[:, 4 + j, :], wkv[:, j * 256:j * 256 + P], kvanT[:, 0:T], start=True, stop=True).then_inc(sig("kn_ps"), 1)
            for j in range(HM):
                i = mm(ps[:, 3, j * META:(j + 1) * META], wkv[:, j * 256:j * 256 + P], kvanT[:, T:L], start=True, stop=True)
            i.then_inc(sig("kn_ps"), 1)
            for t in range(LC):
                r = rows_of(t)
                if t >= 1:
                    pe.wait_ge(sig("vm"), t)
                i = mm(ps[0:r, 2, :], kvanT[:, t * P:t * P + r],
                       wkv.rearrange("p (h n) -> p h n", h=HM)[:, :, P:256], start=True, stop=True)
                i.then_inc(sig("vm_ps"), 1)
            pe.wait_ge(sig("vm"), LC)
            attention(pe)
            for t in range(TC):
                pe.wait_ge(sig("o_norm"), 2 * (t + 1))
                if t >= 1:
                    pe.wait_ge(sig("oT"), 8 * t)
                for k in range(KD):
                    i = nc.tensor.transpose(ps[:, k // 4, (k % 4) * P:(k % 4 + 1) * P], o_tok[:, t, k * P:(k + 1) * P], IDENT)
                i.then_inc(sig("oT_ps"), 1)
            pe.wait_ge(sig("oT"), 8 * TC)
            for n in range(N_O):
                half, g = n // 2, n % 2
                wait_tile(pe, T_O + n)
                w = tile(T_O + n).rearrange("p (k n) -> p k n", k=4)
                for kk in range(4):
                    k = 4 * g + kk
                    for t in range(TC):
                        i = mm(ps[:, 4 * half + t, :], oT[:, k, t * P:(t + 1) * P], w[:, kk, :],
                               start=(k == 0), stop=(k == KD - 1))
                i.then_inc(sig("o_used"), 1)
            for t in range(TC):
                pe.wait_ge(sig("h1_ready"), t + 1)
                if t == 0:
                    pe.wait_ge(sig("mix_taken"), 2 * TC)
                if t >= 1:
                    pe.wait_ge(sig("h1T"), 2 * t)
                for k in range(KD):
                    i = nc.tensor.transpose(ps[:, k // 4, (k % 4) * P:(k % 4 + 1) * P], h1[:, t, k * P:(k + 1) * P], IDENT)
                i.then_inc(sig("h1T_ps"), 1)
            pe.wait_ge(sig("h1T"), 2 * TC)
            pe.wait_ge(sig("router_in"), 16)
            for t in range(TC):
                for k in range(KD):
                    i = mm(ps[:, 2, t * E:(t + 1) * E], h1T[:, k, t * P:(t + 1) * P], wrouter[:, k, :],
                           start=(k == 0), stop=(k == KD - 1))
            i.then_inc(sig("logits_ps"), 1)
            experts(pe)

        @block.scalar
        def _(act):
            A = nc.scalar.activation
            st = Steps(act, sig("act_step"))
            for k in range(KD):
                act.dma_start(hT[:, k, :], a["xT"][k * P:(k + 1) * P, :]).then_inc(sig("xT_in"), 16)
            act.dma_start(gates_w[:, 0:KD, :], a["wr"].rearrange("h d e -> d h e")).then_inc(sig("gates_in"), 16)
            act.dma_start(gates_w[:, KD:, :], a["wi"].rearrange("h d e -> d h e")).then_inc(sig("gates_in"), 16)
            act.dma_start(gate1[:], a["rows"][:, ROWS["gate_b"]:ROWS["gate_b"] + D].partition_broadcast(P)).then_inc(sig("gateb_in"), 16)
            act.dma_start(xtok[:], a["x"].rearrange("(t p) d -> p t d", p=P)).then_inc(sig("xtok_in"), 16)
            act.dma_start(rows[:].rearrange("p a b -> p (a b)"), a["rows"][:, ROWS["final_g"]:ROWS["final_g"] + 3 * D].partition_broadcast(P)).then_inc(sig("rows1_in"), 16)
            act.wait_ge(sig("chan_in"), 16)
            A(c_sig, ch("c", 0, 8), ACT.Sigmoid).then_inc(sig("c_sig"), 1)
            act.wait_ge(sig("xT_in"), 16 * KD)
            for k in range(KD):
                if k >= 2:
                    act.wait_ge(sig("xsq_summed"), k - 1)
                A(rep[:, k % 2, :], hT[:, k, :], ACT.Square).then_inc(sig("xsq"), 1)
            act.wait_ge(sig("xsq_summed"), KD)
            act.wait_ge(sig("const_in"), 16)
            st.link(A(rep[:, 0, :], ps[:, 1, :], ACT.Ln, bias=cst("eps6")))
            A(rep[:, 1, :], rep[:, 0, :], ACT.Exp, scale=-0.5).then_inc(sig("rstd_x"), 1)
            act.wait_ge(sig("lam_abs"), 1)
            A(lam_e, lam_abs, ACT.Exp, scale=-1.0).then_inc(sig("lam_exp"), 1)

            def lru_act(j):
                r, ig, s, al = (lru[:, q, :] for q in range(4))
                b = 4 + 2 * (j % 2)
                act.wait_ge(sig("gates_ps"), j + 1)
                if j == 0:
                    act.wait_ge(sig("rate"), 1)
                if j >= 1:
                    act.wait_ge(sig("ylru"), j)
                A(r, ps[:, b, :], ACT.Sigmoid, bias=ch("br", j)).then_inc(sig("gates_taken"), 1)
                A(ig, ps[:, b + 1, :], ACT.Sigmoid, bias=ch("bi", j)).then_inc(sig("gates_taken"), 1)
                act.wait_ge(sig("gates_taken"), 2 * j + 2)
                st.go(A(s, r, ACT.Tanh, scale=rate[:, j:j + 1]))
                A(al, r, ACT.Exp, scale=nrate[:, j:j + 1]).then_inc(sig("a_ready"), 1)
                st.wait()
                act.wait_ge(sig("a_ready"), j + 1)
                st.link(A(r, s, ACT.Ln, bias=cst("tiny")))
                A(s, s, ACT.Ln, bias=ONE).then_inc(sig("logs"), 1)
                act.wait_ge(sig("logd"), j + 1)
                A(r, r, ACT.Exp, scale=0.5, bias=cst("hln2")).then_inc(sig("mult"), 1)

            for n in range(N_IN):
                b = 2 * (n % 2)
                act.wait_ge(sig("u_ready"), 2 * n + 2)
                if n >= 2:
                    act.wait_ge(sig("u_taken"), n - 1)
                A(sgt[:, n % 2, :], ps[:, b + 1, :], ACT.Sigmoid).then_inc(sig("u_sig"), 1)
                if n >= 16:
                    if n < 18:
                        act.wait_ge(sig("ylru"), n - 9)
                    A(lsil[:, n % 2, :], ps[:, b, :], ACT.Sigmoid).then_inc(sig("u_sig2"), 1)
                if 9 <= n <= 16:
                    lru_act(n - 9)
            for k in range(KD):
                act.wait_ge(sig("vcent"), k + 1)
                if k >= 2:
                    act.wait_ge(sig("vsq_summed"), k - 1)
                A(rep[:, k % 2, :], vc[:, k, :], ACT.Square).then_inc(sig("vsq"), 1)
            act.wait_ge(sig("vsq_summed"), KD)
            st.link(A(rep[:, 0, :], ps[:, 5, :], ACT.Ln, bias=cst("eps6")))
            A(rep[:, 1, :], rep[:, 0, :], ACT.Exp, scale=-0.5).then_inc(sig("rstd_v"), 1)
            act.wait_ge(sig("u_taken"), N_IN)
            for k in range(KD):
                act.wait_ge(sig("vscaled"), k + 1)
                if k >= 2:
                    act.wait_ge(sig("vln"), k - 1)
                A(sgt[:, k % 2, :], vc[:, k, :], ACT.Sigmoid, bias=ch("cln_b", k)).then_inc(sig("v_sig"), 1)
            for t in range(TC):
                act.wait_ge(sig("x2"), TC + t + 1)
                st.link(A(junk, x2[:, t, :], ACT.Square, accum_out=x2_ss[:, t:t + 1]))
            st.link(A(x2_ln, x2_ss, ACT.Ln, scale=1.0 / D, bias=cst("eps6")))
            A(x2_rstd, x2_ln, ACT.Exp, scale=-0.5).then_inc(sig("rstd_x2"), 1)
            act.wait_ge(sig("emb_var"), 1)
            st.link(A(emb_ln, emb_var, ACT.Ln, bias=cst("eps5")))
            A(emb_rstd, emb_ln, ACT.Exp, scale=-0.5).then_inc(sig("emb_rstd"), 1)
            for t in range(LC):
                r = rows_of(t)
                for q in range(2):
                    act.wait_ge(sig("hT2_ps"), 2 * t + q + 1)
                    A(hT2[:, 4 * q:4 * q + 4, t * P:t * P + r],
                      ps[:, 2 * (t % 2) + q, :].rearrange("p (k n) -> p k n", k=4)[:, :, 0:r], ACT.Copy).then_inc(sig("hT2"), 1)
            unit = 0
            for g in range(3):
                z, wd = ((zA, 448), (zB, 512), (zC, 512))[g]
                for t in range(LC):
                    if g == 1 and t == TC:
                        continue
                    r = rows_of(t)
                    act.wait_ge(sig("z_ready"), unit + 1)
                    A(z[0:r, t, :], ps[0:r, 4 + unit % 4, 0:wd], ACT.Copy).then_inc(sig("z"), 1)
                    unit += 1
            act.wait_ge(sig("z_ss"), 1)
            st.link(A(z_ln, z_ss, ACT.Ln, scale=1.0 / P, bias=cst("eps6")))
            A(z_ss, z_ln, ACT.Exp, scale=-0.5).then_inc(sig("z_rstd"), 1)
            for t in range(LC):
                r = rows_of(t)
                tk = slice(t * P, t * P + r)
                act.wait_ge(sig("turned_ps"), 3 * t + 1)
                if t < TC:
                    for k in range(2):
                        st.go(A(qanT[:, k, tk], ps[:, 0, k * P:(k + 1) * P], ACT.Copy, scale=ch("g_q_a", k)))
                st.go(A(kvanT[:, tk], ps[:, 0, 2 * P:2 * P + r], ACT.Copy, scale=ch("g_kv_a")))
                A(krT[:, tk], ps[:, 0, 3 * P:3 * P + r], ACT.Copy).then_inc(sig("turned"), 1)
                st.wait()
                if t < TC:
                    act.wait_ge(sig("turned_ps"), 3 * t + 2)
                    A(qgT[:, :, tk], ps[:, 1, :].rearrange("p (h n) -> p h n", h=4), ACT.Copy).then_inc(sig("turned"), 1)
                act.wait_ge(sig("turned_ps"), 3 * t + (3 if t < TC else 2))
                A(kgT[:, :, tk], ps[:, 2, 0:256].rearrange("p (h n) -> p h n", h=2)[:, :, 0:r], ACT.Copy).then_inc(sig("turned"), 1)
            for j in range(HM):
                act.wait_ge(sig("qn_ps"), j + 1)
                A(qnT[:, j, :], ps[:, 4 + j, :], ACT.Copy).then_inc(sig("qn"), 1)
            for t in range(TC):
                act.wait_ge(sig("qpT_ps"), t + 1)
                A(qpT[:, :, t * P:(t + 1) * P], ps[:, 1, 0:256].rearrange("p (h n) -> p h n", h=2), ACT.Copy).then_inc(sig("qpT"), 1)
            for j in range(HM):
                act.wait_ge(sig("kn_ps"), j + 1)
                A(knT[:, j, 0:T], ps[:, 4 + j, :], ACT.Copy).then_inc(sig("kn"), 1)
            act.wait_ge(sig("kn_ps"), HM + 1)
            A(knT[:, :, T:L], ps[:, 3, 0:HM * META].rearrange("p (h n) -> p h n", h=HM), ACT.Copy).then_inc(sig("kn"), 1)
            for t in range(LC):
                r = rows_of(t)
                act.wait_ge(sig("vm_ps"), t + 1)
                A(vm[0:r, t, :], ps[0:r, 2, :], ACT.Copy).then_inc(sig("vm"), 1)

            def probs(u):
                hh, qt = UNITS[u]
                scale = (NOPE + ROPE) ** -0.5 if hh < HM else P ** -0.5
                act.wait_ge(sig("nmax"), u + 1)
                if u >= 2:
                    act.wait_ge(sig("probT_ps"), u - 1)
                A(pr[:, u % 2, :], ps[:, 2 * (u % 2):2 * (u % 2) + 2, :].rearrange("p a b -> p (a b)")[:, 0:L], ACT.Exp,
                  bias=nmaxs[:, u:u + 1], scale=scale, accum_out=psums[:, u:u + 1]).then_inc(sig("prob"), 1)

            def turned(u):
                act.wait_ge(sig("probT_ps"), u + 1)
                if u >= 2:
                    act.wait_ge(sig("o_ps"), u - 1)
                A(pT[:, u % 2, 0:T], ps[:, 4, :], ACT.Copy).then_inc(sig("probT"), 1)
                A(pT[0:META, u % 2, T:LC * P], ps[0:META, 5, 0:P], ACT.Copy).then_inc(sig("probT"), 1)

            probs(0)
            for u in range(len(UNITS)):
                if u + 1 < len(UNITS):
                    probs(u + 1)
                turned(u)
            for t in range(TC):
                for g in range(2):
                    act.wait_ge(sig("o_taken"), 16 * g + 12 + t + 1)
                    st.link(A(pr[:, g, 0:512], o_tok[:, t, g * 512:(g + 1) * 512], ACT.Square, accum_out=o_ss[:, 2 * t + g:2 * t + g + 1]))
            st.link(A(o_ln, o_ss, ACT.Ln, scale=1.0 / 512, bias=cst("eps6")))
            A(o_rstd, o_ln, ACT.Exp, scale=-0.5).then_inc(sig("o_rstd"), 1)
            for t in range(TC):
                act.wait_ge(sig("oT_ps"), t + 1)
                for k in range(KD):
                    A(oT[:, k, t * P:(t + 1) * P], ps[:, k // 4, (k % 4) * P:(k % 4 + 1) * P], ACT.Copy, scale=ch("g_o", k)).then_inc(sig("oT"), 1)
            act.wait_ge(sig("ln1_var"), 1)
            st.link(A(ln_ln, ln_var, ACT.Ln, bias=cst("eps5")))
            A(ln_rstd, ln_ln, ACT.Exp, scale=-0.5).then_inc(sig("ln1_rstd"), 1)
            for t in range(TC):
                act.wait_ge(sig("h1T_ps"), t + 1)
                for q in range(2):
                    A(h1T[:, 4 * q:4 * q + 4, t * P:(t + 1) * P], ps[:, q, :].rearrange("p (k n) -> p k n", k=4), ACT.Copy).then_inc(sig("h1T"), 1)
            for t in range(TC):
                act.wait_ge(sig("best"), 1)
                A(gates[:, t, :], v8[:, t, 0:TOPK], ACT.Exp, bias=nv0[:, t:t + 1], accum_out=gsum[:, t:t + 1]).then_inc(sig("gate_exp"), 1)
            act.wait_ge(sig("gT_ps"), 1)
            A(gT[0:E, :], ps[0:E, 4, :], ACT.Copy).then_inc(sig("gT"), 1)

            def tokens_out():
                for q in range(2):
                    A(xT[:, 4 * q:4 * q + 4, :], ps[:, 6 + q, :].rearrange("p (k n) -> p k n", k=4), ACT.Copy).then_inc(sig("xt_sb"), 1)

            act.wait_ge(sig("xt_ps"), 2)
            tokens_out()
            act.wait_ge(sig("list_ready"), 3)
            n_items = act.value_load(nint[0:1, 0:1], min_val=E, max_val=E + 16)
            with act.Fori(0, n_items) as i:
                for half in range(2):
                    act.wait_ge(sig("glu_ready"), i * 2 + (half + 1))
                    A(gsig[:, half, :], glu[:, half, :], ACT.Sigmoid, scale=SWALPHA).then_inc(sig("gsig_ready"), 1)
                act.wait_ge(sig("xt_ps"), i * 2 + 4)
                tokens_out()
                for half in range(2):
                    act.wait_ge(sig("at_ps"), i * 2 + (half + 1))
                    A(aT[:, 4 * half:4 * half + 4, :], ps[:, 6 + half, :].rearrange("p (k n) -> p k n", k=4), ACT.Copy).then_inc(sig("at_sb"), 1)
            for t in range(TC):
                act.wait_ge(sig("ln2_var"), t + 1)
                A(ln_ln[:, t:t + 1], ln_var[:, t:t + 1], ACT.Ln, bias=cst("eps5")).then_inc(sig("ln2_log"), 1)
                act.wait_ge(sig("ln2_log"), t + 1)
                A(ln_rstd[:, t:t + 1], ln_ln[:, t:t + 1], ACT.Exp, scale=-0.5).then_inc(sig("ln2_rstd"), 1)

        @block.vector
        def _(dve):
            V = nc.vector
            st = Steps(dve, sig("dve_step"))
            dve.wait_ge(sig("c_sig"), 1)
            V.tensor_tensor(c_act, ch("c", 0, 8), c_sig, ALU.mult).then_inc(sig("c_act"), 1)
            st.link(V.tensor_scalar(lam_neg, ch("lam", 0, 8), -1.0, None, ALU.mult))
            V.tensor_tensor(lam_abs, ch("lam", 0, 8), lam_neg, ALU.max).then_inc(sig("lam_abs"), 1)
            dve.wait_ge(sig("lam_exp"), 1)
            e_, z_, zz, se = lam_e, lam_z, rate, nrate
            st.link(V.tensor_scalar(z_, e_, 2.0, None, ALU.add))
            st.link(V.reciprocal(zz, z_))
            st.link(V.tensor_tensor(z_, zz, e_, ALU.mult))
            st.link(V.tensor_tensor(zz, z_, z_, ALU.mult))
            st.link(V.memset(se, 1.0 / 21))
            for q in range(19, 0, -2):
                st.link(V.tensor_tensor(se, se, zz, ALU.mult))
                st.link(V.tensor_scalar(se, se, 1.0 / q, None, ALU.add))
            st.link(V.tensor_tensor(se, se, z_, ALU.mult))
            st.link(V.tensor_scalar(zz, lam_neg, 0.0, 8.0, ALU.max, ALU.mult))
            st.link(V.tensor_scalar(se, se, 16.0, None, ALU.mult))
            st.link(V.tensor_tensor(zz, zz, se, ALU.add))
            V.tensor_scalar(se, zz, -1.0, None, ALU.mult).then_inc(sig("rate"), 1)
            dve.wait_ge(sig("const_in"), 16)
            for k in range(KD):
                V.tensor_scalar(crep[:, k, :], cst("ones"), c_act[:, k:k + 1], None, ALU.mult).then_inc(sig("crep"), 1)
            dve.wait_ge(sig("mod_used"), N_MOD)
            dve.wait_ge(sig("chan_in"), 16)
            st.go(V.tensor_tensor(shift, ps[:, 0, 0:8], ch("mod_b", 0, 8), ALU.add))
            st.link(V.tensor_tensor(gain, ps[:, 0, 8:16], ch("mod_b", 8, 8), ALU.add))
            st.link(V.scalar_tensor_tensor(gain, gain, 1.0, ch("norm_g", 0, 8), ALU.add, ALU.mult))
            dve.wait_ge(sig("rstd_x"), 1)
            for k in range(KD):
                st.go(V.scalar_tensor_tensor(hT[:, k, :], hT[:, k, :], gain[:, k:k + 1], rep[:, 1, :], ALU.mult, ALU.mult))
            st.wait()
            for k in range(KD):
                V.tensor_scalar(hT[:, k, :], hT[:, k, :], shift[:, k:k + 1], None, ALU.add).then_inc(sig("hT"), 1)

            taps = [(j, q) for j in range(KD) for q in range(TAPS)]
            done = [0]

            def conv_taps(count):
                for _ in range(count):
                    if done[0] == len(taps):
                        return
                    j, q = taps[done[0]]
                    done[0] += 1
                    src = v[:, j, q:q + T]
                    w = ch("dw_w", j * TAPS + q)
                    if q == 0:
                        dve.wait_ge(sig("u_taken"), j + 1)
                        st.link(V.tensor_scalar(vc[:, j, :], src, w, ch("dw_b", j), ALU.mult, ALU.add))
                    else:
                        i = V.scalar_tensor_tensor(vc[:, j, :], src, w, vc[:, j, :], ALU.mult, ALU.add)
                        if q == TAPS - 1:
                            i.then_inc(sig("conv"), 1)
                        else:
                            st.link(i)

            def lru_vec(j):
                r, ig, s, al = (lru[:, q, :] for q in range(4))
                dve.wait_ge(sig("logs"), j + 1)
                V.tensor_tensor(r, r, s, ALU.subtract).then_inc(sig("logd"), 1)
                st.link(V.tensor_tensor(ig, ig, xs[:, j % 2, :], ALU.mult))
                dve.wait_ge(sig("mult"), j + 1)
                dve.wait_ge(sig("a_ready"), j + 1)
                st.link(V.tensor_tensor(ig, ig, r, ALU.mult))
                V.tensor_tensor_scan(s, al, ig, 0.0, ALU.mult, ALU.add).then_inc(sig("scan"), 1)
                dve.wait_ge(sig("scan"), j + 1)
                V.tensor_tensor(ylru[:, j, :], s, lsil[:, j % 2, :], ALU.mult).then_inc(sig("ylru"), 1)

            dve.wait_ge(sig("pads_zero"), 2)
            for n in range(N_IN):
                b = 2 * (n % 2)
                dve.wait_ge(sig("u_ready"), 2 * n + 2)
                dve.wait_ge(sig("u_sig"), n + 1)
                if n < 8:
                    V.tensor_tensor(v[:, n, TAPS - 1:], ps[:, b, :], sgt[:, n % 2, :], ALU.mult).then_inc(sig("u_taken"), 1)
                    conv_taps(22)
                elif n < 16:
                    j = n - 8
                    if j >= 2:
                        dve.wait_ge(sig("ylru"), j - 1)
                    st.go(V.tensor_tensor(lsil[:, j % 2, :], ps[:, b + 1, :], sgt[:, n % 2, :], ALU.mult))
                    V.tensor_copy(lxb[:, j % 2, STAPS - 1:], ps[:, b, :]).then_inc(sig("u_taken"), 1)
                    st.wait()
                    dve.wait_ge(sig("u_taken"), n + 1)
                    x_ = xs[:, j % 2, :]
                    if j == 0:
                        st.wait()
                    st.link(V.tensor_scalar(x_, lxb[:, j % 2, 0:T], ch("sc_w", j * STAPS), ch("sc_b", j), ALU.mult, ALU.add))
                    for q in range(1, STAPS):
                        i = V.scalar_tensor_tensor(x_, lxb[:, j % 2, q:q + T], ch("sc_w", j * STAPS + q), x_, ALU.mult, ALU.add)
                        if q < STAPS - 1:
                            st.link(i)
                    i.then_inc(sig("xs"), 1)
                    conv_taps(6)
                    if j >= 1:
                        lru_vec(j - 1)
                    conv_taps(4)
                else:
                    c = 2 * (n - 16)
                    if n == 16:
                        lru_vec(KD - 1)
                        conv_taps(len(taps))
                    dve.wait_ge(sig("u_sig2"), n - 15)
                    st.go(V.tensor_tensor(scs[:, c, :], ps[:, b, :], lsil[:, n % 2, :], ALU.mult))
                    V.tensor_tensor(scs[:, c + 1, :], ps[:, b + 1, :], sgt[:, n % 2, :], ALU.mult).then_inc(sig("u_taken"), 1)
                    st.wait()
                if n == 18:
                    dve.wait_ge(sig("mean_ps"), 1)
                    for k in range(KD):
                        V.tensor_tensor(vc[:, k, :], vc[:, k, :], ps[:, 4, :], ALU.subtract).then_inc(sig("vcent"), 1)
            dve.wait_ge(sig("rstd_v"), 1)
            for k in range(KD):
                V.scalar_tensor_tensor(vc[:, k, :], vc[:, k, :], ch("cln_g", k), rep[:, 1, :], ALU.mult, ALU.mult).then_inc(sig("vscaled"), 1)
            for k in range(KD):
                dve.wait_ge(sig("v_sig"), k + 1)
                V.scalar_tensor_tensor(vc[:, k, :], vc[:, k, :], ch("cln_b", k), sgt[:, k % 2, :], ALU.add, ALU.mult).then_inc(sig("vln"), 1)
            dve.wait_ge(sig("gateb_in"), 16)
            dve.wait_ge(sig("gate_used"), N_GATE)
            for q in range(2):
                V.scalar_tensor_tensor(gate1[:, q * 512:(q + 1) * 512], ps[:, 6 + q, :], 1.0, gate1[:, q * 512:(q + 1) * 512],
                                       ALU.add, ALU.add).then_inc(sig("gate1"), 1)
            for m in range(KD):
                dve.wait_ge(sig("pw2_ready"), m + 1)
                V.scalar_tensor_tensor(scs[:, m, :], ps[:, m % 4, :], ch("pw2_b", m), scs[:, m, :], ALU.add, ALU.mult).then_inc(sig("yconv"), 1)
            dve.wait_ge(sig("xtok_in"), 16)
            dve.wait_ge(sig("gate1"), 2)
            for half in range(2):
                c_ = slice(half * 512, (half + 1) * 512)
                dve.wait_ge(sig("out_used"), 4 * (half + 1))
                for t in range(TC):
                    tmp = rep[:, t % 2, :]
                    st.link(V.tensor_tensor(tmp, ps[:, 4 * half + t, :], gate1[:, c_], ALU.mult))
                    V.tensor_tensor(x2[:, t, c_], x2[:, t, c_], tmp, ALU.add).then_inc(sig("x2"), 1)
            dve.wait_ge(sig("rows1_in"), 16)
            dve.wait_ge(sig("rstd_x2"), 1)
            dve.wait_ge(sig("meta_in"), 16)
            dve.wait_ge(sig("x2"), 2 * TC)
            st.link(V.memset(emb_var, 1.0))
            for t in range(TC):
                st.link(V.scalar_tensor_tensor(h[:, t, :], x2[:, t, :], x2_rstd[:, t:t + 1], rows[:, 0, :], ALU.mult, ALU.mult))
            st_h = bn_part
            for t in range(LC):
                r = rows_of(t)
                for q in range(2):
                    st.go(V.bn_stats(st_h[0:r, t, 6 * q:6 * q + 6], h[0:r, t, q * 512:(q + 1) * 512]))
                st.wait()
                st.link(V.bn_aggr(bn_mv[0:r, t, :], st_h[0:r, t, :]))
                i = V.tensor_copy(emb_var[0:r, t:t + 1], bn_mv[0:r, t, 1:2])
                if t < LC - 1:
                    st.go(i)
            i.then_inc(sig("emb_var"), 1)
            dve.wait_ge(sig("emb_rstd"), 1)
            for t in range(LC):
                r = rows_of(t)
                st.link(V.tensor_scalar(h[0:r, t, :], h[0:r, t, :], bn_mv[0:r, t, 0:1], emb_rstd[0:r, t:t + 1], ALU.subtract, ALU.mult))
                st.link(V.tensor_tensor(h[0:r, t, :], h[0:r, t, :], rows[0:r, 1, :], ALU.mult))
                V.tensor_tensor(h[0:r, t, :], h[0:r, t, :], rows[0:r, 2, :], ALU.add).then_inc(sig("h_ready"), 1)
            ss = z_ss.rearrange("p (t s) -> p t s", t=LC)
            st.link(V.memset(z_ss, 1.0))
            sq = rot
            for t in range(LC):
                r = rows_of(t)
                dve.wait_ge(sig("z"), t + 1)
                st.link(V.tensor_tensor(sq[0:r, 0:384], zA[0:r, t, 0:384], zA[0:r, t, 0:384], ALU.mult))
                st.link(V.tensor_reduce(ss[0:r, t, 0:3], sq[0:r, 0:384].rearrange("p (g n) -> p g n", g=3), AX.X, ALU.add))
                st.link(V.tensor_tensor(ss[0:r, t, 0:1], ss[0:r, t, 0:1], ss[0:r, t, 1:2], ALU.add))
                st.link(V.tensor_scalar(ss[0:r, t, 0:1], ss[0:r, t, 0:1], 0.5, None, ALU.mult))
            for t in range(TC):
                dve.wait_ge(sig("z"), LC + t + 1)
                st.link(V.tensor_tensor(sq[:, 0:512], zB[:, t, :], zB[:, t, :], ALU.mult))
                st.link(V.tensor_reduce(ss[:, t, 3:7], sq[:, 0:512].rearrange("p (g n) -> p g n", g=4), AX.X, ALU.add))
            for t in range(LC):
                r = rows_of(t)
                dve.wait_ge(sig("z"), LC + TC + t + 1)
                st.link(V.tensor_tensor(sq[0:r, 0:256], zC[0:r, t, 0:256], zC[0:r, t, 0:256], ALU.mult))
                i = V.tensor_reduce(ss[0:r, t, 7:9], sq[0:r, 0:256].rearrange("p (g n) -> p g n", g=2), AX.X, ALU.add)
                if t < LC - 1:
                    st.link(i)
            i.then_inc(sig("z_ss"), 1)
            dve.wait_ge(sig("z_rstd"), 1)
            dve.wait_ge(sig("tab_in"), 32)
            dve.wait_ge(sig("rows2_in"), 48)
            rope = rtmp[:, 0, :]
            rope2 = rtmp[:, 1, :]

            def rotate(dst1, dst2, x1, x2_, cos, sin, t1, t2, signal=None):
                st.go(V.tensor_tensor(t1, x1, cos, ALU.mult))
                st.link(V.tensor_tensor(t2, x2_, sin, ALU.mult))
                st.link(V.tensor_tensor(dst1, t1, t2, ALU.subtract))
                st.go(V.tensor_tensor(t1, x1, sin, ALU.mult))
                st.link(V.tensor_tensor(t2, x2_, cos, ALU.mult))
                i = V.tensor_tensor(dst2, t1, t2, ALU.add)
                if signal is None:
                    st.link(i)
                else:
                    i.then_inc(signal, 1)

            for t in range(LC):
                r = rows_of(t)
                if t >= 1:
                    dve.wait_ge(sig("turned_ps"), 3 * t)
                if t < TC:
                    st.go(V.tensor_scalar(zA[0:r, t, 0:256], zA[0:r, t, 0:256], ss[0:r, t, 0:1], None, ALU.mult))
                st.go(V.tensor_scalar(zA[0:r, t, 256:384], zA[0:r, t, 256:384], ss[0:r, t, 2:3], None, ALU.mult))
                c1, s1 = tab[0:r, t, 0:32], tab[0:r, t, 32:64]
                kr = pe_rot[0:r, 4 * ROPE:4 * ROPE + P]
                x1, x2_ = zA[0:r, t, 384:416], zA[0:r, t, 416:448]
                rotate(kr[:, 0:32], kr[:, 32:64], x1, x2_, c1, s1, rope[0:r, 0:32], rope2[0:r, 0:32])
                st.link(V.tensor_copy(kr[:, 64:128], kr[:, 0:64]))
                lo = 0 if t < TC else 4
                if t < TC:
                    for q in range(4):
                        st.go(V.scalar_tensor_tensor(zB[:, t, q * P:(q + 1) * P], zB[:, t, q * P:(q + 1) * P], ss[:, t, 3 + q:4 + q],
                                                     rows[:, 2, 0:P], ALU.mult, ALU.mult))
                for q in range(2):
                    st.go(V.scalar_tensor_tensor(zC[0:r, t, q * P:(q + 1) * P], zC[0:r, t, q * P:(q + 1) * P], ss[0:r, t, 7 + q:8 + q],
                                                 rows[0:r, 2, P:2 * P], ALU.mult, ALU.mult))
                st.wait()
                cs_, sn_ = tab[0:r, t, 64:128], tab[0:r, t, 128:192]
                for z, n_, at in ((zB, 4, 0), (zC, 2, 4)):
                    if at < lo:
                        continue
                    zz_ = z[0:r, t, 0:n_ * P].rearrange("p (h a b n) -> p h a b n", h=n_, a=2, b=2)
                    rr = rot[0:r, at * P:(at + n_) * P].rearrange("p (h a b n) -> p h a b n", h=n_, a=2, b=2)
                    t1 = rope[0:r, 0:n_ * 64].rearrange("p (h a n) -> p h a n", h=n_, a=2)
                    t2 = rope2[0:r, 0:n_ * 64].rearrange("p (h a n) -> p h a n", h=n_, a=2)
                    cc = cs_.rearrange("p (o a n) -> p o a n", o=1, a=2).to_broadcast([r, n_, 2, 32])
                    sn = sn_.rearrange("p (o a n) -> p o a n", o=1, a=2).to_broadcast([r, n_, 2, 32])
                    rotate(rr[:, :, :, 0, :], rr[:, :, :, 1, :], zz_[:, :, :, 0, :], zz_[:, :, :, 1, :], cc, sn, t1, t2,
                           sig("small_qk") if at == 4 else None)
            for t in range(TC):
                dve.wait_ge(sig("qp_ps"), t + 1)
                if t >= 1:
                    dve.wait_ge(sig("qpT_ps"), t)
                qv = ps[:, 0, 0:256].rearrange("p (h b n) -> p h b n", h=HM, b=2)
                dv = pe_rot[:, 0:256].rearrange("p (h b n) -> p h b n", h=HM, b=2)
                c1 = tab[:, t, 0:32].rearrange("p (o n) -> p o n", o=1).to_broadcast([P, HM, 32])
                s1 = tab[:, t, 32:64].rearrange("p (o n) -> p o n", o=1).to_broadcast([P, HM, 32])
                t1 = rope[:, 0:128].rearrange("p (h n) -> p h n", h=HM)
                t2 = rope2[:, 0:128].rearrange("p (h n) -> p h n", h=HM)
                rotate(dv[:, :, 0, :], dv[:, :, 1, :], qv[:, :, 0, :], qv[:, :, 1, :], c1, s1, t1, t2, sig("qp_rot"))

            def nmax(u):
                hh, qt = UNITS[u]
                scale = (NOPE + ROPE) ** -0.5 if hh < HM else P ** -0.5
                dve.wait_ge(sig("scores_ps"), u + 1)
                st.link(V.tensor_reduce(nmaxs[:, u:u + 1], ps[:, 2 * (u % 2):2 * (u % 2) + 2, :].rearrange("p a b -> p (a b)")[:, 0:L],
                                        AX.X, ALU.max))
                V.tensor_scalar(nmaxs[:, u:u + 1], nmaxs[:, u:u + 1], -scale, None, ALU.mult).then_inc(sig("nmax"), 1)

            def output(u):
                hh, qt = UNITS[u]
                dve.wait_ge(sig("prob"), u + 1)
                st.link(V.reciprocal(psums[:, u:u + 1], psums[:, u:u + 1]))
                dve.wait_ge(sig("o_ps"), u + 1)
                V.tensor_scalar(o_tok[:, qt, hh * P:(hh + 1) * P], ps[:, 6 + u % 2, 0:P], psums[:, u:u + 1], None, ALU.mult).then_inc(sig("o_taken"), 1)

            nmax(0)
            nmax(1)
            for u in range(len(UNITS)):
                if u + 2 < len(UNITS):
                    nmax(u + 2)
                output(u)
            dve.wait_ge(sig("o_rstd"), 1)
            dve.wait_ge(sig("o_taken"), 32)
            for t in range(TC):
                for g in range(2):
                    V.tensor_scalar(o_tok[:, t, g * 512:(g + 1) * 512], o_tok[:, t, g * 512:(g + 1) * 512],
                                    o_rstd[:, 2 * t + g:2 * t + g + 1], None, ALU.mult).then_inc(sig("o_norm"), 1)
            for half in range(2):
                c_ = slice(half * 512, (half + 1) * 512)
                dve.wait_ge(sig("o_used"), 2 * (half + 1))
                for t in range(TC):
                    V.scalar_tensor_tensor(h1[:, t, c_], h[:, t, c_], ALPHA, ps[:, 4 * half + t, :], ALU.mult, ALU.add).then_inc(sig("mix_taken"), 1)
            dve.wait_ge(sig("mix_taken"), 2 * TC)
            for t in range(TC):
                for q in range(2):
                    st.go(V.bn_stats(st_h[:, t, 6 * q:6 * q + 6], h1[:, t, q * 512:(q + 1) * 512]))
                st.wait()
                st.link(V.bn_aggr(bn_mv[:, t, :], st_h[:, t, :]))
                i = V.tensor_copy(ln_var[:, t:t + 1], bn_mv[:, t, 1:2])
                if t < TC - 1:
                    st.go(i)
            i.then_inc(sig("ln1_var"), 1)
            dve.wait_ge(sig("ln1_rstd"), 1)
            for t in range(TC):
                st.link(V.tensor_scalar(h1[:, t, :], h1[:, t, :], bn_mv[:, t, 0:1], ln_rstd[:, t:t + 1], ALU.subtract, ALU.mult))
                st.link(V.tensor_tensor(h1[:, t, :], h1[:, t, :], rows[:, 0, :], ALU.mult))
                V.tensor_tensor(h1[:, t, :], h1[:, t, :], rows[:, 1, :], ALU.add).then_inc(sig("h1_ready"), 1)
            dve.wait_ge(sig("logits_ps"), 1)
            st.link(V.tensor_tensor(logit, ps[:, 2, 0:TC * E].rearrange("p (t e) -> p t e", t=TC),
                                    rows[:, 2, 2 * P:2 * P + E].rearrange("p (o e) -> p o e", o=1).to_broadcast([P, TC, E]), ALU.add))
            for t in range(TC):
                st.link(V.max(v8[:, t, :], logit[:, t, :]))
                st.go(V.max_index(i8[:, t, :], v8[:, t, :], logit[:, t, :]))
            st.wait()
            V.tensor_scalar(nv0.rearrange("p (t o) -> p t o", o=1), v8[:, :, 0:1], -1.0, None, ALU.mult).then_inc(sig("best"), 1)
            st.link(V.tensor_copy(if4.rearrange("p (t k) -> p t k", t=TC), i8[:, :, 0:TOPK]))

            def spread(x, n):
                return x.rearrange("p (m o) -> p m o", o=1).to_broadcast([P, x.shape[1], n])

            st.link(V.tensor_tensor(mk, cst("iota", 0, E).rearrange("p (o e) -> p o e", o=1).to_broadcast([P, TC * TOPK, E]),
                                    spread(if4, E), ALU.is_equal))

            def over_k(x):
                return x.rearrange("p (t k) e -> p t e k", t=TC)

            V.tensor_reduce(routed, over_k(mk), AX.X, ALU.add).then_inc(sig("routed"), 1)
            st.link(V.tensor_tensor(mkt, mk, spread(cst("dst"), E), ALU.mult))
            st.link(V.tensor_reduce(dst, over_k(mkt), AX.X, ALU.add))
            dve.wait_ge(sig("gate_exp"), TC)
            st.link(V.reciprocal(gsum, gsum))
            st.link(V.tensor_tensor(gates, gates, spread(gsum, TOPK), ALU.mult))
            st.link(V.tensor_tensor(mkt, mk, spread(gates.rearrange("p t k -> p (t k)"), E), ALU.mult))
            V.tensor_reduce(gmat, over_k(mkt), AX.X, ALU.add).then_inc(sig("gmat"), 1)
            dve.wait_ge(sig("places_ps"), 1)
            dve.wait_ge(sig("routed"), 1)
            st.link(V.scalar_tensor_tensor(posm.rearrange("p t e -> p (t e)"), ps[:, 3, 0:TC * E], 1.0, routed.rearrange("p t e -> p (t e)"), ALU.add, ALU.mult))
            st.go(V.tensor_scalar(posm, posm, -1.0, None, ALU.add))
            for t in range(3):
                st.go(V.tensor_scalar(flags[:, :, t], ps[:, 3, TC * E:(TC + 1) * E], float(P * (t + 1)), None, ALU.is_gt))
            st.wait()
            fl = flags.rearrange("p e t -> p (e t)")
            st.link(V.tensor_tensor_scan(fsum, cst("ones", 0, 96), fl, 0.0, ALU.mult, ALU.add))
            st.link(V.scalar_tensor_tensor(feq, fsum, cst("part1"), fl, ALU.is_equal, ALU.mult))
            st.link(V.tensor_tensor(ftmp, feq, cst("over_e"), ALU.mult))
            st.link(V.tensor_reduce(ev, ftmp, AX.X, ALU.add))
            st.link(V.tensor_tensor(ftmp, feq, cst("over_t"), ALU.mult))
            st.link(V.tensor_reduce(tv, ftmp, AX.X, ALU.add))
            st.link(V.tensor_scalar(tv, tv, NONE, None, ALU.add))
            for q, x in enumerate((ev, tv)):
                V.tensor_scalar(evb[:, q, :], cst("ones"), x, None, ALU.mult).then_inc(sig("over_ready"), 1)
            st.go(V.tensor_copy(elist[:, 0:E], cst("iota", 0, E)))
            st.go(V.memset(tlist[:, 0:E], 0.0))
            dve.wait_ge(sig("list_ps"), 1)
            st.go(V.tensor_copy(elist[:, E:2 * E], ps[:, 3, 0:E]))
            V.tensor_copy(tlist[:, E:2 * E], ps[:, 3, E:2 * E]).then_inc(sig("list_ready"), 1)
            st.wait()
            V.tensor_copy(eint[0:1, :], elist[0:1, :]).then_inc(sig("list_ready"), 1)
            V.tensor_scalar(nint[0:1, :], fsum[0:1, 95:96], float(E), None, ALU.add).then_inc(sig("list_ready"), 1)
            dve.wait_ge(sig("h1_stored"), 16 * TC)
            for c in range(TC):
                for q in range(2):
                    dve.wait_ge(sig("bdown_ps"), 2 * c + q + 1)
                    x = h1[:, c, q * 512:(q + 1) * 512]
                    V.scalar_tensor_tensor(x, x, ALPHA, ps[:, 4 + 2 * (c % 2) + q, :], ALU.mult, ALU.add).then_inc(sig("acc"), 1)
            st.link(V.tensor_scalar(dcur[:, :, 0], cst("tok"), -NONE, None, ALU.add))
            dve.wait_ge(sig("list_ready"), 3)

            class ItemSteps:
                def __init__(self, i, per, before):
                    self.i, self.per, self.before, self.n = i, per, before, 0

                def link(self, ins):
                    self.n += 1
                    ins.then_inc(sig("item_step"), 1)
                    dve.wait_ge(sig("item_step"), self.i * self.per + (self.before + self.n))

            PER = 5

            def slots_of(m, s):
                e = dve.value_load(eint[0:1, bass.ds(m, 1)], min_val=0, max_val=E - 1)
                s.link(V.tensor_tensor(cur.rearrange("p (t o) -> p t o", o=1), posm[:, :, bass.ds(e, 1)],
                                       tlist[:, bass.ds(m, 1)].rearrange("p (t o) -> p t o", o=1).to_broadcast([P, TC, 1]), ALU.subtract))
                s.link(V.tensor_copy(dcur[:, :, 1:2], dst[:, :, bass.ds(e, 1)]))
                V.tensor_tensor(oh, cst("iota").rearrange("p (o e) -> p o e", o=1).to_broadcast([P, TC, P]), spread(cur, P),
                                ALU.is_equal).then_inc(sig("oh_ready"), 1)

            def expert_of(m):
                e = dve.value_load(eint[0:1, bass.ds(m, 1)], min_val=0, max_val=E - 1)
                V.tensor_copy(eo[0:E, :], cst("ident", 0, E, E)[:, bass.ds(e, 1)].to_broadcast([E, P])).then_inc(sig("eo_ready"), 1)

            def row_numbers(s, signal):
                s.link(V.tensor_scalar(idx_g[:], ps[:, 4, 0:1], NONE, None, ALU.add))
                V.tensor_scalar(idx_2[:], ps[:, 4, 1:2], NONE, None, ALU.add).then_inc(signal, 1)

            s = ItemSteps(0, 0, 0)
            slots_of(0, s)
            expert_of(0)
            dve.wait_ge(sig("idx_ps"), 1)
            row_numbers(s, sig("idx0_ready"))
            dve.wait_ge(sig("idx0_ready"), 1)
            slots_of(1, s)
            before = s.n
            n_items = dve.value_load(nint[0:1, 0:1], min_val=E, max_val=E + 16)
            with dve.Fori(0, n_items) as i:
                s = ItemSteps(i, PER, before)
                dve.wait_ge(sig("scattered"), i * 16)
                dve.wait_ge(sig("idx_ready"), i)
                V.tensor_copy(idx_s[:], idx_2[:]).then_inc(sig("idxs_ready"), 1)
                dve.wait_ge(sig("idxs_ready"), i + 1)
                dve.wait_ge(sig("idx_ps"), i + 2)
                dve.wait_ge(sig("gathered"), i * 16 + 16)
                row_numbers(s, sig("idx_ready"))
                for half in range(2):
                    dve.wait_ge(sig("moe_used"), i * EXPERT_TILES + 4 * (half + 1))
                    gu = ps[:, 2 * half:2 * half + 2, :].rearrange("p b (n o) -> p (b n) o", o=2)
                    g_, a_ = glu[:, half, :], actv[:, half * 512:(half + 1) * 512]
                    V.tensor_scalar(g_, gu[:, :, 0], LIMIT, None, ALU.min).then_inc(sig("glu_ready"), 1)
                    V.tensor_scalar(a_, gu[:, :, 1], LIMIT, -LIMIT, ALU.min, ALU.max).then_inc(sig("lin_ready"), 1)
                    dve.wait_ge(sig("lin_ready"), i * 2 + (half + 1))
                    dve.wait_ge(sig("glu_ready"), i * 2 + (half + 1))
                    s.link(V.scalar_tensor_tensor(a_, a_, 1.0, g_, ALU.add, ALU.mult))
                    dve.wait_ge(sig("gsig_ready"), i * 2 + (half + 1))
                    V.tensor_tensor(a_, a_, gsig[:, half, :], ALU.mult).then_inc(sig("act_ready"), 1)
                expert_of(i + 1)
                slots_of(i + 2, s)
                dve.wait_ge(sig("moe_used"), i * EXPERT_TILES + EXPERT_TILES)
                V.tensor_copy(ysb, ps[:, 4:6, :].rearrange("p a b -> p (a b)")).then_inc(sig("y_ready"), 1)
                assert s.n == PER, s.n
            dve.wait_ge(sig("acc"), 2 * TC)
            dve.wait_ge(sig("rows3_in"), 32)
            fin = Steps(dve, sig("fin_step"))
            for t in range(TC):
                dve.wait_ge(sig(f"y{t}_in"), 16 * TOPK)
                for k in range(TOPK):
                    fin.link(V.scalar_tensor_tensor(h1[:, t, :], ybuf[t * TOPK + k], gates[:, t, k:k + 1], h1[:, t, :], ALU.mult, ALU.add))
                for q in range(2):
                    fin.go(V.bn_stats(bn_part[:, t, 6 * q:6 * q + 6], h1[:, t, q * 512:(q + 1) * 512]))
                fin.wait()
                fin.link(V.bn_aggr(bn_mv[:, t, :], bn_part[:, t, :]))
                V.tensor_copy(ln_var[:, t:t + 1], bn_mv[:, t, 1:2]).then_inc(sig("ln2_var"), 1)
            for t in range(TC):
                dve.wait_ge(sig("ln2_rstd"), t + 1)
                fin.link(V.tensor_scalar(h1[:, t, :], h1[:, t, :], bn_mv[:, t, 0:1], ln_rstd[:, t:t + 1], ALU.subtract, ALU.mult))
                fin.link(V.tensor_tensor(h1[:, t, :], h1[:, t, :], rows[:, 0, :], ALU.mult))
                V.tensor_tensor(h1[:, t, :], h1[:, t, :], rows[:, 1, :], ALU.add).then_inc(sig("out_ready"), 1)



def _chunks(v):
    return v.reshape(-1, P).T


def _tables():
    import numpy as np

    f = np.float32
    inv = (f(10000.0) ** (-np.arange(0, 64, 2, dtype=f) / f(64))).astype(f)
    pos = np.concatenate([np.arange(META, L), np.arange(META)])
    row = np.concatenate([np.repeat(np.arange(T // 64), 64), np.full(META, -1)])
    colm = np.concatenate([np.tile(np.arange(64), T // 64), np.arange(META)])
    ang = [(p.astype(f)[:, None] * inv[None, :]).astype(f) for p in (pos, row, colm)]
    cos, sin = [np.cos(x).astype(f) for x in ang], [np.sin(x).astype(f) for x in ang]
    return np.ascontiguousarray(np.concatenate([cos[0], sin[0], cos[1], cos[2], sin[1], sin[2]], axis=1), dtype=f)


def _constants():
    import numpy as np

    c = np.zeros((P, NCONST), np.float32)

    def put(name, value):
        o, n = CONST[name]
        c[:, o:o + n] = value

    p = np.arange(P)
    put("ident", np.eye(P))
    put("ones", 1.0)
    put("mean", 1.0 / D)
    put("before", (p[:, None] < p[None, :]))
    put("iota", p[None, :])
    put("over_e", np.repeat(np.arange(E), 3)[None, :])
    put("over_t", (np.tile([1, 2, 3], E) * P - NONE)[None, :])
    t, k = np.divmod(np.arange(16), TOPK)
    put("dst", k[None, :] * T + t[None, :] * P + p[:, None] - NONE)
    put("part1", p[:, None] + 1)
    put("tok", np.arange(TC)[None, :] * P + p[:, None])
    put("eps6", EPS_RMS)
    put("eps5", EPS_LN2)
    put("hln2", 0.5 * math.log(2.0))
    put("tiny", 1e-37)
    put("one", 1.0)
    return c


def kernel(**inputs):
    import numpy as np
    import concourse.bacc as bacc
    from concourse.bass_utils import run_bass_kernel_spmd

    x = {k: np.asarray(v) for k, v in inputs.items()}
    arrays = {"x": x["x"][0], "xT": x["x"][0].T, "meta_tokens_2": x["meta_tokens_2"], "tab": _tables(), "const": _constants()}
    per_channel = {"c": x["c"][0], "norm_g": x["norm_g"][0], "mod_b": x["mod_b"][0][:2 * D], "lam": x["lam"][0]}
    for k in ("cln_g", "cln_b", "pw2_b", "sc_b", "br", "bi", "dw_b"):
        per_channel[k] = x[k][0]
    per_channel["g_q_a"], per_channel["g_kv_a"] = x["g_q_a_2"][0], x["g_kv_a_2"][0]
    per_channel["g_o"] = np.concatenate([x["g_o_mla_2"][0], x["g_o_gqa_2"][0]])
    chan = np.zeros((P, NCHAN), np.float32)
    for k, (o, n) in CHAN.items():
        if k in ("sc_w", "dw_w"):
            chan[:, o:o + n] = x[k][0].T.reshape(KD, P, -1).transpose(1, 0, 2).reshape(P, n)
        else:
            chan[:, o:o + n] = _chunks(per_channel[k])
    arrays["chan"] = chan
    arrays["rows"] = np.concatenate([x["mod_b"][0][2 * D:], x["final_g"], x["ln_emb_g_2"], x["ln_emb_b_2"], x["ln1_g_2"][0], x["ln1_b_2"][0],
                                     x["g_q_gqa_2"][0], x["g_k_gqa_2"][0], x["b_router_2"][0], x["ln2_g_2"][0], x["ln2_b_2"][0]])[None, :]
    w = x["w_in"][0].reshape(KD, P, 5 * KD, P)
    cv, cg, cs, lx, ls = (np.arange(KD) + KD * i for i in range(5))
    pairs = np.stack([np.concatenate([cv, lx, cs[0::2]]), np.concatenate([cg, ls, cs[1::2]])], 1)
    arrays["w_in"] = w[:, :, pairs, :].transpose(2, 1, 0, 3, 4).reshape(N_IN, P, TILE)
    for k in ("mod_w", "pw2_w", "w_out", "wr", "wi", "w_in_2", "w_q_b_2", "w_kv_b_2", "w_o_2", "w_router_2", "w_gate_up_2", "b_gate_up_2",
              "w_down_2", "b_down_2"):
        arrays[k] = x[k][0]
    nc = bacc.Bacc("TRN2", target_bir_lowering=False, num_devices=1)
    feeds, a = {}, {}
    for k, v in arrays.items():
        feeds[f"in_{k}"] = np.ascontiguousarray(v)
        a[k] = nc.dram_tensor(f"in_{k}", feeds[f"in_{k}"].shape, F32, kind="ExternalInput").ap()
    h1_dram = nc.dram_tensor("h1_rows", (T, D), F32, kind="Internal").ap()
    y_dram = nc.dram_tensor("y_rows", (TOPK * T, D), F32, kind="Internal").ap()
    out = nc.dram_tensor("out_0", (T, D), F32, kind="ExternalOutput").ap()
    program(nc, a, out, h1_dram, y_dram)
    r = run_bass_kernel_spmd(nc, [feeds], core_ids=[0])
    return r.results[0]["out_0"].reshape(1, T, D)
```

```python
from contextlib import ExitStack
import math

import concourse.bass as bass
from concourse import mybir

F32 = mybir.dt.float32
F32R = mybir.dt.float32r
I32 = mybir.dt.int32
U32 = mybir.dt.uint32
ALU = mybir.AluOpType
ACT = mybir.ActivationFunctionType
AX = mybir.AxisListType

P = 128
D = 1024
KD = D // P
T = 512
TC = T // P
META = 16
L = T + META
LC = TC + 1
TAPS = 31
STAPS = 4
EPS_RMS = 1e-6
EPS_LN1 = 1e-6
EPS_LN2 = 1e-5
ALPHA = 2.0 ** 0.25
E = 32
TOPK = 4
HM = 4
NOPE, ROPE = 128, 64
LIMIT = 7.0
SWALPHA = 1.702
NONE = 4096.0
ITEMS = 64

CHAN = {}
_at = 0
for _name, _n in (("c", 8), ("norm_g", 8), ("mod_b", 16), ("cln_g", 8), ("cln_b", 8), ("pw2_b", 8), ("sc_b", 8),
                  ("br", 8), ("bi", 8), ("lam", 8), ("dw_b", 8), ("sc_w", 8 * STAPS), ("dw_w", 8 * TAPS),
                  ("g_q_a", 2), ("g_kv_a", 1), ("g_o", 8)):
    CHAN[_name] = (_at, _n)
    _at += _n
NCHAN = _at

CONST = {}
_at = 0
for _name, _n in (("ident", P), ("ones", P), ("mean", P), ("before", P), ("iota", P), ("over_e", 96), ("over_t", 96),
                  ("dst", 16), ("part1", 1), ("tok", TC), ("eps6", 1), ("eps5", 1), ("hln2", 1), ("tiny", 1), ("one", 1)):
    CONST[_name] = (_at, _n)
    _at += _n
NCONST = _at

ROWS = {"gate_b": 0, "final_g": 1024, "ln_emb_g": 2048, "ln_emb_b": 3072, "ln1_g": 4096, "ln1_b": 5120, "g_qk": 6144,
        "b_router": 6400, "ln2_g": 6432, "ln2_b": 7456}
NROWS = 8480

RING1 = 3
TILE = 2048
N_MOD, N_IN, N_GATE, N_PW2, N_OUT, N_IN2, N_Q, N_KV, N_O = 8, 20, 4, 4, 8, 6, 1, 1, 4
T_IN = N_MOD
T_GATE = T_IN + N_IN
T_PW2 = T_GATE + N_GATE
T_OUT = T_PW2 + N_PW2
T_IN2 = T_OUT + N_OUT
T_Q = T_IN2 + N_IN2
T_KV = T_Q + N_Q
T_O = T_KV + N_KV
N_PHASE1 = T_O + N_O
EXPERT_TILES = 12
SLOTS = 6
CHUNKS = 2 * EXPERT_TILES
SPLITS = 4
BY_POOL = (6, 13, 18)


class Steps:

    def __init__(self, eng, sem):
        self.eng, self.sem, self.n = eng, sem, 0

    def go(self, ins):
        self.n += 1
        ins.then_inc(self.sem, 1)

    def wait(self):
        self.eng.wait_ge(self.sem, self.n)

    def link(self, ins):
        self.go(ins)
        self.wait()


def program(nc, a, out, h1_dram, y_dram):
    with ExitStack() as ctx:
        sems = {}

        def sig(name):
            if name not in sems:
                sems[name] = ctx.enter_context(nc.semaphore(name))
            return sems[name]

        def sb(name, shape, dt=F32):
            return ctx.enter_context(nc.sbuf_tensor(name, shape, dt))

        ps = ctx.enter_context(nc.psum_tensor("ps", [P, 8, 512], F32))
        ring = sb("ring", [P, RING1, TILE])
        chan = sb("chan", [P, NCHAN])
        const = sb("const", [P, NCONST])
        qk_rows = sb("qk_rows", [P, 2 * P + E])
        small = sb("small", [P, 512])
        ARENA = 29760
        arena = sb("arena", [P, ARENA])
        split = sb("split", [P, SPLITS, 2, D], F32R)
        xTs = sb("xTs", [P, 2, KD, P], F32R)
        aTs = sb("aTs", [P, 2, KD, P], F32R)
        bgu = sb("bgu", [2 * E, 2 * D], F32R)
        eo = sb("eo", [2 * E, P], F32R)

        def ch(name, k=0, n=1):
            o = CHAN[name][0] + k
            return chan[:, o:o + n]

        def cst(name, lo=0, hi=None, p=P):
            o, n = CONST[name]
            return const[0:p, o + lo:o + (n if hi is None else hi)]

        class Area:
            def __init__(self, at=0):
                self.at = at

            def take(self, *shape):
                n = math.prod(shape)
                assert self.at + n <= ARENA, (self.at, n)
                v = arena[:, self.at:self.at + n]
                self.at += n
                if len(shape) == 2:
                    v = v.rearrange("p (a b) -> p a b", b=shape[1])
                if len(shape) == 3:
                    v = v.rearrange("p (a b c) -> p a b c", b=shape[1], c=shape[2])
                return v

        m1 = Area()
        hT = m1.take(KD, T)
        v = m1.take(KD, T + TAPS - 1)
        vc = m1.take(KD, T)
        ylru = m1.take(KD, T)
        sgt = m1.take(2, T)
        lxb = m1.take(2, T + STAPS - 1)
        xs = m1.take(2, T)
        lsil = m1.take(2, T)
        lru = m1.take(4, T)
        gates_w = m1.take(2 * KD, P)
        crep = m1.take(KD, P)
        gate1 = m1.take(D)
        rep = m1.take(2, T)
        assert m1.at - 4 * D >= 0
        rows1 = Area(m1.at - 2 * T - D - 3 * D).take(3, D)
        scs = Area(KD * T).take(KD, T)
        x2 = Area(0).take(TC, D)
        m2 = Area(0)
        qnT = m2.take(HM, T)
        rtmp = m2.take(2, 384)
        tab = m2.take(LC, 192)
        assert m2.at <= KD * T
        m2 = Area(KD * T)
        qanT = m2.take(2, T)
        kvanT = m2.take(L)
        krT = m2.take(L)
        qpT = m2.take(2, T)
        AT_H = m2.at
        pr = Area(KD * T).take(2, L)
        wrouter = Area(AT_H - KD * E).take(KD, E)
        h = m2.take(LC, D)
        after_h = m2.at
        hT2 = m2.take(KD, L)
        at_z = m2.at
        zA = m2.take(LC, 448)
        zB = m2.take(TC, 512)
        zC = m2.take(LC, 512)
        knT = m2.take(HM, L)
        qgT = m2.take(4, T)
        kgT = m2.take(2, L)
        rot = m2.take(6 * P)
        pe_rot = m2.take(4 * ROPE + P)
        m2 = Area(at_z)
        vm = m2.take(LC, 512)
        pT = m2.take(2, LC * P)
        junk = Area(at_z).take(D)
        o_tok = Area(after_h).take(TC, D)
        oT = Area(0).take(KD, T)
        h1 = h
        h1T = hT2
        m3 = Area(0)
        xe = m3.take(D)
        ysb = m3.take(D)
        actv = m3.take(D)
        glu = m3.take(2, T)
        gsig = m3.take(2, T)
        oh = m3.take(TC, P)
        posm = m3.take(TC, E)
        dst = m3.take(TC, E)
        assert m3.at <= AT_H - KD * E
        ext = Area(after_h).take(SLOTS - RING1, TILE)
        m3 = Area(after_h + (SLOTS - RING1) * TILE)
        ln_rows = m3.take(2, D)
        bdown = m3.take(D)
        mk = m3.take(TC * TOPK, E)
        mkt = m3.take(TC * TOPK, E)
        routed = m3.take(TC, E)
        gmat = m3.take(TC, E)
        logit = m3.take(TC, E)
        gT = m3.take(T)
        flags = m3.take(E, 3)
        fsum = m3.take(96)
        feq = m3.take(96)
        ftmp = m3.take(96)
        evb = m3.take(2, P)
        elist = m3.take(ITEMS)
        tlist = m3.take(ITEMS)
        v8 = m3.take(TC, 8)
        if4 = m3.take(TC * TOPK)
        gates = m3.take(TC, TOPK)
        cur = m3.take(TC)
        dcur = m3.take(TC, 2)
        ybuf = [x[:, q // 2, (q % 2) * D:(q % 2 + 1) * D] for x in (ext, ring) for q in range(6)]
        back = m3.take(4, D)
        ybuf += [back[:, q, :] for q in range(4)]
        bgu_raw = Area(m3.at - 4 * D).take(2 * D)

        cols = {}
        used = [0]

        def col(name, n=None):
            if name not in cols:
                cols[name] = (used[0], n)
                used[0] += n
                assert used[0] <= 512
            o, n = cols[name]
            return small[:, o:o + n]

        c_act, c_sig, lam_abs, lam_e, lam_neg = (col(n, 8) for n in ("c_act", "c_sig", "lam_abs", "lam_e", "lam_neg"))
        rate, nrate, lam_z, shift, gain = (col(n, 8) for n in ("rate", "nrate", "lam_z", "shift", "gain"))
        x2_ss, x2_ln, x2_rstd = (col(n, TC) for n in ("x2_ss", "x2_ln", "x2_rstd"))
        emb_mean, emb_var, emb_ln, emb_rstd = (col(n, LC) for n in ("emb_mean", "emb_var", "emb_ln", "emb_rstd"))
        bn_part = col("bn_part", 12 * LC).rearrange("p (t s) -> p t s", t=LC)
        bn_mv = col("bn_mv", 2 * LC).rearrange("p (t s) -> p t s", t=LC)
        z_ss, z_ln = col("z_ss", 9 * LC), col("z_ln", 9 * LC)
        nmaxs, psums = col("nmax", 32), col("psum", 32)
        o_ss, o_ln, o_rstd = (col(n, 2 * TC) for n in ("o_ss", "o_ln", "o_rstd"))
        ln_var, ln_ln, ln_rstd = (col(n, TC) for n in ("ln_var", "ln_ln", "ln_rstd"))
        nv0, gsum = col("nv0", TC), col("gsum", TC)
        ev, tv = col("ev", 1), col("tv", 1)
        i8 = sb("i8", [P, TC, 8], U32)
        idx_g = sb("idx_g", [P, 1], I32)
        idx_2 = sb("idx_2", [P, 1], I32)
        idx_s = sb("idx_s", [P, 1], I32)
        eint = sb("eint", [1, ITEMS], I32)
        nint = sb("nint", [1, 1], I32)

        def rows_of(t):
            return P if t < TC else META

        ONE = cst("one")
        IDENT = cst("ident")

        tile_ready = [sig(f"tile{s}_ready") for s in range(SLOTS)]

        def wait_tile(eng, n):
            eng.wait_ge(tile_ready[n % RING1], 16 * (n // RING1 + 1))

        def tile(n):
            return ring[:, n % RING1, :]

        def last_use(n):
            if n < T_IN:
                return sig("mod_used"), n + 1
            if n < T_GATE:
                return sig("u_ready"), 2 * (n - T_IN) + 2
            if n < T_PW2:
                return sig("gate_used"), n - T_GATE + 1
            if n < T_OUT:
                return sig("pw2_ready"), 2 * (n - T_PW2) + 2
            if n < T_IN2:
                return sig("out_used"), n - T_OUT + 1
            if n < T_Q:
                return sig("z_ready"), (LC, LC + TC, 2 * LC + TC)[(n - T_IN2) // 2]
            if n == T_Q:
                return sig("qp_ps"), TC
            if n == T_KV:
                return sig("vm_ps"), LC
            return sig("o_used"), n - T_O + 1

        UNITS = [(hh, qt) for hh in range(8) for qt in range(TC)]

        loads_before = [len([n for n in range(N_PHASE1) if n % RING1 == s_]) if s_ < RING1 else 0 for s_ in range(SLOTS)]

        def low_ready(i, c):
            if c in BY_POOL:
                return sig("lo_pool"), i * len(BY_POOL) + (BY_POOL.index(c) + 1)
            return sig("lo_ready"), i * (CHUNKS - len(BY_POOL)) + len([x for x in range(c + 1) if x not in BY_POOL])

        def low_chunk(tt, i, c):
            return tt(split[:, c % SPLITS, 1, :], chunk(c), split[:, c % SPLITS, 0, :], ALU.subtract).then_inc(low_ready(0, c)[0], 1)

        def both_rows(tt, e):
            ident = cst("ident", 0, 2 * E, 2 * E)
            return tt(eo[:], ident[:, bass.ds(e, 1)].to_broadcast([2 * E, P]), ident[:, bass.ds(e + E, 1)].to_broadcast([2 * E, P]),
                      ALU.add).then_inc(sig("eo_ready"), 1)

        def chunk(c):
            j = c // 2 % SLOTS
            x = ring[:, j, :] if j < RING1 else ext[:, j - RING1, :]
            return x[:, (c % 2) * D:(c % 2 + 1) * D]

        def wait_alone(eng, sem, value):
            eng.wait_ge(sig("list_ready"), 1)
            eng.wait_ge(sem, value)
            eng.wait_ge(sig("list_ready"), 2)

        block = ctx.enter_context(nc.Block())

        @block.sync
        def _(sp):
            sp.dma_start(chan[:], a["chan"]).then_inc(sig("chan_in"), 16)
            sp.dma_start(const[:], a["const"]).then_inc(sig("const_in"), 16)

            def load(n, dst, src):
                if n >= RING1:
                    sp.wait_ge(*last_use(n - RING1))
                sp.dma_start(dst, src).then_inc(tile_ready[n % RING1], 16)

            for k in range(N_MOD):
                load(k, tile(k), a["mod_w"][k * P:(k + 1) * P, 0:2 * D])
            for n in range(N_IN):
                load(T_IN + n, tile(T_IN + n), a["w_in"][n])
            for n in range(N_GATE):
                load(T_GATE + n, tile(T_GATE + n).rearrange("p (k n) -> p k n", k=2),
                     a["mod_w"][n * 2 * P:(n + 1) * 2 * P, 2 * D:].rearrange("(k p) n -> p k n", p=P))
            for n in range(N_PW2):
                load(T_PW2 + n, tile(T_PW2 + n).rearrange("p (k n) -> p k n", k=KD),
                     a["pw2_w"][:, n * 256:(n + 1) * 256].rearrange("(k p) n -> p k n", p=P))
            for n in range(N_OUT):
                half, g = n // 4, n % 4
                load(T_OUT + n, tile(T_OUT + n).rearrange("p (k n) -> p k n", k=4),
                     a["w_out"][g * 512:(g + 1) * 512, half * 512:(half + 1) * 512].rearrange("(k p) n -> p k n", p=P))
            for n in range(N_IN2):
                g, kk = n // 2, n % 2
                lo, w = ((0, 448), (448, 512), (960, 512))[g]
                load(T_IN2 + n, tile(T_IN2 + n)[:, 0:4 * w].rearrange("p (k n) -> p k n", k=4),
                     a["w_in_2"][kk * 512:(kk + 1) * 512, lo:lo + w].rearrange("(k p) n -> p k n", p=P))
            load(T_Q, tile(T_Q)[:, 0:1536].rearrange("p (k n) -> p k n", k=2), a["w_q_b_2"].rearrange("(k p) n -> p k n", p=P))
            load(T_KV, tile(T_KV)[:, 0:D], a["w_kv_b_2"][:, :])
            for n in range(N_O):
                half, g = n // 2, n % 2
                load(T_O + n, tile(T_O + n).rearrange("p (k n) -> p k n", k=4),
                     a["w_o_2"][g * 512:(g + 1) * 512, half * 512:(half + 1) * 512].rearrange("(k p) n -> p k n", p=P))
            def expert_tile(j, e):
                x = ring[:, j % SLOTS, :] if j % SLOTS < RING1 else ext[:, j % SLOTS - RING1, :]
                if j < 8:
                    half, g = j // 4, j % 4
                    src = a["w_gate_up_2"][bass.ds(e, 1), g * 256:(g + 1) * 256, half * D:(half + 1) * D]
                else:
                    src = a["w_down_2"][bass.ds(e, 1), (j - 8) * 256:(j - 7) * 256, :]
                sp.dma_start(x.rearrange("p (k n) -> p k n", k=2), src.rearrange("o (k p) n -> p (o k) n", p=P)).then_inc(tile_ready[j % SLOTS], 16)

            for j in range(EXPERT_TILES):
                if j < RING1:
                    sp.wait_ge(*last_use(max(n for n in range(N_PHASE1) if n % RING1 == j)))
                elif j == RING1:
                    sp.wait_ge(sig("logits_ps"), 1)
                elif j >= SLOTS:
                    for c in (2 * (j - SLOTS), 2 * (j - SLOTS) + 1):
                        sp.wait_ge(*low_ready(0, c))
                expert_tile(j, 0)
            sp.wait_ge(sig("list_ready"), 3)
            n_items = sp.value_load(nint[0:1, 0:1], min_val=E, max_val=E + 16)
            with sp.Fori(1, n_items) as i:
                e = sp.value_load(eint[0:1, bass.ds(i, 1)], min_val=0, max_val=E - 1)
                for j in range(EXPERT_TILES):
                    before = (i - 1) if j < SLOTS else i
                    c = 2 * ((j - SLOTS) % EXPERT_TILES)
                    for by_pool in sorted({c in BY_POOL, c + 1 in BY_POOL}):
                        signal, count = low_ready(before, c + 1 if (c + 1 in BY_POOL) == by_pool else c)
                        wait_alone(sp, signal, sp.to_reg(count))
                    expert_tile(j, e)
            wait_alone(sp, sig("scattered"), n_items * 16 + 16)
            for t in range(TC):
                for k in range(TOPK):
                    sp.dma_start(ybuf[t * TOPK + k], y_dram[k * T + t * P:k * T + (t + 1) * P, :]).then_inc(sig(f"y{t}_in"), 16)
            for t in range(TC):
                sp.wait_ge(sig("out_ready"), t + 1)
                sp.dma_start(out[t * P:(t + 1) * P, :], h1[:, t, :]).then_inc(sig("out_written"), 16)
            sp.wait_ge(sig("out_written"), 16 * TC)

        @block.gpsimd
        def _(pool):
            nc.gpsimd.memset(v[:, :, 0:TAPS - 1], 0.0).then_inc(sig("pads_zero"), 1)
            nc.gpsimd.memset(lxb[:, :, 0:STAPS - 1], 0.0).then_inc(sig("pads_zero"), 1)
            pool.wait_ge(sig("gate_used"), N_GATE)
            pool.dma_start(rows1.rearrange("p a b -> p (a b)"),
                           a["rows"][:, ROWS["final_g"]:ROWS["final_g"] + 3 * D].partition_broadcast(P)).then_inc(sig("rows1_in"), 16)
            pool.wait_ge(sig("u_ready"), 2 * N_IN)
            pool.dma_start(x2[:], a["x"].rearrange("(t p) d -> p t d", p=P)).then_inc(sig("xtok_in"), 16)
            pool.wait_ge(sig("out_used"), N_OUT)
            pool.dma_start(h[0:META, TC, :], a["meta_tokens_2"][:, :]).then_inc(sig("meta_in"), 16)

            def load_rows(dst, name, n, signal):
                pool.dma_start(dst, a["rows"][:, ROWS[name]:ROWS[name] + n].partition_broadcast(P)).then_inc(signal, 16)

            pool.wait_ge(sig("h_ready"), LC)
            pool.dma_start(tab[:, 0:TC, :], a["tab"][0:T, :].rearrange("(t p) n -> p t n", p=P)).then_inc(sig("tab_in"), 16)
            pool.dma_start(tab[0:META, TC, :], a["tab"][T:L, :]).then_inc(sig("tab_in"), 16)
            load_rows(qk_rows[:], "g_qk", 2 * P + E, sig("rows2_in"))
            pool.wait_ge(sig("o_taken"), 8 * TC)
            pool.dma_start(wrouter, a["w_router_2"].rearrange("(k p) e -> p k e", p=P)).then_inc(sig("router_in"), 16)
            load_rows(ln_rows[:, 0, :], "ln1_g", D, sig("ln1_rows_in"))
            load_rows(ln_rows[:, 1, :], "ln1_b", D, sig("ln1_rows_in"))
            for q in range(2):
                pool.dma_start(bgu_raw[q * E:(q + 1) * E, :], a["b_gate_up_2"][:, :]).then_inc(sig("bgu_in"), 16)
            pool.dma_start(bdown[0:E, :], a["b_down_2"][:, :]).then_inc(sig("bias_in"), 16)
            for t in range(TC):
                pool.wait_ge(sig("h1_ready"), t + 1)
                pool.dma_start(h1_dram[t * P:(t + 1) * P, :], h1[:, t, :]).then_inc(sig("h1_stored"), 16)
            load_rows(ln_rows[:, 0, :], "ln2_g", D, sig("rows3_in"))
            load_rows(ln_rows[:, 1, :], "ln2_b", D, sig("rows3_in"))
            pool.wait_ge(sig("h1T_ps"), TC)
            pool.wait_ge(sig("o_used"), N_O)
            nc.gpsimd.memset(xe, 0.0).then_inc(sig("xe_zero"), 1)
            pool.wait_ge(sig("xe_zero"), 1)
            pool.wait_ge(sig("h1_stored"), 16 * TC)
            last_token = pool.to_reg(T - 1)
            last_row = pool.to_reg(TOPK * T - 1)

            def gather():
                nc.gpsimd.indirect_dma_start(out=xe, out_offset=None, in_=h1_dram, in_offset=bass.IndirectOffsetOnAxis(idx_g[:, 0:1], 0),
                                             bounds_check=last_token, oob_is_err=False).then_inc(sig("gathered"), 16)

            pool.wait_ge(sig("idx0_ready"), 1)
            gather()
            pool.wait_ge(sig("list_ready"), 3)
            n_items = pool.value_load(nint[0:1, 0:1], min_val=E, max_val=E + 16)

            def scatter():
                nc.gpsimd.indirect_dma_start(out=y_dram, out_offset=bass.IndirectOffsetOnAxis(idx_s[:, 0:1], 0), in_=ysb, in_offset=None,
                                             bounds_check=last_row, oob_is_err=False).then_inc(sig("scattered"), 16)

            def low_part(i, c):
                pool.wait_ge(sig("hi_ready"), i * CHUNKS + (c + 1))
                low_chunk(nc.gpsimd.tensor_tensor, i, c)

            outputs = pool.to_reg(n_items + 1)
            with pool.Fori(1, n_items + 1) as m:
                i = m - 1
                wait_alone(pool, sig("y_ready"), m)
                scatter()
                low_part(i, BY_POOL[0])
                wait_alone(pool, sig("idx_ready"), m)
                gather()
                for c in BY_POOL[1:]:
                    low_part(i, c)
                e = pool.value_load(eint[0:1, bass.ds(m, 1)], min_val=0, max_val=E - 1)
                both_rows(nc.gpsimd.tensor_tensor, e)
                e = pool.value_load(eint[0:1, bass.ds(m + 1, 1)], min_val=0, max_val=E - 1)
                nc.gpsimd.tensor_copy(dcur[:, :, 1:2], dst[:, :, bass.ds(e, 1)])
                nc.gpsimd.tensor_tensor(cur.rearrange("p (t o) -> p t o", o=1), posm[:, :, bass.ds(e, 1)],
                                        tlist[:, bass.ds(m + 1, 1)].rearrange("p (t o) -> p t o", o=1).to_broadcast([P, TC, 1]),
                                        ALU.subtract).then_inc(sig("cur_ready"), 1)
            wait_alone(pool, sig("y_ready"), outputs)
            scatter()
            wait_alone(pool, sig("gathered"), n_items * 16 + 16)

        @block.tensor
        def _(pe):
            mm = nc.tensor.matmul

            def lru_gates(pe, j):
                b = 4 + 2 * (j % 2)
                pe.wait_ge(sig("xs"), j + 1)
                if j >= 2:
                    pe.wait_ge(sig("gates_taken"), 2 * (j - 1))
                if j == 0:
                    pe.wait_ge(sig("gates_in"), 32)
                nc.tensor.matmul(ps[:, b, :], gates_w[:, j, :], xs[:, j % 2, :], start=True, stop=True)
                nc.tensor.matmul(ps[:, b + 1, :], gates_w[:, KD + j, :], xs[:, j % 2, :], start=True, stop=True).then_inc(sig("gates_ps"), 1)

            def channel_mean(pe):
                pe.wait_ge(sig("gates_taken"), 16)
                for k in range(KD):
                    pe.wait_ge(sig("conv"), k + 1)
                    i = nc.tensor.matmul(ps[:, 4, :], cst("mean"), vc[:, k, :], start=(k == 0), stop=(k == KD - 1))
                i.then_inc(sig("mean_ps"), 1)

            def channel_var(pe):
                for k in range(KD):
                    pe.wait_ge(sig("vsq"), k + 1)
                    nc.tensor.matmul(ps[:, 5, :], cst("mean"), rep[:, k % 2, :], start=(k == 0), stop=(k == KD - 1)).then_inc(sig("vsq_summed"), 1)

            def attention(pe):
                mm = nc.tensor.matmul

                def scores(u):
                    hh, qt = UNITS[u]
                    b = 2 * (u % 2)
                    q = slice(qt * P, (qt + 1) * P)
                    if u >= 2:
                        pe.wait_ge(sig("prob"), u - 1)
                    for lo, hi, bb in ((0, T, b), (T, L, b + 1)):
                        dst = ps[:, bb, 0:hi - lo]
                        if hh < HM:
                            pb = ROPE * (hh % 2)
                            mm(dst, qnT[:, hh, q], knT[:, hh, lo:hi], start=True, stop=False)
                            i = mm(dst, qpT[pb:pb + ROPE, hh // 2, q], krT[pb:pb + ROPE, lo:hi], start=False, stop=True)
                        else:
                            i = mm(dst, qgT[:, hh - HM, q], kgT[:, (hh - HM) // 2, lo:hi], start=True, stop=True)
                    i.then_inc(sig("scores_ps"), 1)

                def turn(u):
                    if u >= 1:
                        pe.wait_ge(sig("probT"), 2 * u)
                    pe.wait_ge(sig("prob"), u + 1)
                    for c in range(TC):
                        i = nc.tensor.transpose(ps[:, 4, c * P:(c + 1) * P], pr[:, u % 2, c * P:(c + 1) * P], IDENT)
                    i = nc.tensor.transpose(ps[0:META, 5, 0:P], pr[:, u % 2, T:L], IDENT)
                    i.then_inc(sig("probT_ps"), 1)

                def weigh(u):
                    hh, qt = UNITS[u]
                    pe.wait_ge(sig("probT"), 2 * (u + 1))
                    if u >= 2:
                        pe.wait_ge(sig("o_taken"), u - 1)
                    for c in range(LC):
                        r = rows_of(c)
                        if hh < HM:
                            val = vm[0:r, c, hh * P:(hh + 1) * P]
                        else:
                            val = zC[0:r, c, 256 + (hh - HM) // 2 * P:256 + ((hh - HM) // 2 + 1) * P]
                        i = mm(ps[:, 6 + u % 2, 0:P], pT[0:r, u % 2, c * P:(c + 1) * P], val, start=(c == 0), stop=(c == LC - 1))
                    i.then_inc(sig("o_ps"), 1)

                pe.wait_ge(sig("kn"), HM + 1)
                pe.wait_ge(sig("qpT"), TC)
                scores(0)
                scores(1)
                for u in range(len(UNITS)):
                    turn(u)
                    if u + 2 < len(UNITS):
                        scores(u + 2)
                    weigh(u)

            def item_index(first=False):
                for c in range(TC):
                    i = mm(ps[:, 4, 0:2], oh[:, c, :], dcur[:, c, :], start=(c == 0), stop=(c == TC - 1))
                    if first and c == 0:
                        i.then_inc(sig("split_used"), SPLITS)
                i.then_inc(sig("idx_ps"), 1)

            def turn(x, bank):
                for k in range(4):
                    i = nc.tensor.transpose(ps[:, bank, k * P:(k + 1) * P], x[:, k * P:(k + 1) * P], IDENT)
                return i

            def experts(pe):
                pe.wait_ge(sig("routed"), 1)
                for c in range(TC):
                    for cc in range(c + 1):
                        mm(ps[:, 3, c * E:(c + 1) * E], cst("before") if cc == c else cst("ones"), routed[:, cc, :],
                           start=(cc == 0), stop=(cc == c))
                for c in range(TC):
                    i = mm(ps[:, 3, TC * E:(TC + 1) * E], cst("ones"), routed[:, c, :], start=(c == 0), stop=(c == TC - 1))
                i.then_inc(sig("places_ps"), 1)
                pe.wait_ge(sig("over_ready"), 2)
                for q in range(2):
                    i = mm(ps[:, 3, q * E:(q + 1) * E], evb[0:E, q, :], cst("ident", 0, E, E), start=True, stop=True)
                i.then_inc(sig("list_ps"), 1)
                pe.wait_ge(sig("gmat"), 1)
                for c in range(TC):
                    i = nc.tensor.transpose(ps[0:E, 4, c * P:(c + 1) * P], gmat[:, c, :], IDENT)
                i.then_inc(sig("gT_ps"), 1)
                pe.wait_ge(sig("gT"), 1)
                pe.wait_ge(sig("bias_in"), 16)
                for c in range(TC):
                    if c >= 2:
                        pe.wait_ge(sig("acc"), 2 * (c - 1))
                    for q in range(2):
                        mm(ps[:, 4 + 2 * (c % 2) + q, :], gT[0:E, c * P:(c + 1) * P], bdown[0:E, q * 512:(q + 1) * 512],
                           start=True, stop=True).then_inc(sig("bdown_ps"), 1)
                pe.wait_ge(sig("acc"), 2 * TC)
                pe.wait_ge(sig("oh_ready"), 1)
                pe.wait_ge(sig("bgu_lo"), 1)
                item_index(first=True)
                pe.wait_ge(sig("gathered"), 16)
                turn(xe[:, 0:512], 7).then_inc(sig("xt_ps"), 1)
                turn(xe[:, 512:1024], 6).then_inc(sig("xt_ps"), 1)
                pe.wait_ge(sig("list_ready"), 3)
                n_items = pe.value_load(nint[0:1, 0:1], min_val=E, max_val=E + 16)
                with pe.Fori(0, n_items) as i:

                    def product(c, banks, lhs, k, start, stop):
                        pe.wait_ge(*low_ready(i, c))
                        w = split[:, c % SPLITS]
                        for n_, (x_, w_) in enumerate(((0, 0), (0, 1), (1, 0))):
                            for q in range(2):
                                m = mm(ps[:, banks + q, :], lhs[:, x_, k, :], w[:, w_, q * 512:(q + 1) * 512],
                                       start=(start and n_ == 0), stop=(stop and n_ == 2))
                        m.then_inc(sig("split_used"), 1)

                    pe.wait_ge(sig("eo_ready"), i + 1)
                    pe.wait_ge(sig("xt_lo"), i * 2 + 2)
                    for half in range(2):
                        pe.wait_ge(sig("lin_ready"), i * 2 + (half + 1))
                        for q in range(2):
                            mm(ps[:, 2 * half + q, :], eo[:], bgu[:, half * D + q * 512:half * D + (q + 1) * 512], start=True, stop=False)
                        for k in range(KD):
                            if half == 1 and k == 5:
                                pe.wait_ge(sig("act_ready"), i * 2 + 1)
                                turn(actv[:, 0:512], 6).then_inc(sig("at_ps"), 1)
                            product(8 * half + k, 2 * half, xTs, k, False, k == KD - 1)
                        if half == 0:
                            pe.wait_ge(sig("oh_ready"), i + 2)
                            pe.wait_ge(sig("y_ready"), i + 1)
                            item_index()
                    pe.wait_ge(sig("gathered"), i * 16 + 32)
                    turn(xe[:, 0:512], 7).then_inc(sig("xt_ps"), 1)
                    pe.wait_ge(sig("idx_ready"), i + 1)
                    for k in range(KD):
                        if k == 3:
                            pe.wait_ge(sig("act_ready"), i * 2 + 2)
                            pe.wait_ge(sig("at_lo"), i * 2 + 3)
                            turn(actv[:, 512:1024], 6).then_inc(sig("at_ps"), 1)
                        if k == 4:
                            pe.wait_ge(sig("at_lo"), i * 2 + 4)
                        if k == 5:
                            turn(xe[:, 512:1024], 6).then_inc(sig("xt_ps"), 1)
                        product(16 + k, 4, aTs, k, k == 0, k == KD - 1)

            pe.wait_ge(sig("c_act"), 1)
            for k in range(KD):
                wait_tile(pe, k)
                for m in range(16):
                    i = mm(ps[:, 0, m:m + 1], tile(k)[:, m * P:(m + 1) * P], c_act[:, k:k + 1],
                           start=(k == 0 and m == 0), stop=(k == KD - 1), skip_group_check=True)
                i.then_inc(sig("mod_used"), 1)
            pe.wait_ge(sig("const_in"), 16)
            for k in range(KD):
                pe.wait_ge(sig("xsq"), k + 1)
                mm(ps[:, 1, :], cst("mean"), rep[:, k % 2, :], start=(k == 0), stop=(k == KD - 1)).then_inc(sig("xsq_summed"), 1)
            for n in range(N_IN):
                wait_tile(pe, T_IN + n)
                if n == 0:
                    pe.wait_ge(sig("hT"), KD)
                if n >= 2:
                    pe.wait_ge(sig("u_taken"), n - 1)
                w = tile(T_IN + n).rearrange("p (k n) -> p k n", k=KD)
                for half in range(2):
                    for k in range(KD):
                        i = mm(ps[:, 2 * (n % 2) + half, :], w[:, k, half * P:(half + 1) * P], hT[:, k, :],
                               start=(k == 0), stop=(k == KD - 1))
                    i.then_inc(sig("u_ready"), 1)
                if 9 <= n <= 16:
                    lru_gates(pe, n - 9)
                if n == 17:
                    channel_mean(pe)
            channel_var(pe)
            pe.wait_ge(sig("crep"), KD)
            for n in range(N_GATE):
                wait_tile(pe, T_GATE + n)
                w = tile(T_GATE + n).rearrange("p (k n) -> p k n", k=2)
                for kk in range(2):
                    k = 2 * n + kk
                    for half in range(2):
                        i = mm(ps[:, 6 + half, :], crep[:, k, :], w[:, kk, half * 512:(half + 1) * 512],
                               start=(k == 0), stop=(k == KD - 1))
                i.then_inc(sig("gate_used"), 1)
            pe.wait_ge(sig("u_taken"), N_IN)
            for n in range(N_PW2):
                wait_tile(pe, T_PW2 + n)
                w = tile(T_PW2 + n).rearrange("p (k n) -> p k n", k=KD)
                for half in range(2):
                    m = 2 * n + half
                    if m >= 4:
                        pe.wait_ge(sig("yconv"), m - 3)
                    for k in range(KD):
                        if m == 0:
                            pe.wait_ge(sig("vln"), k + 1)
                        i = mm(ps[:, m % 4, :], w[:, k, half * P:(half + 1) * P], vc[:, k, :],
                               start=(k == 0), stop=(k == KD - 1))
                    i.then_inc(sig("pw2_ready"), 1)
            pe.wait_ge(sig("yconv"), KD)
            pe.wait_ge(sig("ylru"), KD)
            pe.wait_ge(sig("gate1"), 2)
            for n in range(N_OUT):
                half, g = n // 4, n % 4
                wait_tile(pe, T_OUT + n)
                w = tile(T_OUT + n).rearrange("p (k n) -> p k n", k=4)
                for kk in range(4):
                    k = 4 * g + kk
                    src = scs[:, k, :] if k < KD else ylru[:, k - KD, :]
                    for t in range(TC):
                        i = mm(ps[:, 4 * half + t, :], src[:, t * P:(t + 1) * P], w[:, kk, :],
                               start=(k == 0), stop=(k == 2 * KD - 1))
                i.then_inc(sig("out_used"), 1)
            for t in range(LC):
                r = rows_of(t)
                b = 2 * (t % 2)
                if t < 2:
                    pe.wait_ge(sig("x2"), 2 * TC)
                pe.wait_ge(sig("h_ready"), t + 1)
                if t >= 2:
                    pe.wait_ge(sig("hT2"), 2 * (t - 1))
                for k in range(KD):
                    i = nc.tensor.transpose(ps[:, b + k // 4, (k % 4) * P:(k % 4) * P + r], h[0:r, t, k * P:(k + 1) * P],
                                            cst("ident", 0, r, r))
                    if k % 4 == 3:
                        i.then_inc(sig("hT2_ps"), 1)
            unit = 0
            for g in range(3):
                wd = (448, 512, 512)[g]
                for t in range(LC):
                    if g == 1 and t == TC:
                        continue
                    r = rows_of(t)
                    b = 4 + unit % 4
                    if unit >= 4:
                        pe.wait_ge(sig("z"), unit - 3)
                    for k in range(KD):
                        if t == 0 and k % 4 == 0:
                            wait_tile(pe, T_IN2 + 2 * g + k // 4)
                        if unit == 0 and k == 0:
                            pe.wait_ge(sig("hT2"), 2 * LC)
                        w = tile(T_IN2 + 2 * g + k // 4)[:, 0:4 * wd].rearrange("p (k n) -> p k n", k=4)
                        i = mm(ps[0:r, b, 0:wd], hT2[:, k, t * P:t * P + r], w[:, k % 4, :],
                               start=(k == 0), stop=(k == KD - 1))
                    i.then_inc(sig("z_ready"), 1)
                    unit += 1
            for t in range(LC):
                r = rows_of(t)
                pe.wait_ge(sig("small_qk"), t + 1)
                if t >= 1:
                    pe.wait_ge(sig("turned"), 3 * t)
                ident = cst("ident", 0, r, r)
                for j in range(4):
                    if j < 2 and t == TC:
                        continue
                    src = zA[0:r, t, j * P:(j + 1) * P] if j < 3 else pe_rot[0:r, 4 * ROPE:4 * ROPE + P]
                    i = nc.tensor.transpose(ps[:, 0, j * P:j * P + r], src, ident)
                i.then_inc(sig("turned_ps"), 1)
                for j in range(4):
                    if t < TC:
                        i = nc.tensor.transpose(ps[:, 1, j * P:j * P + r], rot[0:r, j * P:(j + 1) * P], ident)
                if t < TC:
                    i.then_inc(sig("turned_ps"), 1)
                for j in range(2):
                    i = nc.tensor.transpose(ps[:, 2, j * P:j * P + r], rot[0:r, (4 + j) * P:(5 + j) * P], ident)
                i.then_inc(sig("turned_ps"), 1)
            pe.wait_ge(sig("turned"), 3 * LC - 1)
            wait_tile(pe, T_Q)
            wq = tile(T_Q)[:, 0:1536].rearrange("p (k n) -> p k n", k=2)
            for j in range(HM):
                for k in range(2):
                    i = mm(ps[:, 4 + j, :], wq[:, k, j * 192:j * 192 + P], qanT[:, k, :], start=(k == 0), stop=(k == 1))
                i.then_inc(sig("qn_ps"), 1)
            for t in range(TC):
                for k in range(2):
                    i = mm(ps[:, 0, 0:256], qanT[:, k, t * P:(t + 1) * P],
                           wq[:, k, :].rearrange("p (h n) -> p h n", h=HM)[:, :, P:192], start=(k == 0), stop=(k == 1))
                i.then_inc(sig("qp_ps"), 1)
                pe.wait_ge(sig("qp_rot"), t + 1)
                for j in range(2):
                    i = nc.tensor.transpose(ps[:, 1, j * P:(j + 1) * P], pe_rot[:, j * P:(j + 1) * P], IDENT)
                i.then_inc(sig("qpT_ps"), 1)
                pe.wait_ge(sig("qpT"), t + 1)
            wait_tile(pe, T_KV)
            wkv = tile(T_KV)[:, 0:D]
            for j in range(HM):
                pe.wait_ge(sig("qn"), j + 1)
                mm(ps[:, 4 + j, :], wkv[:, j * 256:j * 256 + P], kvanT[:, 0:T], start=True, stop=True).then_inc(sig("kn_ps"), 1)
            for j in range(HM):
                i = mm(ps[:, 3, j * META:(j + 1) * META], wkv[:, j * 256:j * 256 + P], kvanT[:, T:L], start=True, stop=True)
            i.then_inc(sig("kn_ps"), 1)
            for t in range(LC):
                r = rows_of(t)
                if t >= 1:
                    pe.wait_ge(sig("vm"), t)
                i = mm(ps[0:r, 2, :], kvanT[:, t * P:t * P + r],
                       wkv.rearrange("p (h n) -> p h n", h=HM)[:, :, P:256], start=True, stop=True)
                i.then_inc(sig("vm_ps"), 1)
            pe.wait_ge(sig("vm"), LC)
            attention(pe)
            for t in range(TC):
                pe.wait_ge(sig("o_norm"), 2 * (t + 1))
                if t >= 1:
                    pe.wait_ge(sig("oT"), 8 * t)
                for k in range(KD):
                    i = nc.tensor.transpose(ps[:, k // 4, (k % 4) * P:(k % 4 + 1) * P], o_tok[:, t, k * P:(k + 1) * P], IDENT)
                i.then_inc(sig("oT_ps"), 1)
            pe.wait_ge(sig("oT"), 8 * TC)
            for n in range(N_O):
                half, g = n // 2, n % 2
                wait_tile(pe, T_O + n)
                w = tile(T_O + n).rearrange("p (k n) -> p k n", k=4)
                for kk in range(4):
                    k = 4 * g + kk
                    for t in range(TC):
                        i = mm(ps[:, 4 * half + t, :], oT[:, k, t * P:(t + 1) * P], w[:, kk, :],
                               start=(k == 0), stop=(k == KD - 1))
                i.then_inc(sig("o_used"), 1)
            for t in range(TC):
                pe.wait_ge(sig("h1_ready"), t + 1)
                if t == 0:
                    pe.wait_ge(sig("mix_taken"), 2 * TC)
                if t >= 1:
                    pe.wait_ge(sig("h1T"), 2 * t)
                for k in range(KD):
                    i = nc.tensor.transpose(ps[:, k // 4, (k % 4) * P:(k % 4 + 1) * P], h1[:, t, k * P:(k + 1) * P], IDENT)
                i.then_inc(sig("h1T_ps"), 1)
            pe.wait_ge(sig("h1T"), 2 * TC)
            pe.wait_ge(sig("router_in"), 16)
            for t in range(TC):
                for k in range(KD):
                    i = mm(ps[:, 2, t * E:(t + 1) * E], h1T[:, k, t * P:(t + 1) * P], wrouter[:, k, :],
                           start=(k == 0), stop=(k == KD - 1))
            i.then_inc(sig("logits_ps"), 1)
            experts(pe)

        @block.scalar
        def _(act):
            A = nc.scalar.activation
            st = Steps(act, sig("act_step"))
            for k in range(KD):
                act.dma_start(hT[:, k, :], a["xT"][k * P:(k + 1) * P, :]).then_inc(sig("xT_in"), 16)
            act.dma_start(gates_w[:, 0:KD, :], a["wr"].rearrange("h d e -> d h e")).then_inc(sig("gates_in"), 16)
            act.dma_start(gates_w[:, KD:, :], a["wi"].rearrange("h d e -> d h e")).then_inc(sig("gates_in"), 16)
            act.dma_start(gate1[:], a["rows"][:, ROWS["gate_b"]:ROWS["gate_b"] + D].partition_broadcast(P)).then_inc(sig("gateb_in"), 16)
            act.wait_ge(sig("chan_in"), 16)
            A(c_sig, ch("c", 0, 8), ACT.Sigmoid).then_inc(sig("c_sig"), 1)
            act.wait_ge(sig("xT_in"), 16 * KD)
            for k in range(KD):
                if k >= 2:
                    act.wait_ge(sig("xsq_summed"), k - 1)
                A(rep[:, k % 2, :], hT[:, k, :], ACT.Square).then_inc(sig("xsq"), 1)
            act.wait_ge(sig("xsq_summed"), KD)
            act.wait_ge(sig("const_in"), 16)
            st.link(A(rep[:, 0, :], ps[:, 1, :], ACT.Ln, bias=cst("eps6")))
            A(rep[:, 1, :], rep[:, 0, :], ACT.Exp, scale=-0.5).then_inc(sig("rstd_x"), 1)
            act.wait_ge(sig("lam_abs"), 1)
            A(lam_e, lam_abs, ACT.Exp, scale=-1.0).then_inc(sig("lam_exp"), 1)

            def lru_act(j):
                r, ig, s, al = (lru[:, q, :] for q in range(4))
                b = 4 + 2 * (j % 2)
                act.wait_ge(sig("gates_ps"), j + 1)
                if j == 0:
                    act.wait_ge(sig("rate"), 1)
                if j >= 1:
                    act.wait_ge(sig("ylru"), j)
                A(r, ps[:, b, :], ACT.Sigmoid, bias=ch("br", j)).then_inc(sig("gates_taken"), 1)
                A(ig, ps[:, b + 1, :], ACT.Sigmoid, bias=ch("bi", j)).then_inc(sig("gates_taken"), 1)
                act.wait_ge(sig("gates_taken"), 2 * j + 2)
                st.go(A(s, r, ACT.Tanh, scale=rate[:, j:j + 1]))
                A(al, r, ACT.Exp, scale=nrate[:, j:j + 1]).then_inc(sig("a_ready"), 1)
                st.wait()
                act.wait_ge(sig("a_ready"), j + 1)
                st.link(A(r, s, ACT.Ln, bias=cst("tiny")))
                A(s, s, ACT.Ln, bias=ONE).then_inc(sig("logs"), 1)
                act.wait_ge(sig("logd"), j + 1)
                A(r, r, ACT.Exp, scale=0.5, bias=cst("hln2")).then_inc(sig("mult"), 1)

            for n in range(N_IN):
                b = 2 * (n % 2)
                act.wait_ge(sig("u_ready"), 2 * n + 2)
                if n >= 2:
                    act.wait_ge(sig("u_taken"), n - 1)
                A(sgt[:, n % 2, :], ps[:, b + 1, :], ACT.Sigmoid).then_inc(sig("u_sig"), 1)
                if n >= 16:
                    if n < 18:
                        act.wait_ge(sig("ylru"), n - 9)
                    A(lsil[:, n % 2, :], ps[:, b, :], ACT.Sigmoid).then_inc(sig("u_sig2"), 1)
                if 9 <= n <= 16:
                    lru_act(n - 9)
            for k in range(KD):
                act.wait_ge(sig("vcent"), k + 1)
                if k >= 2:
                    act.wait_ge(sig("vsq_summed"), k - 1)
                A(rep[:, k % 2, :], vc[:, k, :], ACT.Square).then_inc(sig("vsq"), 1)
            act.wait_ge(sig("vsq_summed"), KD)
            st.link(A(rep[:, 0, :], ps[:, 5, :], ACT.Ln, bias=cst("eps6")))
            A(rep[:, 1, :], rep[:, 0, :], ACT.Exp, scale=-0.5).then_inc(sig("rstd_v"), 1)
            act.wait_ge(sig("u_taken"), N_IN)
            for k in range(KD):
                act.wait_ge(sig("vscaled"), k + 1)
                if k >= 2:
                    act.wait_ge(sig("vln"), k - 1)
                A(sgt[:, k % 2, :], vc[:, k, :], ACT.Sigmoid, bias=ch("cln_b", k)).then_inc(sig("v_sig"), 1)
            for t in range(TC):
                act.wait_ge(sig("x2"), TC + t + 1)
                st.link(A(junk, x2[:, t, :], ACT.Square, accum_out=x2_ss[:, t:t + 1]))
            st.link(A(x2_ln, x2_ss, ACT.Ln, scale=1.0 / D, bias=cst("eps6")))
            A(x2_rstd, x2_ln, ACT.Exp, scale=-0.5).then_inc(sig("rstd_x2"), 1)
            act.wait_ge(sig("emb_var"), 1)
            st.link(A(emb_ln, emb_var, ACT.Ln, bias=cst("eps5")))
            A(emb_rstd, emb_ln, ACT.Exp, scale=-0.5).then_inc(sig("emb_rstd"), 1)
            for t in range(LC):
                r = rows_of(t)
                for q in range(2):
                    act.wait_ge(sig("hT2_ps"), 2 * t + q + 1)
                    A(hT2[:, 4 * q:4 * q + 4, t * P:t * P + r],
                      ps[:, 2 * (t % 2) + q, :].rearrange("p (k n) -> p k n", k=4)[:, :, 0:r], ACT.Copy).then_inc(sig("hT2"), 1)
            unit = 0
            for g in range(3):
                z, wd = ((zA, 448), (zB, 512), (zC, 512))[g]
                for t in range(LC):
                    if g == 1 and t == TC:
                        continue
                    r = rows_of(t)
                    act.wait_ge(sig("z_ready"), unit + 1)
                    A(z[0:r, t, :], ps[0:r, 4 + unit % 4, 0:wd], ACT.Copy).then_inc(sig("z"), 1)
                    unit += 1
            act.wait_ge(sig("z_ss"), 1)
            st.link(A(z_ln, z_ss, ACT.Ln, scale=1.0 / P, bias=cst("eps6")))
            A(z_ss, z_ln, ACT.Exp, scale=-0.5).then_inc(sig("z_rstd"), 1)
            for t in range(LC):
                r = rows_of(t)
                tk = slice(t * P, t * P + r)
                act.wait_ge(sig("turned_ps"), 3 * t + 1)
                if t < TC:
                    for k in range(2):
                        st.go(A(qanT[:, k, tk], ps[:, 0, k * P:(k + 1) * P], ACT.Copy, scale=ch("g_q_a", k)))
                st.go(A(kvanT[:, tk], ps[:, 0, 2 * P:2 * P + r], ACT.Copy, scale=ch("g_kv_a")))
                A(krT[:, tk], ps[:, 0, 3 * P:3 * P + r], ACT.Copy).then_inc(sig("turned"), 1)
                st.wait()
                if t < TC:
                    act.wait_ge(sig("turned_ps"), 3 * t + 2)
                    A(qgT[:, :, tk], ps[:, 1, :].rearrange("p (h n) -> p h n", h=4), ACT.Copy).then_inc(sig("turned"), 1)
                act.wait_ge(sig("turned_ps"), 3 * t + (3 if t < TC else 2))
                A(kgT[:, :, tk], ps[:, 2, 0:256].rearrange("p (h n) -> p h n", h=2)[:, :, 0:r], ACT.Copy).then_inc(sig("turned"), 1)
            for j in range(HM):
                act.wait_ge(sig("qn_ps"), j + 1)
                A(qnT[:, j, :], ps[:, 4 + j, :], ACT.Copy).then_inc(sig("qn"), 1)
            for t in range(TC):
                act.wait_ge(sig("qpT_ps"), t + 1)
                A(qpT[:, :, t * P:(t + 1) * P], ps[:, 1, 0:256].rearrange("p (h n) -> p h n", h=2), ACT.Copy).then_inc(sig("qpT"), 1)
            for j in range(HM):
                act.wait_ge(sig("kn_ps"), j + 1)
                A(knT[:, j, 0:T], ps[:, 4 + j, :], ACT.Copy).then_inc(sig("kn"), 1)
            act.wait_ge(sig("kn_ps"), HM + 1)
            A(knT[:, :, T:L], ps[:, 3, 0:HM * META].rearrange("p (h n) -> p h n", h=HM), ACT.Copy).then_inc(sig("kn"), 1)
            for t in range(LC):
                r = rows_of(t)
                act.wait_ge(sig("vm_ps"), t + 1)
                A(vm[0:r, t, :], ps[0:r, 2, :], ACT.Copy).then_inc(sig("vm"), 1)

            def probs(u):
                hh, qt = UNITS[u]
                scale = (NOPE + ROPE) ** -0.5 if hh < HM else P ** -0.5
                act.wait_ge(sig("nmax"), u + 1)
                if u >= 2:
                    act.wait_ge(sig("probT_ps"), u - 1)
                A(pr[:, u % 2, :], ps[:, 2 * (u % 2):2 * (u % 2) + 2, :].rearrange("p a b -> p (a b)")[:, 0:L], ACT.Exp,
                  bias=nmaxs[:, u:u + 1], scale=scale, accum_out=psums[:, u:u + 1]).then_inc(sig("prob"), 1)

            def turned(u):
                act.wait_ge(sig("probT_ps"), u + 1)
                if u >= 2:
                    act.wait_ge(sig("o_ps"), u - 1)
                A(pT[:, u % 2, 0:T], ps[:, 4, :], ACT.Copy).then_inc(sig("probT"), 1)
                A(pT[0:META, u % 2, T:LC * P], ps[0:META, 5, 0:P], ACT.Copy).then_inc(sig("probT"), 1)

            probs(0)
            for u in range(len(UNITS)):
                if u + 1 < len(UNITS):
                    probs(u + 1)
                turned(u)
            for t in range(TC):
                for g in range(2):
                    act.wait_ge(sig("o_taken"), 16 * g + 12 + t + 1)
                    st.link(A(pr[:, g, 0:512], o_tok[:, t, g * 512:(g + 1) * 512], ACT.Square, accum_out=o_ss[:, 2 * t + g:2 * t + g + 1]))
            st.link(A(o_ln, o_ss, ACT.Ln, scale=1.0 / 512, bias=cst("eps6")))
            A(o_rstd, o_ln, ACT.Exp, scale=-0.5).then_inc(sig("o_rstd"), 1)
            for t in range(TC):
                act.wait_ge(sig("oT_ps"), t + 1)
                for k in range(KD):
                    A(oT[:, k, t * P:(t + 1) * P], ps[:, k // 4, (k % 4) * P:(k % 4 + 1) * P], ACT.Copy, scale=ch("g_o", k)).then_inc(sig("oT"), 1)
            act.wait_ge(sig("ln1_var"), 1)
            st.link(A(ln_ln, ln_var, ACT.Ln, bias=cst("eps5")))
            A(ln_rstd, ln_ln, ACT.Exp, scale=-0.5).then_inc(sig("ln1_rstd"), 1)
            for t in range(TC):
                act.wait_ge(sig("h1T_ps"), t + 1)
                for q in range(2):
                    A(h1T[:, 4 * q:4 * q + 4, t * P:(t + 1) * P], ps[:, q, :].rearrange("p (k n) -> p k n", k=4), ACT.Copy).then_inc(sig("h1T"), 1)
            for t in range(TC):
                act.wait_ge(sig("best"), 1)
                A(gates[:, t, :], v8[:, t, 0:TOPK], ACT.Exp, bias=nv0[:, t:t + 1], accum_out=gsum[:, t:t + 1]).then_inc(sig("gate_exp"), 1)
            act.wait_ge(sig("gT_ps"), 1)
            A(gT[0:E, :], ps[0:E, 4, :], ACT.Copy).then_inc(sig("gT"), 1)

            act.wait_ge(sig("bgu_in"), 32)
            A(bgu[:], bgu_raw[0:2 * E, :], ACT.Copy).then_inc(sig("bgu_hi"), 1)

            def high(x, q, bank, signal):
                A(x[:, 0, 4 * q:4 * q + 4, :], ps[:, bank, :].rearrange("p (k n) -> p k n", k=4), ACT.Copy).then_inc(signal, 1)

            for q in range(2):
                act.wait_ge(sig("xt_ps"), q + 1)
                high(xTs, q, 7 - q, sig("xt_hi"))
            act.wait_ge(sig("list_ready"), 3)
            act.wait_ge(sig("gate_exp"), TC)
            A(x2_ln[:, 0:1], ONE, ACT.Sigmoid)
            n_items = act.value_load(nint[0:1, 0:1], min_val=E, max_val=E + 16)

            def output(n):
                act.wait_ge(sig("split_used"), n * CHUNKS + SPLITS)
                act.wait_ge(sig("idxs_ready"), n + 1)
                A(ysb, ps[:, 4:6, :].rearrange("p a b -> p (a b)"), ACT.Copy).then_inc(sig("y_ready"), 1)

            with act.Fori(0, n_items) as i:

                def split_high(lo, hi):
                    for c in range(lo, hi):
                        if c % 2 == 0:
                            j = c // 2
                            act.wait_ge(tile_ready[j % SLOTS], i * 32 + 16 * (loads_before[j % SLOTS] + j // SLOTS + 1))
                        act.wait_ge(sig("split_used"), i * CHUNKS + (c + 1))
                        A(split[:, c % SPLITS, 0, :], chunk(c), ACT.Copy).then_inc(sig("hi_ready"), 1)

                def sigmoid(half):
                    act.wait_ge(sig("glu_ready"), i * 2 + (half + 1))
                    A(gsig[:, half, :], glu[:, half, :], ACT.Sigmoid, scale=SWALPHA).then_inc(sig("gsig_ready"), 1)

                split_high(0, 4)
                output(i)
                split_high(4, 12)
                sigmoid(0)
                split_high(12, 16)
                act.wait_ge(sig("at_ps"), i * 2 + 1)
                high(aTs, 0, 6, sig("at_hi"))
                split_high(16, 19)
                sigmoid(1)
                split_high(19, 20)
                act.wait_ge(sig("xt_ps"), i * 2 + 3)
                high(xTs, 0, 7, sig("xt_hi"))
                split_high(20, 23)
                act.wait_ge(sig("at_ps"), i * 2 + 2)
                high(aTs, 1, 6, sig("at_hi"))
                split_high(23, 24)
                act.wait_ge(sig("xt_ps"), i * 2 + 4)
                high(xTs, 1, 6, sig("xt_hi"))
            output(n_items)
            for t in range(TC):
                act.wait_ge(sig("ln2_var"), t + 1)
                A(ln_ln[:, t:t + 1], ln_var[:, t:t + 1], ACT.Ln, bias=cst("eps5")).then_inc(sig("ln2_log"), 1)
                act.wait_ge(sig("ln2_log"), t + 1)
                A(ln_rstd[:, t:t + 1], ln_ln[:, t:t + 1], ACT.Exp, scale=-0.5).then_inc(sig("ln2_rstd"), 1)

        @block.vector
        def _(dve):
            V = nc.vector
            st = Steps(dve, sig("dve_step"))
            dve.wait_ge(sig("c_sig"), 1)
            V.tensor_tensor(c_act, ch("c", 0, 8), c_sig, ALU.mult).then_inc(sig("c_act"), 1)
            st.link(V.tensor_scalar(lam_neg, ch("lam", 0, 8), -1.0, None, ALU.mult))
            V.tensor_tensor(lam_abs, ch("lam", 0, 8), lam_neg, ALU.max).then_inc(sig("lam_abs"), 1)
            dve.wait_ge(sig("lam_exp"), 1)
            e_, z_, zz, se = lam_e, lam_z, rate, nrate
            st.link(V.tensor_scalar(z_, e_, 2.0, None, ALU.add))
            st.link(V.reciprocal(zz, z_))
            st.link(V.tensor_tensor(z_, zz, e_, ALU.mult))
            st.link(V.tensor_tensor(zz, z_, z_, ALU.mult))
            st.link(V.memset(se, 1.0 / 21))
            for q in range(19, 0, -2):
                st.link(V.tensor_tensor(se, se, zz, ALU.mult))
                st.link(V.tensor_scalar(se, se, 1.0 / q, None, ALU.add))
            st.link(V.tensor_tensor(se, se, z_, ALU.mult))
            st.link(V.tensor_scalar(zz, lam_neg, 0.0, 8.0, ALU.max, ALU.mult))
            st.link(V.tensor_scalar(se, se, 16.0, None, ALU.mult))
            st.link(V.tensor_tensor(zz, zz, se, ALU.add))
            V.tensor_scalar(se, zz, -1.0, None, ALU.mult).then_inc(sig("rate"), 1)
            dve.wait_ge(sig("const_in"), 16)
            for k in range(KD):
                V.tensor_scalar(crep[:, k, :], cst("ones"), c_act[:, k:k + 1], None, ALU.mult).then_inc(sig("crep"), 1)
            dve.wait_ge(sig("mod_used"), N_MOD)
            dve.wait_ge(sig("chan_in"), 16)
            st.go(V.tensor_tensor(shift, ps[:, 0, 0:8], ch("mod_b", 0, 8), ALU.add))
            st.link(V.tensor_tensor(gain, ps[:, 0, 8:16], ch("mod_b", 8, 8), ALU.add))
            st.link(V.scalar_tensor_tensor(gain, gain, 1.0, ch("norm_g", 0, 8), ALU.add, ALU.mult))
            dve.wait_ge(sig("rstd_x"), 1)
            for k in range(KD):
                st.go(V.scalar_tensor_tensor(hT[:, k, :], hT[:, k, :], gain[:, k:k + 1], rep[:, 1, :], ALU.mult, ALU.mult))
            st.wait()
            for k in range(KD):
                V.tensor_scalar(hT[:, k, :], hT[:, k, :], shift[:, k:k + 1], None, ALU.add).then_inc(sig("hT"), 1)

            taps = [(j, q) for j in range(KD) for q in range(TAPS)]
            done = [0]

            def conv_taps(count):
                for _ in range(count):
                    if done[0] == len(taps):
                        return
                    j, q = taps[done[0]]
                    done[0] += 1
                    src = v[:, j, q:q + T]
                    w = ch("dw_w", j * TAPS + q)
                    if q == 0:
                        dve.wait_ge(sig("u_taken"), j + 1)
                        st.link(V.tensor_scalar(vc[:, j, :], src, w, ch("dw_b", j), ALU.mult, ALU.add))
                    else:
                        i = V.scalar_tensor_tensor(vc[:, j, :], src, w, vc[:, j, :], ALU.mult, ALU.add)
                        if q == TAPS - 1:
                            i.then_inc(sig("conv"), 1)
                        else:
                            st.link(i)

            def lru_vec(j):
                r, ig, s, al = (lru[:, q, :] for q in range(4))
                dve.wait_ge(sig("logs"), j + 1)
                V.tensor_tensor(r, r, s, ALU.subtract).then_inc(sig("logd"), 1)
                st.link(V.tensor_tensor(ig, ig, xs[:, j % 2, :], ALU.mult))
                dve.wait_ge(sig("mult"), j + 1)
                dve.wait_ge(sig("a_ready"), j + 1)
                st.link(V.tensor_tensor(ig, ig, r, ALU.mult))
                V.tensor_tensor_scan(s, al, ig, 0.0, ALU.mult, ALU.add).then_inc(sig("scan"), 1)
                dve.wait_ge(sig("scan"), j + 1)
                V.tensor_tensor(ylru[:, j, :], s, lsil[:, j % 2, :], ALU.mult).then_inc(sig("ylru"), 1)

            dve.wait_ge(sig("pads_zero"), 2)
            for n in range(N_IN):
                b = 2 * (n % 2)
                dve.wait_ge(sig("u_ready"), 2 * n + 2)
                dve.wait_ge(sig("u_sig"), n + 1)
                if n < 8:
                    V.tensor_tensor(v[:, n, TAPS - 1:], ps[:, b, :], sgt[:, n % 2, :], ALU.mult).then_inc(sig("u_taken"), 1)
                    conv_taps(22)
                elif n < 16:
                    j = n - 8
                    if j >= 2:
                        dve.wait_ge(sig("ylru"), j - 1)
                    st.go(V.tensor_tensor(lsil[:, j % 2, :], ps[:, b + 1, :], sgt[:, n % 2, :], ALU.mult))
                    V.tensor_copy(lxb[:, j % 2, STAPS - 1:], ps[:, b, :]).then_inc(sig("u_taken"), 1)
                    st.wait()
                    dve.wait_ge(sig("u_taken"), n + 1)
                    x_ = xs[:, j % 2, :]
                    if j == 0:
                        st.wait()
                    st.link(V.tensor_scalar(x_, lxb[:, j % 2, 0:T], ch("sc_w", j * STAPS), ch("sc_b", j), ALU.mult, ALU.add))
                    for q in range(1, STAPS):
                        i = V.scalar_tensor_tensor(x_, lxb[:, j % 2, q:q + T], ch("sc_w", j * STAPS + q), x_, ALU.mult, ALU.add)
                        if q < STAPS - 1:
                            st.link(i)
                    i.then_inc(sig("xs"), 1)
                    conv_taps(6)
                    if j >= 1:
                        lru_vec(j - 1)
                    conv_taps(4)
                else:
                    c = 2 * (n - 16)
                    if n == 16:
                        lru_vec(KD - 1)
                        conv_taps(len(taps))
                    dve.wait_ge(sig("u_sig2"), n - 15)
                    st.go(V.tensor_tensor(scs[:, c, :], ps[:, b, :], lsil[:, n % 2, :], ALU.mult))
                    V.tensor_tensor(scs[:, c + 1, :], ps[:, b + 1, :], sgt[:, n % 2, :], ALU.mult).then_inc(sig("u_taken"), 1)
                    st.wait()
                if n == 18:
                    dve.wait_ge(sig("mean_ps"), 1)
                    for k in range(KD):
                        V.tensor_tensor(vc[:, k, :], vc[:, k, :], ps[:, 4, :], ALU.subtract).then_inc(sig("vcent"), 1)
            dve.wait_ge(sig("rstd_v"), 1)
            for k in range(KD):
                V.scalar_tensor_tensor(vc[:, k, :], vc[:, k, :], ch("cln_g", k), rep[:, 1, :], ALU.mult, ALU.mult).then_inc(sig("vscaled"), 1)
            for k in range(KD):
                dve.wait_ge(sig("v_sig"), k + 1)
                V.scalar_tensor_tensor(vc[:, k, :], vc[:, k, :], ch("cln_b", k), sgt[:, k % 2, :], ALU.add, ALU.mult).then_inc(sig("vln"), 1)
            dve.wait_ge(sig("gateb_in"), 16)
            dve.wait_ge(sig("gate_used"), N_GATE)
            for q in range(2):
                V.scalar_tensor_tensor(gate1[:, q * 512:(q + 1) * 512], ps[:, 6 + q, :], 1.0, gate1[:, q * 512:(q + 1) * 512],
                                       ALU.add, ALU.add).then_inc(sig("gate1"), 1)
            for m in range(KD):
                dve.wait_ge(sig("pw2_ready"), m + 1)
                V.scalar_tensor_tensor(scs[:, m, :], ps[:, m % 4, :], ch("pw2_b", m), scs[:, m, :], ALU.add, ALU.mult).then_inc(sig("yconv"), 1)
            dve.wait_ge(sig("xtok_in"), 16)
            dve.wait_ge(sig("gate1"), 2)
            for half in range(2):
                c_ = slice(half * 512, (half + 1) * 512)
                dve.wait_ge(sig("out_used"), 4 * (half + 1))
                for t in range(TC):
                    tmp = rep[:, t % 2, :]
                    st.link(V.tensor_tensor(tmp, ps[:, 4 * half + t, :], gate1[:, c_], ALU.mult))
                    V.tensor_tensor(x2[:, t, c_], x2[:, t, c_], tmp, ALU.add).then_inc(sig("x2"), 1)
            dve.wait_ge(sig("rows1_in"), 16)
            dve.wait_ge(sig("rstd_x2"), 1)
            dve.wait_ge(sig("meta_in"), 16)
            dve.wait_ge(sig("x2"), 2 * TC)
            st.link(V.memset(emb_var, 1.0))
            for t in range(TC):
                st.link(V.scalar_tensor_tensor(h[:, t, :], x2[:, t, :], x2_rstd[:, t:t + 1], rows1[:, 0, :], ALU.mult, ALU.mult))
            st_h = bn_part
            for t in range(LC):
                r = rows_of(t)
                for q in range(2):
                    st.go(V.bn_stats(st_h[0:r, t, 6 * q:6 * q + 6], h[0:r, t, q * 512:(q + 1) * 512]))
                st.wait()
                st.link(V.bn_aggr(bn_mv[0:r, t, :], st_h[0:r, t, :]))
                i = V.tensor_copy(emb_var[0:r, t:t + 1], bn_mv[0:r, t, 1:2])
                if t < LC - 1:
                    st.go(i)
            i.then_inc(sig("emb_var"), 1)
            dve.wait_ge(sig("emb_rstd"), 1)
            for t in range(LC):
                r = rows_of(t)
                st.link(V.tensor_scalar(h[0:r, t, :], h[0:r, t, :], bn_mv[0:r, t, 0:1], emb_rstd[0:r, t:t + 1], ALU.subtract, ALU.mult))
                st.link(V.tensor_tensor(h[0:r, t, :], h[0:r, t, :], rows1[0:r, 1, :], ALU.mult))
                V.tensor_tensor(h[0:r, t, :], h[0:r, t, :], rows1[0:r, 2, :], ALU.add).then_inc(sig("h_ready"), 1)
            ss = z_ss.rearrange("p (t s) -> p t s", t=LC)
            st.link(V.memset(z_ss, 1.0))
            sq = rot
            for t in range(LC):
                r = rows_of(t)
                dve.wait_ge(sig("z"), t + 1)
                st.link(V.tensor_tensor(sq[0:r, 0:384], zA[0:r, t, 0:384], zA[0:r, t, 0:384], ALU.mult))
                st.link(V.tensor_reduce(ss[0:r, t, 0:3], sq[0:r, 0:384].rearrange("p (g n) -> p g n", g=3), AX.X, ALU.add))
                st.link(V.tensor_tensor(ss[0:r, t, 0:1], ss[0:r, t, 0:1], ss[0:r, t, 1:2], ALU.add))
                st.link(V.tensor_scalar(ss[0:r, t, 0:1], ss[0:r, t, 0:1], 0.5, None, ALU.mult))
            for t in range(TC):
                dve.wait_ge(sig("z"), LC + t + 1)
                st.link(V.tensor_tensor(sq[:, 0:512], zB[:, t, :], zB[:, t, :], ALU.mult))
                st.link(V.tensor_reduce(ss[:, t, 3:7], sq[:, 0:512].rearrange("p (g n) -> p g n", g=4), AX.X, ALU.add))
            for t in range(LC):
                r = rows_of(t)
                dve.wait_ge(sig("z"), LC + TC + t + 1)
                st.link(V.tensor_tensor(sq[0:r, 0:256], zC[0:r, t, 0:256], zC[0:r, t, 0:256], ALU.mult))
                i = V.tensor_reduce(ss[0:r, t, 7:9], sq[0:r, 0:256].rearrange("p (g n) -> p g n", g=2), AX.X, ALU.add)
                if t < LC - 1:
                    st.link(i)
            i.then_inc(sig("z_ss"), 1)
            dve.wait_ge(sig("z_rstd"), 1)
            dve.wait_ge(sig("tab_in"), 32)
            dve.wait_ge(sig("rows2_in"), 16)
            rope = rtmp[:, 0, :]
            rope2 = rtmp[:, 1, :]

            def rotate(dst1, dst2, x1, x2_, cos, sin, t1, t2, signal=None):
                st.go(V.tensor_tensor(t1, x1, cos, ALU.mult))
                st.link(V.tensor_tensor(t2, x2_, sin, ALU.mult))
                st.link(V.tensor_tensor(dst1, t1, t2, ALU.subtract))
                st.go(V.tensor_tensor(t1, x1, sin, ALU.mult))
                st.link(V.tensor_tensor(t2, x2_, cos, ALU.mult))
                i = V.tensor_tensor(dst2, t1, t2, ALU.add)
                if signal is None:
                    st.link(i)
                else:
                    i.then_inc(signal, 1)

            for t in range(LC):
                r = rows_of(t)
                if t >= 1:
                    dve.wait_ge(sig("turned_ps"), 3 * t)
                if t < TC:
                    st.go(V.tensor_scalar(zA[0:r, t, 0:256], zA[0:r, t, 0:256], ss[0:r, t, 0:1], None, ALU.mult))
                st.go(V.tensor_scalar(zA[0:r, t, 256:384], zA[0:r, t, 256:384], ss[0:r, t, 2:3], None, ALU.mult))
                c1, s1 = tab[0:r, t, 0:32], tab[0:r, t, 32:64]
                kr = pe_rot[0:r, 4 * ROPE:4 * ROPE + P]
                x1, x2_ = zA[0:r, t, 384:416], zA[0:r, t, 416:448]
                rotate(kr[:, 0:32], kr[:, 32:64], x1, x2_, c1, s1, rope[0:r, 0:32], rope2[0:r, 0:32])
                st.link(V.tensor_copy(kr[:, 64:128], kr[:, 0:64]))
                lo = 0 if t < TC else 4
                if t < TC:
                    for q in range(4):
                        st.go(V.scalar_tensor_tensor(zB[:, t, q * P:(q + 1) * P], zB[:, t, q * P:(q + 1) * P], ss[:, t, 3 + q:4 + q],
                                                     qk_rows[:, 0:P], ALU.mult, ALU.mult))
                for q in range(2):
                    st.go(V.scalar_tensor_tensor(zC[0:r, t, q * P:(q + 1) * P], zC[0:r, t, q * P:(q + 1) * P], ss[0:r, t, 7 + q:8 + q],
                                                 qk_rows[0:r, P:2 * P], ALU.mult, ALU.mult))
                st.wait()
                cs_, sn_ = tab[0:r, t, 64:128], tab[0:r, t, 128:192]
                for z, n_, at in ((zB, 4, 0), (zC, 2, 4)):
                    if at < lo:
                        continue
                    zz_ = z[0:r, t, 0:n_ * P].rearrange("p (h a b n) -> p h a b n", h=n_, a=2, b=2)
                    rr = rot[0:r, at * P:(at + n_) * P].rearrange("p (h a b n) -> p h a b n", h=n_, a=2, b=2)
                    t1 = rope[0:r, 0:n_ * 64].rearrange("p (h a n) -> p h a n", h=n_, a=2)
                    t2 = rope2[0:r, 0:n_ * 64].rearrange("p (h a n) -> p h a n", h=n_, a=2)
                    cc = cs_.rearrange("p (o a n) -> p o a n", o=1, a=2).to_broadcast([r, n_, 2, 32])
                    sn = sn_.rearrange("p (o a n) -> p o a n", o=1, a=2).to_broadcast([r, n_, 2, 32])
                    rotate(rr[:, :, :, 0, :], rr[:, :, :, 1, :], zz_[:, :, :, 0, :], zz_[:, :, :, 1, :], cc, sn, t1, t2,
                           sig("small_qk") if at == 4 else None)
            for t in range(TC):
                dve.wait_ge(sig("qp_ps"), t + 1)
                if t >= 1:
                    dve.wait_ge(sig("qpT_ps"), t)
                qv = ps[:, 0, 0:256].rearrange("p (h b n) -> p h b n", h=HM, b=2)
                dv = pe_rot[:, 0:256].rearrange("p (h b n) -> p h b n", h=HM, b=2)
                c1 = tab[:, t, 0:32].rearrange("p (o n) -> p o n", o=1).to_broadcast([P, HM, 32])
                s1 = tab[:, t, 32:64].rearrange("p (o n) -> p o n", o=1).to_broadcast([P, HM, 32])
                t1 = rope[:, 0:128].rearrange("p (h n) -> p h n", h=HM)
                t2 = rope2[:, 0:128].rearrange("p (h n) -> p h n", h=HM)
                rotate(dv[:, :, 0, :], dv[:, :, 1, :], qv[:, :, 0, :], qv[:, :, 1, :], c1, s1, t1, t2, sig("qp_rot"))

            def nmax(u):
                hh, qt = UNITS[u]
                scale = (NOPE + ROPE) ** -0.5 if hh < HM else P ** -0.5
                dve.wait_ge(sig("scores_ps"), u + 1)
                st.link(V.tensor_reduce(nmaxs[:, u:u + 1], ps[:, 2 * (u % 2):2 * (u % 2) + 2, :].rearrange("p a b -> p (a b)")[:, 0:L],
                                        AX.X, ALU.max))
                V.tensor_scalar(nmaxs[:, u:u + 1], nmaxs[:, u:u + 1], -scale, None, ALU.mult).then_inc(sig("nmax"), 1)

            def output(u):
                hh, qt = UNITS[u]
                dve.wait_ge(sig("prob"), u + 1)
                st.link(V.reciprocal(psums[:, u:u + 1], psums[:, u:u + 1]))
                dve.wait_ge(sig("o_ps"), u + 1)
                V.tensor_scalar(o_tok[:, qt, hh * P:(hh + 1) * P], ps[:, 6 + u % 2, 0:P], psums[:, u:u + 1], None, ALU.mult).then_inc(sig("o_taken"), 1)

            nmax(0)
            nmax(1)
            for u in range(len(UNITS)):
                if u + 2 < len(UNITS):
                    nmax(u + 2)
                output(u)
            dve.wait_ge(sig("o_rstd"), 1)
            dve.wait_ge(sig("o_taken"), 32)
            for t in range(TC):
                for g in range(2):
                    V.tensor_scalar(o_tok[:, t, g * 512:(g + 1) * 512], o_tok[:, t, g * 512:(g + 1) * 512],
                                    o_rstd[:, 2 * t + g:2 * t + g + 1], None, ALU.mult).then_inc(sig("o_norm"), 1)
            for half in range(2):
                c_ = slice(half * 512, (half + 1) * 512)
                dve.wait_ge(sig("o_used"), 2 * (half + 1))
                for t in range(TC):
                    V.scalar_tensor_tensor(h1[:, t, c_], h[:, t, c_], ALPHA, ps[:, 4 * half + t, :], ALU.mult, ALU.add).then_inc(sig("mix_taken"), 1)
            dve.wait_ge(sig("mix_taken"), 2 * TC)
            for t in range(TC):
                for q in range(2):
                    st.go(V.bn_stats(st_h[:, t, 6 * q:6 * q + 6], h1[:, t, q * 512:(q + 1) * 512]))
                st.wait()
                st.link(V.bn_aggr(bn_mv[:, t, :], st_h[:, t, :]))
                i = V.tensor_copy(ln_var[:, t:t + 1], bn_mv[:, t, 1:2])
                if t < TC - 1:
                    st.go(i)
            i.then_inc(sig("ln1_var"), 1)
            dve.wait_ge(sig("ln1_rstd"), 1)
            dve.wait_ge(sig("ln1_rows_in"), 32)
            for t in range(TC):
                st.link(V.tensor_scalar(h1[:, t, :], h1[:, t, :], bn_mv[:, t, 0:1], ln_rstd[:, t:t + 1], ALU.subtract, ALU.mult))
                st.link(V.tensor_tensor(h1[:, t, :], h1[:, t, :], ln_rows[:, 0, :], ALU.mult))
                V.tensor_tensor(h1[:, t, :], h1[:, t, :], ln_rows[:, 1, :], ALU.add).then_inc(sig("h1_ready"), 1)
            dve.wait_ge(sig("logits_ps"), 1)
            st.link(V.tensor_tensor(logit, ps[:, 2, 0:TC * E].rearrange("p (t e) -> p t e", t=TC),
                                    qk_rows[:, 2 * P:2 * P + E].rearrange("p (o e) -> p o e", o=1).to_broadcast([P, TC, E]), ALU.add))
            for t in range(TC):
                st.link(V.max(v8[:, t, :], logit[:, t, :]))
                st.go(V.max_index(i8[:, t, :], v8[:, t, :], logit[:, t, :]))
            st.wait()
            V.tensor_scalar(nv0.rearrange("p (t o) -> p t o", o=1), v8[:, :, 0:1], -1.0, None, ALU.mult).then_inc(sig("best"), 1)
            st.link(V.tensor_copy(if4.rearrange("p (t k) -> p t k", t=TC), i8[:, :, 0:TOPK]))

            def spread(x, n):
                return x.rearrange("p (m o) -> p m o", o=1).to_broadcast([P, x.shape[1], n])

            st.link(V.tensor_tensor(mk, cst("iota", 0, E).rearrange("p (o e) -> p o e", o=1).to_broadcast([P, TC * TOPK, E]),
                                    spread(if4, E), ALU.is_equal))

            def over_k(x):
                return x.rearrange("p (t k) e -> p t e k", t=TC)

            V.tensor_reduce(routed, over_k(mk), AX.X, ALU.add).then_inc(sig("routed"), 1)
            st.link(V.tensor_tensor(mkt, mk, spread(cst("dst"), E), ALU.mult))
            st.link(V.tensor_reduce(dst, over_k(mkt), AX.X, ALU.add))
            dve.wait_ge(sig("gate_exp"), TC)
            st.link(V.reciprocal(gsum, gsum))
            st.link(V.tensor_tensor(gates, gates, spread(gsum, TOPK), ALU.mult))
            st.link(V.tensor_tensor(mkt, mk, spread(gates.rearrange("p t k -> p (t k)"), E), ALU.mult))
            V.tensor_reduce(gmat, over_k(mkt), AX.X, ALU.add).then_inc(sig("gmat"), 1)
            dve.wait_ge(sig("places_ps"), 1)
            dve.wait_ge(sig("routed"), 1)
            st.link(V.scalar_tensor_tensor(posm.rearrange("p t e -> p (t e)"), ps[:, 3, 0:TC * E], 1.0, routed.rearrange("p t e -> p (t e)"), ALU.add, ALU.mult))
            st.go(V.tensor_scalar(posm, posm, -1.0, None, ALU.add))
            for t in range(3):
                st.go(V.tensor_scalar(flags[:, :, t], ps[:, 3, TC * E:(TC + 1) * E], float(P * (t + 1)), None, ALU.is_gt))
            st.wait()
            fl = flags.rearrange("p e t -> p (e t)")
            st.link(V.tensor_tensor_scan(fsum, cst("ones", 0, 96), fl, 0.0, ALU.mult, ALU.add))
            st.link(V.scalar_tensor_tensor(feq, fsum, cst("part1"), fl, ALU.is_equal, ALU.mult))
            st.link(V.tensor_tensor(ftmp, feq, cst("over_e"), ALU.mult))
            st.link(V.tensor_reduce(ev, ftmp, AX.X, ALU.add))
            st.link(V.tensor_tensor(ftmp, feq, cst("over_t"), ALU.mult))
            st.link(V.tensor_reduce(tv, ftmp, AX.X, ALU.add))
            st.link(V.tensor_scalar(tv, tv, NONE, None, ALU.add))
            for q, x in enumerate((ev, tv)):
                V.tensor_scalar(evb[:, q, :], cst("ones"), x, None, ALU.mult).then_inc(sig("over_ready"), 1)
            st.go(V.tensor_copy(elist[:, 0:E], cst("iota", 0, E)))
            st.go(V.memset(tlist[:, 0:E], 0.0))
            dve.wait_ge(sig("list_ps"), 1)
            st.go(V.tensor_copy(elist[:, E:2 * E], ps[:, 3, 0:E]))
            V.tensor_copy(tlist[:, E:2 * E], ps[:, 3, E:2 * E]).then_inc(sig("list_ready"), 1)
            st.wait()
            V.tensor_copy(eint[0:1, :], elist[0:1, :]).then_inc(sig("list_ready"), 1)
            V.tensor_scalar(nint[0:1, :], fsum[0:1, 95:96], float(E), None, ALU.add).then_inc(sig("list_ready"), 1)
            dve.wait_ge(sig("h1_stored"), 16 * TC)
            for c in range(TC):
                for q in range(2):
                    dve.wait_ge(sig("bdown_ps"), 2 * c + q + 1)
                    x = h1[:, c, q * 512:(q + 1) * 512]
                    V.scalar_tensor_tensor(x, x, ALPHA, ps[:, 4 + 2 * (c % 2) + q, :], ALU.mult, ALU.add).then_inc(sig("acc"), 1)
            st.link(V.tensor_scalar(dcur[:, :, 0], cst("tok"), -NONE, None, ALU.add))
            dve.wait_ge(sig("list_ready"), 3)

            class ItemSteps:
                def __init__(self, i, per, before):
                    self.i, self.per, self.before, self.n = i, per, before, 0

                def link(self, ins):
                    self.n += 1
                    ins.then_inc(sig("item_step"), 1)
                    dve.wait_ge(sig("item_step"), self.i * self.per + (self.before + self.n))

            PER = 2

            def slots_of(m, s):
                e = dve.value_load(eint[0:1, bass.ds(m, 1)], min_val=0, max_val=E - 1)
                s.link(V.tensor_tensor(cur.rearrange("p (t o) -> p t o", o=1), posm[:, :, bass.ds(e, 1)],
                                       tlist[:, bass.ds(m, 1)].rearrange("p (t o) -> p t o", o=1).to_broadcast([P, TC, 1]), ALU.subtract))
                s.link(V.tensor_copy(dcur[:, :, 1:2], dst[:, :, bass.ds(e, 1)]))
                one_hot()

            def one_hot():
                V.tensor_tensor(oh, cst("iota").rearrange("p (o e) -> p o e", o=1).to_broadcast([P, TC, P]), spread(cur, P),
                                ALU.is_equal).then_inc(sig("oh_ready"), 1)

            def expert_of(m):
                e = dve.value_load(eint[0:1, bass.ds(m, 1)], min_val=0, max_val=E - 1)
                both_rows(V.tensor_tensor, e)

            def row_numbers(signal):
                V.tensor_scalar(idx_2[:], ps[:, 4, 1:2], NONE, None, ALU.add).then_inc(sig("idx2_ready"), 1)
                V.tensor_scalar(idx_g[:], ps[:, 4, 0:1], NONE, None, ALU.add).then_inc(signal, 1)

            def low(x, q, bank, signal):
                V.tensor_tensor(x[:, 1, 4 * q:4 * q + 4, :], ps[:, bank, :].rearrange("p (k n) -> p k n", k=4),
                                x[:, 0, 4 * q:4 * q + 4, :], ALU.subtract).then_inc(signal, 1)

            dve.wait_ge(sig("bgu_hi"), 1)
            V.tensor_tensor(bgu[E:2 * E, :], bgu_raw[E:2 * E, :], bgu[E:2 * E, :], ALU.subtract).then_inc(sig("bgu_lo"), 1)
            V.memset(idx_s[:], int(NONE)).then_inc(sig("idxs_ready"), 1)
            V.memset(glu[:, 0, 0:1], 0.0).then_inc(sig("lin_ready"), 2)
            V.memset(glu[:, 1, 0:1], 0.0).then_inc(sig("at_lo"), 2)
            s = ItemSteps(0, 0, 0)
            slots_of(0, s)
            expert_of(0)
            dve.wait_ge(sig("idx_ps"), 1)
            row_numbers(sig("idx0_ready"))
            slots_of(1, s)
            before = s.n
            for q in range(2):
                dve.wait_ge(sig("xt_hi"), q + 1)
                low(xTs, q, 7 - q, sig("xt_lo"))
            dve.wait_ge(sig("lin_ready"), 2)
            dve.wait_ge(sig("at_lo"), 2)
            n_items = dve.value_load(nint[0:1, 0:1], min_val=E, max_val=E + 16)
            with dve.Fori(0, n_items) as i:
                s = ItemSteps(i, PER, before)

                def split_low(lo, hi):
                    for c in [x for x in range(lo, hi) if x not in BY_POOL]:
                        dve.wait_ge(sig("hi_ready"), i * CHUNKS + (c + 1))
                        low_chunk(V.tensor_tensor, i, c)

                def swiglu(half):
                    dve.wait_ge(sig("split_used"), i * CHUNKS + (8 * (half + 1) + SPLITS))
                    gu = ps[:, 2 * half:2 * half + 2, :].rearrange("p b (n o) -> p (b n) o", o=2)
                    g_, a_ = glu[:, half, :], actv[:, half * 512:(half + 1) * 512]
                    V.tensor_scalar(g_, gu[:, :, 0], LIMIT, None, ALU.min).then_inc(sig("glu_ready"), 1)
                    V.tensor_scalar(a_, gu[:, :, 1], LIMIT, -LIMIT, ALU.min, ALU.max).then_inc(sig("lin_ready"), 1)
                    dve.wait_ge(sig("lin_ready"), i * 2 + (half + 3))
                    dve.wait_ge(sig("glu_ready"), i * 2 + (half + 1))
                    s.link(V.scalar_tensor_tensor(a_, a_, 1.0, g_, ALU.add, ALU.mult))
                    dve.wait_ge(sig("gsig_ready"), i * 2 + (half + 1))
                    V.tensor_tensor(a_, a_, gsig[:, half, :], ALU.mult).then_inc(sig("act_ready"), 1)

                split_low(0, 12)
                dve.wait_ge(sig("scattered"), i * 16 + 16)
                dve.wait_ge(sig("idx2_ready"), i + 1)
                V.tensor_copy(idx_s[:], idx_2[:]).then_inc(sig("idxs_ready"), 1)
                dve.wait_ge(sig("idxs_ready"), i + 2)
                dve.wait_ge(sig("idx_ps"), i + 2)
                dve.wait_ge(sig("gathered"), i * 16 + 16)
                row_numbers(sig("idx_ready"))
                swiglu(0)
                split_low(12, 16)
                dve.wait_ge(sig("at_hi"), i * 2 + 1)
                low(aTs, 0, 6, sig("at_lo"))
                split_low(16, 18)
                swiglu(1)
                split_low(18, 21)
                dve.wait_ge(sig("xt_hi"), i * 2 + 3)
                low(xTs, 0, 7, sig("xt_lo"))
                dve.wait_ge(sig("at_hi"), i * 2 + 2)
                low(aTs, 1, 6, sig("at_lo"))
                split_low(21, 24)
                dve.wait_ge(sig("xt_hi"), i * 2 + 4)
                low(xTs, 1, 6, sig("xt_lo"))
                dve.wait_ge(sig("cur_ready"), i + 1)
                one_hot()
                assert s.n == PER, s.n
            dve.wait_ge(sig("acc"), 2 * TC)
            dve.wait_ge(sig("rows3_in"), 32)
            fin = Steps(dve, sig("fin_step"))
            for t in range(TC):
                dve.wait_ge(sig(f"y{t}_in"), 16 * TOPK)
                for k in range(TOPK):
                    fin.link(V.scalar_tensor_tensor(h1[:, t, :], ybuf[t * TOPK + k], gates[:, t, k:k + 1], h1[:, t, :], ALU.mult, ALU.add))
                for q in range(2):
                    fin.go(V.bn_stats(bn_part[:, t, 6 * q:6 * q + 6], h1[:, t, q * 512:(q + 1) * 512]))
                fin.wait()
                fin.link(V.bn_aggr(bn_mv[:, t, :], bn_part[:, t, :]))
                V.tensor_copy(ln_var[:, t:t + 1], bn_mv[:, t, 1:2]).then_inc(sig("ln2_var"), 1)
            for t in range(TC):
                dve.wait_ge(sig("ln2_rstd"), t + 1)
                fin.link(V.tensor_scalar(h1[:, t, :], h1[:, t, :], bn_mv[:, t, 0:1], ln_rstd[:, t:t + 1], ALU.subtract, ALU.mult))
                fin.link(V.tensor_tensor(h1[:, t, :], h1[:, t, :], ln_rows[:, 0, :], ALU.mult))
                V.tensor_tensor(h1[:, t, :], h1[:, t, :], ln_rows[:, 1, :], ALU.add).then_inc(sig("out_ready"), 1)



def _chunks(v):
    return v.reshape(-1, P).T


def _tables():
    import numpy as np

    f = np.float32
    inv = (f(10000.0) ** (-np.arange(0, 64, 2, dtype=f) / f(64))).astype(f)
    pos = np.concatenate([np.arange(META, L), np.arange(META)])
    row = np.concatenate([np.repeat(np.arange(T // 64), 64), np.full(META, -1)])
    colm = np.concatenate([np.tile(np.arange(64), T // 64), np.arange(META)])
    ang = [(p.astype(f)[:, None] * inv[None, :]).astype(f) for p in (pos, row, colm)]
    cos, sin = [np.cos(x).astype(f) for x in ang], [np.sin(x).astype(f) for x in ang]
    return np.ascontiguousarray(np.concatenate([cos[0], sin[0], cos[1], cos[2], sin[1], sin[2]], axis=1), dtype=f)


def _constants():
    import numpy as np

    c = np.zeros((P, NCONST), np.float32)

    def put(name, value):
        o, n = CONST[name]
        c[:, o:o + n] = value

    p = np.arange(P)
    put("ident", np.eye(P))
    put("ones", 1.0)
    put("mean", 1.0 / D)
    put("before", (p[:, None] < p[None, :]))
    put("iota", p[None, :])
    put("over_e", np.repeat(np.arange(E), 3)[None, :])
    put("over_t", (np.tile([1, 2, 3], E) * P - NONE)[None, :])
    t, k = np.divmod(np.arange(16), TOPK)
    put("dst", k[None, :] * T + t[None, :] * P + p[:, None] - NONE)
    put("part1", p[:, None] + 1)
    put("tok", np.arange(TC)[None, :] * P + p[:, None])
    put("eps6", EPS_RMS)
    put("eps5", EPS_LN2)
    put("hln2", 0.5 * math.log(2.0))
    put("tiny", 1e-37)
    put("one", 1.0)
    return c


def kernel(**inputs):
    import numpy as np
    import concourse.bacc as bacc
    from concourse.bass_utils import run_bass_kernel_spmd

    x = {k: np.asarray(v) for k, v in inputs.items()}
    arrays = {"x": x["x"][0], "xT": x["x"][0].T, "meta_tokens_2": x["meta_tokens_2"], "tab": _tables(), "const": _constants()}
    per_channel = {"c": x["c"][0], "norm_g": x["norm_g"][0], "mod_b": x["mod_b"][0][:2 * D], "lam": x["lam"][0]}
    for k in ("cln_g", "cln_b", "pw2_b", "sc_b", "br", "bi", "dw_b"):
        per_channel[k] = x[k][0]
    per_channel["g_q_a"], per_channel["g_kv_a"] = x["g_q_a_2"][0], x["g_kv_a_2"][0]
    per_channel["g_o"] = np.concatenate([x["g_o_mla_2"][0], x["g_o_gqa_2"][0]])
    chan = np.zeros((P, NCHAN), np.float32)
    for k, (o, n) in CHAN.items():
        if k in ("sc_w", "dw_w"):
            chan[:, o:o + n] = x[k][0].T.reshape(KD, P, -1).transpose(1, 0, 2).reshape(P, n)
        else:
            chan[:, o:o + n] = _chunks(per_channel[k])
    arrays["chan"] = chan
    arrays["rows"] = np.concatenate([x["mod_b"][0][2 * D:], x["final_g"], x["ln_emb_g_2"], x["ln_emb_b_2"], x["ln1_g_2"][0], x["ln1_b_2"][0],
                                     x["g_q_gqa_2"][0], x["g_k_gqa_2"][0], x["b_router_2"][0], x["ln2_g_2"][0], x["ln2_b_2"][0]])[None, :]
    w = x["w_in"][0].reshape(KD, P, 5 * KD, P)
    cv, cg, cs, lx, ls = (np.arange(KD) + KD * i for i in range(5))
    pairs = np.stack([np.concatenate([cv, lx, cs[0::2]]), np.concatenate([cg, ls, cs[1::2]])], 1)
    arrays["w_in"] = w[:, :, pairs, :].transpose(2, 1, 0, 3, 4).reshape(N_IN, P, TILE)
    for k in ("mod_w", "pw2_w", "w_out", "wr", "wi", "w_in_2", "w_q_b_2", "w_kv_b_2", "w_o_2", "w_router_2", "w_gate_up_2", "b_gate_up_2",
              "w_down_2", "b_down_2"):
        arrays[k] = x[k][0]
    nc = bacc.Bacc("TRN2", target_bir_lowering=False, num_devices=1)
    feeds, a = {}, {}
    for k, v in arrays.items():
        feeds[f"in_{k}"] = np.ascontiguousarray(v)
        a[k] = nc.dram_tensor(f"in_{k}", feeds[f"in_{k}"].shape, F32, kind="ExternalInput").ap()
    h1_dram = nc.dram_tensor("h1_rows", (T, D), F32, kind="Internal").ap()
    y_dram = nc.dram_tensor("y_rows", (TOPK * T, D), F32, kind="Internal").ap()
    out = nc.dram_tensor("out_0", (T, D), F32, kind="ExternalOutput").ap()
    program(nc, a, out, h1_dram, y_dram)
    r = run_bass_kernel_spmd(nc, [feeds], core_ids=[0])
    return r.results[0]["out_0"].reshape(1, T, D)
```

```python
from contextlib import ExitStack
import math

import concourse.bass as bass
from concourse import mybir

F32 = mybir.dt.float32
F32R = mybir.dt.float32r
I32 = mybir.dt.int32
U32 = mybir.dt.uint32
ALU = mybir.AluOpType
ACT = mybir.ActivationFunctionType
AX = mybir.AxisListType

P = 128
D = 1024
KD = D // P
T = 512
TC = T // P
META = 16
L = T + META
LC = TC + 1
TAPS = 31
STAPS = 4
EPS_RMS = 1e-6
EPS_LN2 = 1e-5
ALPHA = 2.0 ** 0.25
E = 32
TOPK = 4
HM = 4
NOPE, ROPE = 128, 64
LIMIT = 7.0
SWALPHA = 1.702
NONE = 4096.0
ITEMS = 64

CHAN = {}
_at = 0
for _name, _n in (("c", 8), ("norm_g", 8), ("mod_b", 16), ("cln_g", 8), ("cln_b", 8), ("pw2_b", 8), ("sc_b", 8),
                  ("br", 8), ("bi", 8), ("lam", 8), ("dw_b", 8), ("sc_w", 8 * STAPS), ("dw_w", 8 * TAPS),
                  ("g_q_a", 2), ("g_kv_a", 1), ("g_o", 8)):
    CHAN[_name] = (_at, _n)
    _at += _n
NCHAN = _at

CONST = {}
_at = 0
for _name, _n in (("ident", P), ("ones", P), ("mean", P), ("before", P), ("iota", P), ("over_e", 96), ("over_t", 96),
                  ("dst", 16), ("part1", 1), ("tok", TC), ("eps6", 1), ("eps5", 1), ("hln2", 1), ("tiny", 1), ("one", 1)):
    CONST[_name] = (_at, _n)
    _at += _n
NCONST = _at

ROWS = {"gate_b": 0, "final_g": 1024, "ln_emb_g": 2048, "ln_emb_b": 3072, "ln1_g": 4096, "ln1_b": 5120, "g_qk": 6144,
        "b_router": 6400, "ln2_g": 6432, "ln2_b": 7456}
NROWS = 8480

RING1 = 3
TILE = 2048
N_MOD, N_IN, N_GATE, N_PW2, N_OUT, N_IN2, N_Q, N_KV, N_O = 8, 20, 4, 4, 8, 6, 1, 1, 4
T_IN = N_MOD
T_GATE = T_IN + N_IN
T_PW2 = T_GATE + N_GATE
T_OUT = T_PW2 + N_PW2
T_IN2 = T_OUT + N_OUT
T_Q = T_IN2 + N_IN2
T_KV = T_Q + N_Q
T_O = T_KV + N_KV
N_PHASE1 = T_O + N_O
EXPERT_TILES = 12
SLOTS = 6
CHUNKS = 2 * EXPERT_TILES
SPLITS = 4
BY_POOL = (6, 13, 18)


class Steps:

    def __init__(self, eng, sem):
        self.eng, self.sem, self.n = eng, sem, 0

    def go(self, ins):
        self.n += 1
        ins.then_inc(self.sem, 1)

    def wait(self):
        self.eng.wait_ge(self.sem, self.n)

    def link(self, ins):
        self.go(ins)
        self.wait()


def program(nc, a, out, h1_dram, y_dram):
    with ExitStack() as ctx:
        sems = {}

        def sig(name):
            if name not in sems:
                sems[name] = ctx.enter_context(nc.semaphore(name))
            return sems[name]

        def sb(name, shape, dt=F32):
            return ctx.enter_context(nc.sbuf_tensor(name, shape, dt))

        ps = ctx.enter_context(nc.psum_tensor("ps", [P, 8, 512], F32))
        ring = sb("ring", [P, RING1, TILE])
        chan = sb("chan", [P, NCHAN])
        const = sb("const", [P, NCONST])
        qk_rows = sb("qk_rows", [P, 2 * P + E])
        small = sb("small", [P, 512])
        ARENA = 29760
        arena = sb("arena", [P, ARENA])
        split = sb("split", [P, SPLITS, 2, D], F32R)
        xTs = sb("xTs", [P, 2, KD, P], F32R)
        aTs = sb("aTs", [P, 2, KD, P], F32R)
        bgu = sb("bgu", [2 * E, 2 * D], F32R)
        eo = sb("eo", [2 * E, P], F32R)

        def ch(name, k=0, n=1):
            o = CHAN[name][0] + k
            return chan[:, o:o + n]

        def cst(name, lo=0, hi=None, p=P):
            o, n = CONST[name]
            return const[0:p, o + lo:o + (n if hi is None else hi)]

        class Area:
            def __init__(self, at=0):
                self.at = at

            def take(self, *shape):
                n = math.prod(shape)
                assert self.at + n <= ARENA, (self.at, n)
                v = arena[:, self.at:self.at + n]
                self.at += n
                if len(shape) == 2:
                    v = v.rearrange("p (a b) -> p a b", b=shape[1])
                if len(shape) == 3:
                    v = v.rearrange("p (a b c) -> p a b c", b=shape[1], c=shape[2])
                return v

        m1 = Area()
        hT = m1.take(KD, T)
        v = m1.take(KD, T + TAPS - 1)
        vc = m1.take(KD, T)
        ylru = m1.take(KD, T)
        sgt = m1.take(2, T)
        lxb = m1.take(2, T + STAPS - 1)
        xs = m1.take(2, T)
        lsil = m1.take(2, T)
        lru = m1.take(4, T)
        gates_w = m1.take(2 * KD, P)
        crep = m1.take(KD, P)
        gate1 = m1.take(D)
        mod_row = lru.rearrange("p a b -> p (a b)")
        rep = m1.take(2, T)
        rows1 = Area(m1.at - 2 * T - D - 3 * D).take(3, D)
        scs = Area(KD * T).take(KD, T)
        x2 = Area(0).take(TC, D)
        m2 = Area(0)
        qnT = m2.take(HM, T)
        rtmp = m2.take(2, 384)
        tab = m2.take(LC, 192)
        assert m2.at <= KD * T
        m2 = Area(KD * T)
        qanT = m2.take(2, T)
        kvanT = m2.take(L)
        krT = m2.take(L)
        qpT = m2.take(2, T)
        AT_H = m2.at
        pr = Area(KD * T).take(2, L)
        wrouter = Area(AT_H - KD * E).take(KD, E)
        h = m2.take(LC, D)
        after_h = m2.at
        hT2 = m2.take(KD, L)
        at_z = m2.at
        zA = m2.take(LC, 448)
        zB = m2.take(TC, 512)
        zC = m2.take(LC, 512)
        knT = m2.take(HM, L)
        qgT = m2.take(4, T)
        kgT = m2.take(2, L)
        rot = m2.take(6 * P)
        pe_rot = m2.take(4 * ROPE + P)
        m2 = Area(at_z)
        vm = m2.take(LC, 512)
        pT = m2.take(2, LC * P)
        junk = Area(m1.at).take(D)
        qrot = Area(at_z + 5 * 512).take(TC, 256)
        o_tok = Area(after_h).take(TC, D)
        oT = Area(0).take(KD, T)
        h1 = h
        h1T = hT2
        m3 = Area(0)
        xe = m3.take(D)
        ysb = m3.take(D)
        actv = m3.take(D)
        glu = m3.take(2, T)
        gsig = m3.take(2, T)
        oh = m3.take(TC, P)
        posm = m3.take(TC, E)
        dst = m3.take(TC, E)
        assert m3.at <= AT_H - KD * E
        ext = Area(after_h).take(SLOTS - RING1, TILE)
        m3 = Area(after_h + (SLOTS - RING1) * TILE)
        ln_rows = m3.take(2, D)
        bdown = m3.take(D)
        mk = m3.take(TC * TOPK, E)
        mkt = m3.take(TC * TOPK, E)
        routed = m3.take(TC, E)
        gmat = m3.take(TC, E)
        logit = m3.take(TC, E)
        gT = m3.take(T)
        flags = m3.take(E, 3)
        fsum = m3.take(96)
        feq = m3.take(96)
        ftmp = m3.take(96)
        evb = m3.take(2, P)
        elist = m3.take(ITEMS)
        tlist = m3.take(ITEMS)
        v8 = m3.take(TC, 8)
        if4 = m3.take(TC * TOPK)
        gates = m3.take(TC, TOPK)
        cur = m3.take(TC)
        dcur = m3.take(TC, 2)
        ybuf = [x[:, q // 2, (q % 2) * D:(q % 2 + 1) * D] for x in (ext, ring) for q in range(6)]
        back = m3.take(4, D)
        ybuf += [back[:, q, :] for q in range(4)]
        bgu_raw = Area(m3.at - 4 * D).take(2 * D)

        cols = {}
        used = [0]

        def col(name, n=None):
            if name not in cols:
                cols[name] = (used[0], n)
                used[0] += n
                assert used[0] <= 512
            o, n = cols[name]
            return small[:, o:o + n]

        c_act, c_sig, lam_abs, lam_e, lam_neg = (col(n, 8) for n in ("c_act", "c_sig", "lam_abs", "lam_e", "lam_neg"))
        rate, nrate, lam_z, shift, gain = (col(n, 8) for n in ("rate", "nrate", "lam_z", "shift", "gain"))
        x2_ss, unused = col("x2_ss", TC), col("unused", 1)
        emb_var, emb_ln, emb_rstd = (col(n, LC) for n in ("emb_var", "emb_ln", "emb_rstd"))
        bn_part = col("bn_part", 12 * LC).rearrange("p (t s) -> p t s", t=LC)
        bn_mv = col("bn_mv", 2 * LC).rearrange("p (t s) -> p t s", t=LC)
        z_ss, z_ln = col("z_ss", 9 * LC), col("z_ln", 9 * LC)
        nmaxs, psums = col("nmax", 32), col("psum", 32)
        o_ss, o_ln, o_rstd = (col(n, 2 * TC) for n in ("o_ss", "o_ln", "o_rstd"))
        ln_var, ln_ln, ln_rstd = (col(n, TC) for n in ("ln_var", "ln_ln", "ln_rstd"))
        nv0, gsum = col("nv0", TC), col("gsum", TC)
        ev, tv = col("ev", 1), col("tv", 1)
        i8 = sb("i8", [P, TC, 8], U32)
        idx_g = sb("idx_g", [P, 1], I32)
        idx_2 = sb("idx_2", [P, 1], I32)
        idx_s = sb("idx_s", [P, 1], I32)
        eint = sb("eint", [1, ITEMS], I32)
        nint = sb("nint", [1, 1], I32)

        def rows_of(t):
            return P if t < TC else META

        BANK_QN = [4 + (2 * LC + TC - 4 + j) % 4 for j in range(HM)]
        ONE = cst("one")
        IDENT = cst("ident")

        tile_ready = [sig(f"tile{s}_ready") for s in range(SLOTS)]

        def wait_tile(eng, n):
            eng.wait_ge(tile_ready[n % RING1], 16 * (n // RING1 + 1))

        def tile(n):
            return ring[:, n % RING1, :]

        def last_use(n):
            if n < T_IN:
                return sig("mod_used"), n + 1
            if n < T_GATE:
                return sig("u_ready"), 2 * (n - T_IN) + 2
            if n < T_PW2:
                return sig("gate_used"), n - T_GATE + 1
            if n < T_OUT:
                return sig("pw2_ready"), 2 * (n - T_PW2) + 2
            if n < T_IN2:
                return sig("out_used"), n - T_OUT + 1
            if n < T_Q:
                return sig("z_ready"), (LC, LC + TC, 2 * LC + TC)[(n - T_IN2) // 2]
            if n == T_Q:
                return sig("qp_ps"), TC
            if n == T_KV:
                return sig("vm_ps"), LC
            return sig("o_used"), n - T_O + 1

        Z_UNITS = [(g, t) for g in range(3) for t in range(LC) if (g, t) != (1, TC)]
        AT_A, AT_B, AT_C, AT_QP = 0, LC, LC + TC, 2 * LC + TC
        UNITS = [(hh, qt) for hh in range(8) for qt in range(TC)]

        loads_before = [len([n for n in range(N_PHASE1) if n % RING1 == s_]) if s_ < RING1 else 0 for s_ in range(SLOTS)]

        def low_ready(i, c):
            if c in BY_POOL:
                return sig("lo_pool"), i * len(BY_POOL) + (BY_POOL.index(c) + 1)
            return sig("lo_ready"), i * (CHUNKS - len(BY_POOL)) + len([x for x in range(c + 1) if x not in BY_POOL])

        def low_chunk(tt, i, c):
            return tt(split[:, c % SPLITS, 1, :], chunk(c), split[:, c % SPLITS, 0, :], ALU.subtract).then_inc(low_ready(0, c)[0], 1)

        def both_rows(tt, e):
            ident = cst("ident", 0, 2 * E, 2 * E)
            return tt(eo[:], ident[:, bass.ds(e, 1)].to_broadcast([2 * E, P]), ident[:, bass.ds(e + E, 1)].to_broadcast([2 * E, P]),
                      ALU.add).then_inc(sig("eo_ready"), 1)

        def chunk(c):
            j = c // 2 % SLOTS
            x = ring[:, j, :] if j < RING1 else ext[:, j - RING1, :]
            return x[:, (c % 2) * D:(c % 2 + 1) * D]

        def wait_alone(eng, sem, value):
            eng.wait_ge(sig("list_ready"), 1)
            eng.wait_ge(sem, value)
            eng.wait_ge(sig("list_ready"), 2)

        block = ctx.enter_context(nc.Block())

        @block.sync
        def _(sp):
            sp.dma_start(chan[:], a["chan"]).then_inc(sig("chan_in"), 16)
            sp.dma_start(const[:], a["const"]).then_inc(sig("const_in"), 16)

            def load(n, dst, src):
                if n >= RING1:
                    sp.wait_ge(*last_use(n - RING1))
                sp.dma_start(dst, src).then_inc(tile_ready[n % RING1], 16)

            for k in range(N_MOD):
                load(k, tile(k), a["mod_w"][k * P:(k + 1) * P, 0:2 * D])
            for n in range(N_IN):
                load(T_IN + n, tile(T_IN + n), a["w_in"][n])
            for n in range(N_GATE):
                load(T_GATE + n, tile(T_GATE + n).rearrange("p (k n) -> p k n", k=2),
                     a["mod_w"][n * 2 * P:(n + 1) * 2 * P, 2 * D:].rearrange("(k p) n -> p k n", p=P))
            for n in range(N_PW2):
                load(T_PW2 + n, tile(T_PW2 + n).rearrange("p (k n) -> p k n", k=KD),
                     a["pw2_w"][:, n * 256:(n + 1) * 256].rearrange("(k p) n -> p k n", p=P))
            for n in range(N_OUT):
                half, g = n // 4, n % 4
                load(T_OUT + n, tile(T_OUT + n).rearrange("p (k n) -> p k n", k=4),
                     a["w_out"][g * 512:(g + 1) * 512, half * 512:(half + 1) * 512].rearrange("(k p) n -> p k n", p=P))
            for n in range(N_IN2):
                g, kk = n // 2, n % 2
                lo, w = ((0, 448), (448, 512), (960, 512))[g]
                load(T_IN2 + n, tile(T_IN2 + n)[:, 0:4 * w].rearrange("p (k n) -> p k n", k=4),
                     a["w_in_2"][kk * 512:(kk + 1) * 512, lo:lo + w].rearrange("(k p) n -> p k n", p=P))
            load(T_Q, tile(T_Q)[:, 0:1536].rearrange("p (k n) -> p k n", k=2), a["w_q_b_2"].rearrange("(k p) n -> p k n", p=P))
            load(T_KV, tile(T_KV)[:, 0:D], a["w_kv_b_2"][:, :])
            for n in range(N_O):
                half, g = n // 2, n % 2
                load(T_O + n, tile(T_O + n).rearrange("p (k n) -> p k n", k=4),
                     a["w_o_2"][g * 512:(g + 1) * 512, half * 512:(half + 1) * 512].rearrange("(k p) n -> p k n", p=P))
            def expert_tile(j, e):
                x = ring[:, j % SLOTS, :] if j % SLOTS < RING1 else ext[:, j % SLOTS - RING1, :]
                if j < 8:
                    half, g = j // 4, j % 4
                    src = a["w_gate_up_2"][bass.ds(e, 1), g * 256:(g + 1) * 256, half * D:(half + 1) * D]
                else:
                    src = a["w_down_2"][bass.ds(e, 1), (j - 8) * 256:(j - 7) * 256, :]
                sp.dma_start(x.rearrange("p (k n) -> p k n", k=2), src.rearrange("o (k p) n -> p (o k) n", p=P)).then_inc(tile_ready[j % SLOTS], 16)

            for j in range(EXPERT_TILES):
                if j < RING1:
                    sp.wait_ge(*last_use(max(n for n in range(N_PHASE1) if n % RING1 == j)))
                elif j == RING1:
                    sp.wait_ge(sig("logits_ps"), 1)
                elif j >= SLOTS:
                    for c in (2 * (j - SLOTS), 2 * (j - SLOTS) + 1):
                        sp.wait_ge(*low_ready(0, c))
                expert_tile(j, 0)
            sp.wait_ge(sig("list_ready"), 3)
            n_items = sp.value_load(nint[0:1, 0:1], min_val=E, max_val=E + 16)
            with sp.Fori(1, n_items) as i:
                e = sp.value_load(eint[0:1, bass.ds(i, 1)], min_val=0, max_val=E - 1)
                for j in range(EXPERT_TILES):
                    before = (i - 1) if j < SLOTS else i
                    c = 2 * ((j - SLOTS) % EXPERT_TILES)
                    for by_pool in sorted({c in BY_POOL, c + 1 in BY_POOL}):
                        signal, count = low_ready(before, c + 1 if (c + 1 in BY_POOL) == by_pool else c)
                        wait_alone(sp, signal, sp.to_reg(count))
                    expert_tile(j, e)
            wait_alone(sp, sig("scattered"), n_items * 16 + 16)
            for t in range(TC):
                for k in range(TOPK):
                    sp.dma_start(ybuf[t * TOPK + k], y_dram[k * T + t * P:k * T + (t + 1) * P, :]).then_inc(sig(f"y{t}_in"), 16)
            for t in range(TC):
                sp.wait_ge(sig("out_ready"), t + 1)
                sp.dma_start(out[t * P:(t + 1) * P, :], h1[:, t, :]).then_inc(sig("out_written"), 16)
            sp.wait_ge(sig("out_written"), 16 * TC)

        @block.gpsimd
        def _(pool):
            nc.gpsimd.memset(v[:, :, 0:TAPS - 1], 0.0).then_inc(sig("pads_zero"), 1)
            nc.gpsimd.memset(lxb[:, :, 0:STAPS - 1], 0.0).then_inc(sig("pads_zero"), 1)
            pool.wait_ge(sig("gate_used"), N_GATE)
            pool.dma_start(rows1.rearrange("p a b -> p (a b)"),
                           a["rows"][:, ROWS["final_g"]:ROWS["final_g"] + 3 * D].partition_broadcast(P)).then_inc(sig("rows1_in"), 16)
            pool.wait_ge(sig("u_ready"), 2 * N_IN)
            pool.dma_start(x2[:], a["x"].rearrange("(t p) d -> p t d", p=P)).then_inc(sig("xtok_in"), 16)
            pool.wait_ge(sig("out_used"), N_OUT)
            pool.dma_start(h[0:META, TC, :], a["meta_tokens_2"][:, :]).then_inc(sig("meta_in"), 16)

            for t in range(LC):
                r = rows_of(t)
                pool.wait_ge(sig("h_scaled"), t + 1)
                if t == 0:
                    pool.wait_ge(sig("rows1_in"), 16)
                nc.gpsimd.tensor_tensor(h[0:r, t, :], h[0:r, t, :], rows1[0:r, 2, :], ALU.add).then_inc(sig("h_ready"), 1)

            def load_rows(dst, name, n, signal):
                pool.dma_start(dst, a["rows"][:, ROWS[name]:ROWS[name] + n].partition_broadcast(P)).then_inc(signal, 16)

            pool.wait_ge(sig("h_ready"), LC)
            pool.dma_start(tab[:, 0:TC, :], a["tab"][0:T, :].rearrange("(t p) n -> p t n", p=P)).then_inc(sig("tab_in"), 16)
            pool.dma_start(tab[0:META, TC, :], a["tab"][T:L, :]).then_inc(sig("tab_in"), 16)
            load_rows(qk_rows[:], "g_qk", 2 * P + E, sig("rows2_in"))
            pool.wait_ge(sig("o_taken"), 8 * TC)
            pool.dma_start(wrouter, a["w_router_2"].rearrange("(k p) e -> p k e", p=P)).then_inc(sig("router_in"), 16)
            load_rows(ln_rows[:, 0, :], "ln1_g", D, sig("ln1_rows_in"))
            load_rows(ln_rows[:, 1, :], "ln1_b", D, sig("ln1_rows_in"))
            for q in range(2):
                pool.dma_start(bgu_raw[q * E:(q + 1) * E, :], a["b_gate_up_2"][:, :]).then_inc(sig("bgu_in"), 16)
            pool.dma_start(bdown[0:E, :], a["b_down_2"][:, :]).then_inc(sig("bias_in"), 16)
            for t in range(TC):
                pool.wait_ge(sig("h_scaled"), LC + t + 1)
                if t == 0:
                    pool.wait_ge(sig("ln1_rows_in"), 32)
                nc.gpsimd.tensor_tensor(h1[:, t, :], h1[:, t, :], ln_rows[:, 1, :], ALU.add).then_inc(sig("h1_ready"), 1)
                pool.wait_ge(sig("h1_ready"), t + 1)
                pool.dma_start(h1_dram[t * P:(t + 1) * P, :], h1[:, t, :]).then_inc(sig("h1_stored"), 16)
            load_rows(ln_rows[:, 0, :], "ln2_g", D, sig("rows3_in"))
            load_rows(ln_rows[:, 1, :], "ln2_b", D, sig("rows3_in"))
            pool.wait_ge(sig("h1T_ps"), TC)
            pool.wait_ge(sig("o_used"), N_O)
            nc.gpsimd.memset(xe, 0.0).then_inc(sig("xe_zero"), 1)
            pool.wait_ge(sig("xe_zero"), 1)
            pool.wait_ge(sig("h1_stored"), 16 * TC)
            last_token = pool.to_reg(T - 1)
            last_row = pool.to_reg(TOPK * T - 1)

            def gather():
                nc.gpsimd.indirect_dma_start(out=xe, out_offset=None, in_=h1_dram, in_offset=bass.IndirectOffsetOnAxis(idx_g[:, 0:1], 0),
                                             bounds_check=last_token, oob_is_err=False).then_inc(sig("gathered"), 16)

            pool.wait_ge(sig("idx0_ready"), 1)
            gather()
            pool.wait_ge(sig("list_ready"), 3)
            n_items = pool.value_load(nint[0:1, 0:1], min_val=E, max_val=E + 16)

            def scatter():
                nc.gpsimd.indirect_dma_start(out=y_dram, out_offset=bass.IndirectOffsetOnAxis(idx_s[:, 0:1], 0), in_=ysb, in_offset=None,
                                             bounds_check=last_row, oob_is_err=False).then_inc(sig("scattered"), 16)

            def low_part(i, c):
                pool.wait_ge(sig("hi_ready"), i * CHUNKS + (c + 1))
                low_chunk(nc.gpsimd.tensor_tensor, i, c)

            outputs = pool.to_reg(n_items + 1)
            with pool.Fori(1, n_items + 1) as m:
                i = m - 1
                wait_alone(pool, sig("y_ready"), m)
                scatter()
                low_part(i, BY_POOL[0])
                wait_alone(pool, sig("idx_ready"), m)
                gather()
                for c in BY_POOL[1:]:
                    low_part(i, c)
                e = pool.value_load(eint[0:1, bass.ds(m, 1)], min_val=0, max_val=E - 1)
                both_rows(nc.gpsimd.tensor_tensor, e)
                e = pool.value_load(eint[0:1, bass.ds(m + 1, 1)], min_val=0, max_val=E - 1)
                nc.gpsimd.tensor_copy(dcur[:, :, 1:2], dst[:, :, bass.ds(e, 1)])
                nc.gpsimd.tensor_tensor(cur.rearrange("p (t o) -> p t o", o=1), posm[:, :, bass.ds(e, 1)],
                                        tlist[:, bass.ds(m + 1, 1)].rearrange("p (t o) -> p t o", o=1).to_broadcast([P, TC, 1]),
                                        ALU.subtract).then_inc(sig("cur_ready"), 1)
            wait_alone(pool, sig("y_ready"), outputs)
            scatter()
            wait_alone(pool, sig("gathered"), n_items * 16 + 16)
            for t in range(TC - 1):
                pool.wait_ge(sig("h_scaled"), LC + TC + t + 1)
                if t == 0:
                    pool.wait_ge(sig("rows3_in"), 32)
                nc.gpsimd.tensor_tensor(h1[:, t, :], h1[:, t, :], ln_rows[:, 1, :], ALU.add).then_inc(sig("out_ready"), 1)

        @block.tensor
        def _(pe):
            mm = nc.tensor.matmul

            def lru_gates(pe, j):
                b = 4 + 2 * (j % 2)
                pe.wait_ge(sig("xs"), j + 1)
                if j >= 2:
                    pe.wait_ge(sig("gates_taken"), 2 * (j - 1))
                if j == 0:
                    pe.wait_ge(sig("gates_in"), 32)
                nc.tensor.matmul(ps[:, b, :], gates_w[:, j, :], xs[:, j % 2, :], start=True, stop=True)
                nc.tensor.matmul(ps[:, b + 1, :], gates_w[:, KD + j, :], xs[:, j % 2, :], start=True, stop=True).then_inc(sig("gates_ps"), 1)

            def channel_mean(pe):
                pe.wait_ge(sig("gates_taken"), 16)
                for k in range(KD):
                    pe.wait_ge(sig("conv"), k + 1)
                    i = nc.tensor.matmul(ps[:, 4, :], cst("mean"), vc[:, k, :], start=(k == 0), stop=(k == KD - 1))
                i.then_inc(sig("mean_ps"), 1)

            def channel_var(pe):
                for k in range(KD):
                    pe.wait_ge(sig("vsq"), k + 1)
                    nc.tensor.matmul(ps[:, 5, :], cst("mean"), rep[:, k % 2, :], start=(k == 0), stop=(k == KD - 1)).then_inc(sig("vsq_summed"), 1)

            def attention(pe):
                mm = nc.tensor.matmul

                def scores(u):
                    hh, qt = UNITS[u]
                    b = 2 * (u % 2)
                    q = slice(qt * P, (qt + 1) * P)
                    if u >= 2:
                        pe.wait_ge(sig("prob"), u - 1)
                    for lo, hi, bb in ((0, T, b), (T, L, b + 1)):
                        dst = ps[:, bb, 0:hi - lo]
                        if hh < HM:
                            pb = ROPE * (hh % 2)
                            mm(dst, qnT[:, hh, q], knT[:, hh, lo:hi], start=True, stop=False)
                            i = mm(dst, qpT[pb:pb + ROPE, hh // 2, q], krT[pb:pb + ROPE, lo:hi], start=False, stop=True)
                        else:
                            i = mm(dst, qgT[:, hh - HM, q], kgT[:, (hh - HM) // 2, lo:hi], start=True, stop=True)
                    i.then_inc(sig("scores_ps"), 1)

                def turn(u):
                    if u >= 1:
                        pe.wait_ge(sig("probT"), 2 * u)
                    pe.wait_ge(sig("prob"), u + 1)
                    for c in range(TC):
                        i = nc.tensor.transpose(ps[:, 4, c * P:(c + 1) * P], pr[:, u % 2, c * P:(c + 1) * P], IDENT)
                    i = nc.tensor.transpose(ps[0:META, 5, 0:P], pr[:, u % 2, T:L], IDENT)
                    i.then_inc(sig("probT_ps"), 1)

                def weigh(u):
                    hh, qt = UNITS[u]
                    pe.wait_ge(sig("probT"), 2 * (u + 1))
                    if u >= 2:
                        pe.wait_ge(sig("o_taken"), u - 1)
                    for c in range(LC):
                        r = rows_of(c)
                        if hh < HM:
                            val = vm[0:r, c, hh * P:(hh + 1) * P]
                        else:
                            val = zC[0:r, c, 256 + (hh - HM) // 2 * P:256 + ((hh - HM) // 2 + 1) * P]
                        i = mm(ps[:, 6 + u % 2, 0:P], pT[0:r, u % 2, c * P:(c + 1) * P], val, start=(c == 0), stop=(c == LC - 1))
                    i.then_inc(sig("o_ps"), 1)

                pe.wait_ge(sig("qkn"), 2 * HM + 1)
                pe.wait_ge(sig("qpT"), TC)
                scores(0)
                scores(1)
                for u in range(len(UNITS)):
                    turn(u)
                    if u + 2 < len(UNITS):
                        scores(u + 2)
                    weigh(u)

            def item_index():
                for c in range(TC):
                    i = mm(ps[:, 4, 0:2], oh[:, c, :], dcur[:, c, :], start=(c == 0), stop=(c == TC - 1))
                i.then_inc(sig("idx_ps"), 1)

            def turn(x, bank):
                for k in range(4):
                    i = nc.tensor.transpose(ps[:, bank, k * P:(k + 1) * P], x[:, k * P:(k + 1) * P], IDENT)
                return i

            def experts(pe):
                pe.wait_ge(sig("masks"), 1)
                for c in range(TC):
                    for cc in range(c + 1):
                        mm(ps[:, 3, c * E:(c + 1) * E], cst("before") if cc == c else cst("ones"), routed[:, cc, :],
                           start=(cc == 0), stop=(cc == c))
                for c in range(TC):
                    i = mm(ps[:, 3, TC * E:(TC + 1) * E], cst("ones"), routed[:, c, :], start=(c == 0), stop=(c == TC - 1))
                i.then_inc(sig("lists_ps"), 1)
                pe.wait_ge(sig("oh_ready"), 1)
                item_index()
                pe.wait_ge(sig("over_ready"), 2)
                for q in range(2):
                    i = mm(ps[:, 3, q * E:(q + 1) * E], evb[0:E, q, :], cst("ident", 0, E, E), start=True, stop=True)
                i.then_inc(sig("lists_ps"), 1)
                pe.wait_ge(sig("masks"), 2)
                for c in range(TC):
                    i = nc.tensor.transpose(ps[0:E, 5, c * P:(c + 1) * P], gmat[:, c, :], IDENT)
                i.then_inc(sig("lists_ps"), 1)
                pe.wait_ge(sig("gT"), 1)
                pe.wait_ge(sig("bias_in"), 16)
                pe.wait_ge(sig("idx0_ready"), 1)
                for c in range(TC):
                    if c >= 2:
                        pe.wait_ge(sig("acc"), 2 * (c - 1))
                    for q in range(2):
                        mm(ps[:, 4 + 2 * (c % 2) + q, :], gT[0:E, c * P:(c + 1) * P], bdown[0:E, q * 512:(q + 1) * 512],
                           start=True, stop=True).then_inc(sig("bdown_ps"), 1)
                pe.wait_ge(sig("acc"), 2 * TC)
                pe.wait_ge(sig("bgu_lo"), 1)
                pe.wait_ge(sig("gathered"), 16)
                nc.tensor.transpose(ps[:, 7, 0:P], xe[:, 0:P], IDENT).then_inc(sig("split_used"), SPLITS)
                turn(xe[:, 0:512], 7).then_inc(sig("xt_ps"), 1)
                turn(xe[:, 512:1024], 6).then_inc(sig("xt_ps"), 1)
                pe.wait_ge(sig("list_ready"), 3)
                n_items = pe.value_load(nint[0:1, 0:1], min_val=E, max_val=E + 16)
                with pe.Fori(0, n_items) as i:

                    def product(c, banks, lhs, k, start, stop):
                        pe.wait_ge(*low_ready(i, c))
                        w = split[:, c % SPLITS]
                        for n_, (x_, w_) in enumerate(((0, 0), (0, 1), (1, 0))):
                            for q in range(2):
                                m = mm(ps[:, banks + q, :], lhs[:, x_, k, :], w[:, w_, q * 512:(q + 1) * 512],
                                       start=(start and n_ == 0), stop=(stop and n_ == 2))
                        m.then_inc(sig("split_used"), 1)

                    pe.wait_ge(sig("eo_ready"), i + 1)
                    pe.wait_ge(sig("xt_lo"), i * 2 + 2)
                    for half in range(2):
                        pe.wait_ge(sig("lin_ready"), i * 2 + (half + 1))
                        for q in range(2):
                            mm(ps[:, 2 * half + q, :], eo[:], bgu[:, half * D + q * 512:half * D + (q + 1) * 512], start=True, stop=False)
                        for k in range(KD):
                            if half == 1 and k == 5:
                                pe.wait_ge(sig("act_ready"), i * 2 + 1)
                                turn(actv[:, 0:512], 6).then_inc(sig("at_ps"), 1)
                            product(8 * half + k, 2 * half, xTs, k, False, k == KD - 1)
                        if half == 0:
                            pe.wait_ge(sig("oh_ready"), i + 2)
                            pe.wait_ge(sig("y_ready"), i + 1)
                            item_index()
                    pe.wait_ge(sig("gathered"), i * 16 + 32)
                    turn(xe[:, 0:512], 7).then_inc(sig("xt_ps"), 1)
                    pe.wait_ge(sig("idx_ready"), i + 1)
                    for k in range(KD):
                        if k == 3:
                            pe.wait_ge(sig("act_ready"), i * 2 + 2)
                            pe.wait_ge(sig("at_lo"), i * 2 + 3)
                            turn(actv[:, 512:1024], 6).then_inc(sig("at_ps"), 1)
                        if k == 4:
                            pe.wait_ge(sig("at_lo"), i * 2 + 4)
                        if k == 5:
                            turn(xe[:, 512:1024], 6).then_inc(sig("xt_ps"), 1)
                        product(16 + k, 4, aTs, k, k == 0, k == KD - 1)

            pe.wait_ge(sig("c_act"), 1)
            for k in range(KD):
                wait_tile(pe, k)
                for q in range(4):
                    i = mm(ps[0:1, q, :], c_act[:, k:k + 1], tile(k)[:, q * 512:(q + 1) * 512], start=(k == 0), stop=(k == KD - 1))
                i.then_inc(sig("mod_used"), 1)
                if k == 3:
                    pe.wait_ge(sig("const_in"), 16)
                    for kk in range(KD):
                        pe.wait_ge(sig("xsq"), kk + 1)
                        mm(ps[:, 4, :], cst("mean"), rep[:, kk % 2, :], start=(kk == 0), stop=(kk == KD - 1)).then_inc(sig("xsq_summed"), 1)
            pe.wait_ge(sig("mod_row"), 2)
            for m in range(2 * KD):
                i = mm(ps[:, 5, m:m + 1], mod_row[0:1, m * P:(m + 1) * P], cst("one", p=1), start=True, stop=True)
            i.then_inc(sig("mod_cols"), 1)
            for n in range(N_IN):
                wait_tile(pe, T_IN + n)
                if n >= 2:
                    pe.wait_ge(sig("u_taken"), n - 1)
                w = tile(T_IN + n).rearrange("p (k n) -> p k n", k=KD)
                for half in range(2):
                    for k in range(KD):
                        if n == 0 and half == 0:
                            pe.wait_ge(sig("hT"), k + 1)
                        i = mm(ps[:, 2 * (n % 2) + half, :], w[:, k, half * P:(half + 1) * P], hT[:, k, :],
                               start=(k == 0), stop=(k == KD - 1))
                    i.then_inc(sig("u_ready"), 1)
                if 9 <= n <= 16:
                    lru_gates(pe, n - 9)
                if n == 17:
                    channel_mean(pe)
            channel_var(pe)
            pe.wait_ge(sig("crep"), KD)
            for n in range(N_GATE):
                wait_tile(pe, T_GATE + n)
                w = tile(T_GATE + n).rearrange("p (k n) -> p k n", k=2)
                for kk in range(2):
                    k = 2 * n + kk
                    for half in range(2):
                        i = mm(ps[:, 6 + half, :], crep[:, k, :], w[:, kk, half * 512:(half + 1) * 512],
                               start=(k == 0), stop=(k == KD - 1))
                i.then_inc(sig("gate_used"), 1)
            pe.wait_ge(sig("u_taken"), N_IN)
            for n in range(N_PW2):
                wait_tile(pe, T_PW2 + n)
                w = tile(T_PW2 + n).rearrange("p (k n) -> p k n", k=KD)
                for half in range(2):
                    m = 2 * n + half
                    if m >= 4:
                        pe.wait_ge(sig("yconv"), m - 3)
                    for k in range(KD):
                        if m == 0:
                            pe.wait_ge(sig("vln"), k + 1)
                        i = mm(ps[:, m % 4, :], w[:, k, half * P:(half + 1) * P], vc[:, k, :],
                               start=(k == 0), stop=(k == KD - 1))
                    i.then_inc(sig("pw2_ready"), 1)
            pe.wait_ge(sig("yconv"), KD)
            pe.wait_ge(sig("ylru"), KD)
            pe.wait_ge(sig("gate1"), 2)
            for n in range(N_OUT):
                half, g = n // 4, n % 4
                wait_tile(pe, T_OUT + n)
                w = tile(T_OUT + n).rearrange("p (k n) -> p k n", k=4)
                for kk in range(4):
                    k = 4 * g + kk
                    src = scs[:, k, :] if k < KD else ylru[:, k - KD, :]
                    for t in range(TC):
                        i = mm(ps[:, 4 * half + t, :], src[:, t * P:(t + 1) * P], w[:, kk, :],
                               start=(k == 0), stop=(k == 2 * KD - 1))
                i.then_inc(sig("out_used"), 1)
            def turn_h(t):
                r = rows_of(t)
                b = 2 * (t % 2)
                if t == 0:
                    pe.wait_ge(sig("x2"), TC)
                pe.wait_ge(sig("h_ready"), t + 1)
                if t >= 2:
                    pe.wait_ge(sig("hT2"), 2 * (t - 1))
                for k in range(KD):
                    i = nc.tensor.transpose(ps[:, b + k // 4, (k % 4) * P:(k % 4) * P + r], h[0:r, t, k * P:(k + 1) * P],
                                            cst("ident", 0, r, r))
                    if k % 4 == 3:
                        i.then_inc(sig("hT2_ps"), 1)

            def z_unit(unit):
                g, t = Z_UNITS[unit]
                wd = (448, 512, 512)[g]
                r = rows_of(t)
                if unit < 4:
                    pe.wait_ge(sig("x2"), TC + unit + 1)
                else:
                    pe.wait_ge(sig("z"), unit - 3)
                if g == 0:
                    pe.wait_ge(sig("hT2"), 2 * t + 2)
                for k in range(KD):
                    if t == 0 and k % 4 == 0:
                        wait_tile(pe, T_IN2 + 2 * g + k // 4)
                    w = tile(T_IN2 + 2 * g + k // 4)[:, 0:4 * wd].rearrange("p (k n) -> p k n", k=4)
                    i = mm(ps[0:r, 4 + unit % 4, 0:wd], hT2[:, k, t * P:t * P + r], w[:, k % 4, :],
                           start=(k == 0), stop=(k == KD - 1))
                i.then_inc(sig("z_ready"), 1)

            def turn_a(t):
                r = rows_of(t)
                pe.wait_ge(sig("rotated"), AT_A + t + 1)
                if t == 0:
                    pe.wait_ge(sig("hT2"), 2 * LC)
                else:
                    pe.wait_ge(sig("turned"), t)
                for j in range(4):
                    if j < 2 and t == TC:
                        continue
                    src = zA[0:r, t, j * P:(j + 1) * P] if j < 3 else pe_rot[0:r, 4 * ROPE:4 * ROPE + P]
                    i = nc.tensor.transpose(ps[:, 0, j * P:j * P + r], src, cst("ident", 0, r, r))
                i.then_inc(sig("turned_ps"), 1)

            def turn_heads(t, n_, src, bank, first):
                r = rows_of(t)
                pe.wait_ge(sig("rotated"), first + t + 1)
                if t >= 1:
                    pe.wait_ge(sig("turned"), first + t)
                for j in range(n_):
                    i = nc.tensor.transpose(ps[:, bank, j * P:j * P + r], src[0:r, j * P:(j + 1) * P], cst("ident", 0, r, r))
                i.then_inc(sig("turned_ps"), 1)

            turn_h(0)
            for t in range(LC):
                if t + 1 < LC:
                    turn_h(t + 1)
                z_unit(t)
            for t in range(LC):
                if t < TC:
                    z_unit(LC + t)
                turn_a(t)
            for t in range(LC):
                z_unit(LC + TC + t)
                if t < TC:
                    turn_heads(t, 4, rot[:, 0:512], 1, AT_B)
            wait_tile(pe, T_Q)
            wq = tile(T_Q)[:, 0:1536].rearrange("p (k n) -> p k n", k=2)
            pe.wait_ge(sig("turned"), LC)
            for j in range(HM):
                pe.wait_ge(sig("z"), 2 * LC + TC - 3 + j)
                for k in range(2):
                    i = mm(ps[:, BANK_QN[j], :], wq[:, k, j * 192:j * 192 + P], qanT[:, k, :], start=(k == 0), stop=(k == 1))
                i.then_inc(sig("qkn_ps"), 1)
            pe.wait_ge(sig("turned"), LC + TC)
            for t in range(TC):
                for k in range(2):
                    i = mm(ps[:, t // 2, t % 2 * 256:(t % 2 + 1) * 256], qanT[:, k, t * P:(t + 1) * P],
                           wq[:, k, :].rearrange("p (h n) -> p h n", h=HM)[:, :, P:192], start=(k == 0), stop=(k == 1))
                i.then_inc(sig("qp_ps"), 1)
            wait_tile(pe, T_KV)
            wkv = tile(T_KV)[:, 0:D]
            for t in range(LC):
                turn_heads(t, 2, rot[:, 512:768], 2 + t % 2, AT_C)
                if t < HM:
                    pe.wait_ge(sig("qkn"), t + 1)
                    mm(ps[:, BANK_QN[t], :], wkv[:, t * 256:t * 256 + P], kvanT[:, 0:T], start=True, stop=True).then_inc(sig("qkn_ps"), 1)
            for j in range(HM):
                i = mm(ps[:, 3, j * META:(j + 1) * META], wkv[:, j * 256:j * 256 + P], kvanT[:, T:L], start=True, stop=True)
            i.then_inc(sig("qkn_ps"), 1)
            for t in range(LC):
                r = rows_of(t)
                if t < TC:
                    pe.wait_ge(sig("qkn"), HM + t + 1)
                else:
                    pe.wait_ge(sig("turned"), 2 * LC + TC)
                bank = BANK_QN[t] if t < TC else 2
                i = mm(ps[0:r, bank, :], kvanT[:, t * P:t * P + r],
                       wkv.rearrange("p (h n) -> p h n", h=HM)[:, :, P:256], start=True, stop=True)
                i.then_inc(sig("vm_ps"), 1)
            for t in range(TC):
                pe.wait_ge(sig("rotated"), AT_QP + t + 1)
                if t < 2:
                    pe.wait_ge(sig("vm"), t + 1)
                else:
                    pe.wait_ge(sig("qpT"), t - 1)
                for j in range(2):
                    i = nc.tensor.transpose(ps[:, BANK_QN[t % 2], j * P:(j + 1) * P], qrot[:, t, j * P:(j + 1) * P], IDENT)
                i.then_inc(sig("qpT_ps"), 1)
            pe.wait_ge(sig("vm"), LC)
            attention(pe)
            for t in range(TC):
                pe.wait_ge(sig("o_norm"), 2 * (t + 1))
                if t >= 2:
                    pe.wait_ge(sig("oT"), 8 * (t - 1))
                for k in range(KD):
                    i = nc.tensor.transpose(ps[:, 2 * (t % 2) + k // 4, (k % 4) * P:(k % 4 + 1) * P], o_tok[:, t, k * P:(k + 1) * P], IDENT)
                i.then_inc(sig("oT_ps"), 1)
            pe.wait_ge(sig("oT"), 8 * TC)
            for n in range(N_O):
                half, g = n // 2, n % 2
                wait_tile(pe, T_O + n)
                w = tile(T_O + n).rearrange("p (k n) -> p k n", k=4)
                for kk in range(4):
                    k = 4 * g + kk
                    for t in range(TC):
                        i = mm(ps[:, 4 * half + t, :], oT[:, k, t * P:(t + 1) * P], w[:, kk, :],
                               start=(k == 0), stop=(k == KD - 1))
                i.then_inc(sig("o_used"), 1)
            for t in range(TC):
                pe.wait_ge(sig("h1_ready"), t + 1)
                if t == 0:
                    pe.wait_ge(sig("mix_taken"), 2 * TC)
                if t >= 2:
                    pe.wait_ge(sig("h1T"), 2 * (t - 1))
                for k in range(KD):
                    i = nc.tensor.transpose(ps[:, 2 * (t % 2) + k // 4, (k % 4) * P:(k % 4 + 1) * P], h1[:, t, k * P:(k + 1) * P], IDENT)
                i.then_inc(sig("h1T_ps"), 1)
            pe.wait_ge(sig("h1T"), 2 * TC)
            pe.wait_ge(sig("router_in"), 16)
            for t in range(TC):
                for k in range(KD):
                    i = mm(ps[:, 2, t * E:(t + 1) * E], h1T[:, k, t * P:(t + 1) * P], wrouter[:, k, :],
                           start=(k == 0), stop=(k == KD - 1))
            i.then_inc(sig("logits_ps"), 1)
            experts(pe)

        @block.scalar
        def _(act):
            A = nc.scalar.activation
            st = Steps(act, sig("act_step"))
            for k in range(KD):
                act.dma_start(hT[:, k, :], a["xT"][k * P:(k + 1) * P, :]).then_inc(sig("xT_in"), 16)
            act.dma_start(gates_w[:, 0:KD, :], a["wr"].rearrange("h d e -> d h e")).then_inc(sig("gates_in"), 16)
            act.dma_start(gates_w[:, KD:, :], a["wi"].rearrange("h d e -> d h e")).then_inc(sig("gates_in"), 16)
            act.dma_start(gate1[:], a["rows"][:, ROWS["gate_b"]:ROWS["gate_b"] + D].partition_broadcast(P)).then_inc(sig("gateb_in"), 16)
            act.wait_ge(sig("chan_in"), 16)
            A(c_sig, ch("c", 0, 8), ACT.Sigmoid).then_inc(sig("c_sig"), 1)
            act.wait_ge(sig("xT_in"), 16 * KD)
            for k in range(KD):
                if k >= 2:
                    act.wait_ge(sig("xsq_summed"), k - 1)
                A(rep[:, k % 2, :], hT[:, k, :], ACT.Square).then_inc(sig("xsq"), 1)
            act.wait_ge(sig("xsq_summed"), KD)
            act.wait_ge(sig("const_in"), 16)
            st.link(A(rep[:, 0, :], ps[:, 4, :], ACT.Ln, bias=cst("eps6")))
            A(rep[:, 1, :], rep[:, 0, :], ACT.Exp, scale=-0.5).then_inc(sig("rstd"), 1)
            act.wait_ge(sig("lam_abs"), 1)
            A(lam_e, lam_abs, ACT.Exp, scale=-1.0).then_inc(sig("lam_exp"), 1)
            act.wait_ge(sig("mod_used"), N_MOD)
            A(mod_row[0:1, 0:D], ps[0:1, 0:2, :].rearrange("p a b -> p (a b)"), ACT.Copy).then_inc(sig("mod_row"), 1)

            def lru_act(j):
                r, ig, s, al = (lru[:, q, :] for q in range(4))
                b = 4 + 2 * (j % 2)
                act.wait_ge(sig("gates_ps"), j + 1)
                if j == 0:
                    act.wait_ge(sig("rate"), 1)
                if j >= 1:
                    act.wait_ge(sig("ylru"), j)
                A(r, ps[:, b, :], ACT.Sigmoid, bias=ch("br", j)).then_inc(sig("gates_taken"), 1)
                A(ig, ps[:, b + 1, :], ACT.Sigmoid, bias=ch("bi", j)).then_inc(sig("gates_taken"), 1)
                act.wait_ge(sig("gates_taken"), 2 * j + 2)
                st.go(A(s, r, ACT.Tanh, scale=rate[:, j:j + 1]))
                A(al, r, ACT.Exp, scale=nrate[:, j:j + 1]).then_inc(sig("a_ready"), 1)
                st.wait()
                act.wait_ge(sig("a_ready"), j + 1)
                st.link(A(r, s, ACT.Ln, bias=cst("tiny")))
                A(s, s, ACT.Ln, bias=ONE).then_inc(sig("logs"), 1)
                act.wait_ge(sig("logd"), j + 1)
                A(r, r, ACT.Exp, scale=0.5, bias=cst("hln2")).then_inc(sig("mult"), 1)

            for n in range(N_IN):
                b = 2 * (n % 2)
                act.wait_ge(sig("u_ready"), 2 * n + 2)
                if n >= 2:
                    act.wait_ge(sig("u_taken"), n - 1)
                A(sgt[:, n % 2, :], ps[:, b + 1, :], ACT.Sigmoid).then_inc(sig("u_sig"), 1)
                if n >= 16:
                    if n < 18:
                        act.wait_ge(sig("ylru"), n - 9)
                    A(lsil[:, n % 2, :], ps[:, b, :], ACT.Sigmoid).then_inc(sig("u_sig2"), 1)
                if 9 <= n <= 16:
                    lru_act(n - 9)
            for k in range(KD):
                act.wait_ge(sig("vcent"), k + 1)
                if k >= 2:
                    act.wait_ge(sig("vsq_summed"), k - 1)
                A(rep[:, k % 2, :], vc[:, k, :], ACT.Square).then_inc(sig("vsq"), 1)
            act.wait_ge(sig("vsq_summed"), KD)
            st.link(A(rep[:, 0, :], ps[:, 5, :], ACT.Ln, bias=cst("eps6")))
            A(rep[:, 1, :], rep[:, 0, :], ACT.Exp, scale=-0.5).then_inc(sig("rstd"), 1)
            act.wait_ge(sig("u_taken"), N_IN)
            for k in range(KD):
                act.wait_ge(sig("vscaled"), k + 1)
                if k >= 2:
                    act.wait_ge(sig("vln"), k - 1)
                A(sgt[:, k % 2, :], vc[:, k, :], ACT.Sigmoid, bias=ch("cln_b", k)).then_inc(sig("v_sig"), 1)
            def norm_h(t):
                if t < TC:
                    act.wait_ge(sig("x2"), TC + t + 1)
                    if t >= 1:
                        act.wait_ge(sig("x2_ss"), t)
                    A(junk, x2[:, t, :], ACT.Square, accum_out=x2_ss[:, t:t + 1]).then_inc(sig("x2_ss"), 1)
                r = rows_of(t)
                act.wait_ge(sig("emb_var"), t + 1)
                st.link(A(emb_ln[0:r, t:t + 1], emb_var[0:r, t:t + 1], ACT.Ln))
                A(emb_rstd[0:r, t:t + 1], emb_ln[0:r, t:t + 1], ACT.Exp, scale=-0.5).then_inc(sig("emb_rstd"), 1)

            def h_out(t):
                r = rows_of(t)
                for q in range(2):
                    act.wait_ge(sig("hT2_ps"), 2 * t + q + 1)
                    A(hT2[:, 4 * q:4 * q + 4, t * P:t * P + r],
                      ps[:, 2 * (t % 2) + q, :].rearrange("p (k n) -> p k n", k=4)[:, :, 0:r], ACT.Copy).then_inc(sig("hT2"), 1)

            def z_out(unit):
                g, t = Z_UNITS[unit]
                r = rows_of(t)
                z, wd = ((zA, 448), (zB, 512), (zC, 512))[g]
                act.wait_ge(sig("z_ready"), unit + 1)
                A(z[0:r, t, :], ps[0:r, 4 + unit % 4, 0:wd], ACT.Copy).then_inc(sig("z"), 1)

            def z_rstd(unit):
                g, t = Z_UNITS[unit]
                c_ = slice(9 * t + (0, 3, 7)[g], 9 * t + (3, 7, 9)[g])
                act.wait_ge(sig("z_ss"), unit + 1)
                st.link(A(z_ln[:, c_], z_ss[:, c_], ACT.Ln, scale=1.0 / P, bias=cst("eps6")))
                A(z_ss[:, c_], z_ln[:, c_], ACT.Exp, scale=-0.5).then_inc(sig("z_rstd"), 1)

            def a_out(t):
                r = rows_of(t)
                tk = slice(t * P, t * P + r)
                act.wait_ge(sig("turned_ps"), AT_A + t + 1)
                if t < TC:
                    for k in range(2):
                        st.go(A(qanT[:, k, tk], ps[:, 0, k * P:(k + 1) * P], ACT.Copy, scale=ch("g_q_a", k)))
                st.link(A(kvanT[:, tk], ps[:, 0, 2 * P:2 * P + r], ACT.Copy, scale=ch("g_kv_a")))
                A(krT[:, tk], ps[:, 0, 3 * P:3 * P + r], ACT.Copy).then_inc(sig("turned"), 1)

            def b_out(t):
                act.wait_ge(sig("turned_ps"), AT_B + t + 1)
                A(qgT[:, :, t * P:(t + 1) * P], ps[:, 1, :].rearrange("p (h n) -> p h n", h=4), ACT.Copy).then_inc(sig("turned"), 1)

            def c_out(t):
                r = rows_of(t)
                act.wait_ge(sig("turned_ps"), AT_C + t + 1)
                A(kgT[:, :, t * P:t * P + r], ps[:, 2 + t % 2, 0:256].rearrange("p (h n) -> p h n", h=2)[:, :, 0:r], ACT.Copy).then_inc(sig("turned"), 1)

            norm_h(0)
            for t in range(LC):
                if t + 1 < LC:
                    norm_h(t + 1)
                h_out(t)
                if t >= 1:
                    z_out(t - 1)
            z_out(TC)
            for t in range(LC):
                z_rstd(t)
            for t in range(LC):
                if t < TC:
                    z_out(LC + t)
                a_out(t)
                if t < TC:
                    z_rstd(LC + t)
            for t in range(LC):
                z_out(LC + TC + t)
                if t < TC:
                    b_out(t)
                z_rstd(LC + TC + t)
            for j in range(HM):
                act.wait_ge(sig("qkn_ps"), j + 1)
                A(qnT[:, j, :], ps[:, BANK_QN[j], :], ACT.Copy).then_inc(sig("qkn"), 1)
            for t in range(LC):
                c_out(t)
                if t < HM:
                    act.wait_ge(sig("qkn_ps"), HM + t + 1)
                    A(knT[:, t, 0:T], ps[:, BANK_QN[t], :], ACT.Copy).then_inc(sig("qkn"), 1)
            act.wait_ge(sig("qkn_ps"), 2 * HM + 1)
            A(knT[:, :, T:L], ps[:, 3, 0:HM * META].rearrange("p (h n) -> p h n", h=HM), ACT.Copy).then_inc(sig("qkn"), 1)
            for t in range(LC):
                r = rows_of(t)
                act.wait_ge(sig("vm_ps"), t + 1)
                A(vm[0:r, t, :], ps[0:r, BANK_QN[t] if t < TC else 2, :], ACT.Copy).then_inc(sig("vm"), 1)
            for t in range(TC):
                act.wait_ge(sig("qpT_ps"), t + 1)
                A(qpT[:, :, t * P:(t + 1) * P], ps[:, BANK_QN[t % 2], 0:256].rearrange("p (h n) -> p h n", h=2), ACT.Copy).then_inc(sig("qpT"), 1)

            def probs(u):
                hh, qt = UNITS[u]
                scale = (NOPE + ROPE) ** -0.5 if hh < HM else P ** -0.5
                act.wait_ge(sig("nmax"), u + 1)
                if u >= 2:
                    act.wait_ge(sig("probT_ps"), u - 1)
                A(pr[:, u % 2, :], ps[:, 2 * (u % 2):2 * (u % 2) + 2, :].rearrange("p a b -> p (a b)")[:, 0:L], ACT.Exp,
                  bias=nmaxs[:, u:u + 1], scale=scale, accum_out=psums[:, u:u + 1]).then_inc(sig("prob"), 1)

            def turned(u):
                act.wait_ge(sig("probT_ps"), u + 1)
                if u >= 2:
                    act.wait_ge(sig("o_ps"), u - 1)
                A(pT[:, u % 2, 0:T], ps[:, 4, :], ACT.Copy).then_inc(sig("probT"), 1)
                A(pT[0:META, u % 2, T:LC * P], ps[0:META, 5, 0:P], ACT.Copy).then_inc(sig("probT"), 1)

            probs(0)
            for u in range(len(UNITS)):
                if u + 1 < len(UNITS):
                    probs(u + 1)
                turned(u)
            for t in range(TC):
                for g in range(2):
                    act.wait_ge(sig("o_taken"), 16 * g + 12 + t + 1)
                    st.link(A(pr[:, g, 0:512], o_tok[:, t, g * 512:(g + 1) * 512], ACT.Square, accum_out=o_ss[:, 2 * t + g:2 * t + g + 1]))
            st.link(A(o_ln, o_ss, ACT.Ln, scale=1.0 / 512, bias=cst("eps6")))
            A(o_rstd, o_ln, ACT.Exp, scale=-0.5).then_inc(sig("o_rstd"), 1)
            for t in range(TC):
                act.wait_ge(sig("oT_ps"), t + 1)
                for k in range(KD):
                    A(oT[:, k, t * P:(t + 1) * P], ps[:, 2 * (t % 2) + k // 4, (k % 4) * P:(k % 4 + 1) * P], ACT.Copy, scale=ch("g_o", k)).then_inc(sig("oT"), 1)
            for t in range(TC):
                act.wait_ge(sig("ln1_var"), t + 1)
                st.link(A(ln_ln[:, t:t + 1], ln_var[:, t:t + 1], ACT.Ln, bias=cst("eps5")))
                A(ln_rstd[:, t:t + 1], ln_ln[:, t:t + 1], ACT.Exp, scale=-0.5).then_inc(sig("ln1_rstd"), 1)
            for t in range(TC):
                act.wait_ge(sig("h1T_ps"), t + 1)
                for q in range(2):
                    A(h1T[:, 4 * q:4 * q + 4, t * P:(t + 1) * P], ps[:, 2 * (t % 2) + q, :].rearrange("p (k n) -> p k n", k=4), ACT.Copy).then_inc(sig("h1T"), 1)
            for t in range(TC):
                act.wait_ge(sig("best"), 1)
                A(gates[:, t, :], v8[:, t, 0:TOPK], ACT.Exp, bias=nv0[:, t:t + 1], accum_out=gsum[:, t:t + 1]).then_inc(sig("gate_exp"), 1)
            act.wait_ge(sig("lists_ps"), 3)
            A(gT[0:E, :], ps[0:E, 5, :], ACT.Copy).then_inc(sig("gT"), 1)

            act.wait_ge(sig("bgu_in"), 32)
            A(bgu[:], bgu_raw[0:2 * E, :], ACT.Copy).then_inc(sig("bgu_hi"), 1)

            def high(x, q, bank, signal):
                A(x[:, 0, 4 * q:4 * q + 4, :], ps[:, bank, :].rearrange("p (k n) -> p k n", k=4), ACT.Copy).then_inc(signal, 1)

            for q in range(2):
                act.wait_ge(sig("xt_ps"), q + 1)
                high(xTs, q, 7 - q, sig("xt_hi"))
            act.wait_ge(sig("list_ready"), 3)
            act.wait_ge(sig("gate_exp"), TC)
            A(unused, ONE, ACT.Sigmoid)
            n_items = act.value_load(nint[0:1, 0:1], min_val=E, max_val=E + 16)

            def output(n):
                act.wait_ge(sig("split_used"), n * CHUNKS + SPLITS)
                act.wait_ge(sig("idxs_ready"), n + 1)
                A(ysb, ps[:, 4:6, :].rearrange("p a b -> p (a b)"), ACT.Copy).then_inc(sig("y_ready"), 1)

            with act.Fori(0, n_items) as i:

                def split_high(lo, hi):
                    for c in range(lo, hi):
                        if c % 2 == 0:
                            j = c // 2
                            act.wait_ge(tile_ready[j % SLOTS], i * 32 + 16 * (loads_before[j % SLOTS] + j // SLOTS + 1))
                        act.wait_ge(sig("split_used"), i * CHUNKS + (c + 1))
                        A(split[:, c % SPLITS, 0, :], chunk(c), ACT.Copy).then_inc(sig("hi_ready"), 1)

                def sigmoid(half):
                    act.wait_ge(sig("glu_ready"), i * 2 + (half + 1))
                    A(gsig[:, half, :], glu[:, half, :], ACT.Sigmoid, scale=SWALPHA).then_inc(sig("gsig_ready"), 1)

                split_high(0, 4)
                output(i)
                split_high(4, 12)
                sigmoid(0)
                split_high(12, 16)
                act.wait_ge(sig("at_ps"), i * 2 + 1)
                high(aTs, 0, 6, sig("at_hi"))
                split_high(16, 19)
                sigmoid(1)
                split_high(19, 20)
                act.wait_ge(sig("xt_ps"), i * 2 + 3)
                high(xTs, 0, 7, sig("xt_hi"))
                split_high(20, 23)
                act.wait_ge(sig("at_ps"), i * 2 + 2)
                high(aTs, 1, 6, sig("at_hi"))
                split_high(23, 24)
                act.wait_ge(sig("xt_ps"), i * 2 + 4)
                high(xTs, 1, 6, sig("xt_hi"))
            output(n_items)
            for t in range(TC):
                act.wait_ge(sig("ln2_var"), t + 1)
                A(ln_ln[:, t:t + 1], ln_var[:, t:t + 1], ACT.Ln, bias=cst("eps5")).then_inc(sig("ln2_log"), 1)
                act.wait_ge(sig("ln2_log"), t + 1)
                A(ln_rstd[:, t:t + 1], ln_ln[:, t:t + 1], ACT.Exp, scale=-0.5).then_inc(sig("ln2_rstd"), 1)

        @block.vector
        def _(dve):
            V = nc.vector
            st = Steps(dve, sig("dve_step"))
            dve.wait_ge(sig("c_sig"), 1)
            V.tensor_tensor(c_act, ch("c", 0, 8), c_sig, ALU.mult).then_inc(sig("c_act"), 1)
            st.link(V.tensor_scalar(lam_neg, ch("lam", 0, 8), -1.0, None, ALU.mult))
            V.tensor_tensor(lam_abs, ch("lam", 0, 8), lam_neg, ALU.max).then_inc(sig("lam_abs"), 1)
            dve.wait_ge(sig("lam_exp"), 1)
            e_, z_, zz, se = lam_e, lam_z, rate, nrate
            st.link(V.tensor_scalar(z_, e_, 2.0, None, ALU.add))
            st.link(V.reciprocal(zz, z_))
            st.link(V.tensor_tensor(z_, zz, e_, ALU.mult))
            st.link(V.tensor_tensor(zz, z_, z_, ALU.mult))
            st.link(V.memset(se, 1.0 / 21))
            for q in range(19, 0, -2):
                st.link(V.tensor_tensor(se, se, zz, ALU.mult))
                st.link(V.tensor_scalar(se, se, 1.0 / q, None, ALU.add))
            st.link(V.tensor_tensor(se, se, z_, ALU.mult))
            st.link(V.tensor_scalar(zz, lam_neg, 0.0, 8.0, ALU.max, ALU.mult))
            st.link(V.tensor_scalar(se, se, 16.0, None, ALU.mult))
            st.link(V.tensor_tensor(zz, zz, se, ALU.add))
            V.tensor_scalar(se, zz, -1.0, None, ALU.mult).then_inc(sig("rate"), 1)
            dve.wait_ge(sig("const_in"), 16)
            for k in range(KD):
                V.tensor_scalar(crep[:, k, :], cst("ones"), c_act[:, k:k + 1], None, ALU.mult).then_inc(sig("crep"), 1)
            dve.wait_ge(sig("rstd"), 1)
            for k in range(KD):
                st.go(V.tensor_tensor(hT[:, k, :], hT[:, k, :], rep[:, 1, :], ALU.mult))
            dve.wait_ge(sig("mod_used"), N_MOD)
            V.tensor_copy(mod_row[0:1, D:2 * D], ps[0:1, 2:4, :].rearrange("p a b -> p (a b)")).then_inc(sig("mod_row"), 1)
            dve.wait_ge(sig("mod_cols"), 1)
            dve.wait_ge(sig("chan_in"), 16)
            st.go(V.tensor_tensor(shift, ps[:, 5, 0:8], ch("mod_b", 0, 8), ALU.add))
            st.link(V.tensor_tensor(gain, ps[:, 5, 8:16], ch("mod_b", 8, 8), ALU.add))
            st.link(V.scalar_tensor_tensor(gain, gain, 1.0, ch("norm_g", 0, 8), ALU.add, ALU.mult))
            for k in range(KD):
                V.tensor_scalar(hT[:, k, :], hT[:, k, :], gain[:, k:k + 1], shift[:, k:k + 1], ALU.mult, ALU.add).then_inc(sig("hT"), 1)

            taps = [(j, q) for j in range(KD) for q in range(TAPS)]
            done = [0]

            def conv_taps(count):
                for _ in range(count):
                    if done[0] == len(taps):
                        return
                    j, q = taps[done[0]]
                    done[0] += 1
                    src = v[:, j, q:q + T]
                    w = ch("dw_w", j * TAPS + q)
                    if q == 0:
                        dve.wait_ge(sig("u_taken"), j + 1)
                        st.link(V.tensor_scalar(vc[:, j, :], src, w, ch("dw_b", j), ALU.mult, ALU.add))
                    else:
                        i = V.scalar_tensor_tensor(vc[:, j, :], src, w, vc[:, j, :], ALU.mult, ALU.add)
                        if q == TAPS - 1:
                            i.then_inc(sig("conv"), 1)
                        else:
                            st.link(i)

            def lru_vec(j):
                r, ig, s, al = (lru[:, q, :] for q in range(4))
                dve.wait_ge(sig("logs"), j + 1)
                V.tensor_tensor(r, r, s, ALU.subtract).then_inc(sig("logd"), 1)
                st.link(V.tensor_tensor(ig, ig, xs[:, j % 2, :], ALU.mult))
                dve.wait_ge(sig("mult"), j + 1)
                dve.wait_ge(sig("a_ready"), j + 1)
                st.link(V.tensor_tensor(ig, ig, r, ALU.mult))
                V.tensor_tensor_scan(s, al, ig, 0.0, ALU.mult, ALU.add).then_inc(sig("scan"), 1)
                dve.wait_ge(sig("scan"), j + 1)
                V.tensor_tensor(ylru[:, j, :], s, lsil[:, j % 2, :], ALU.mult).then_inc(sig("ylru"), 1)

            dve.wait_ge(sig("pads_zero"), 2)
            for n in range(N_IN):
                b = 2 * (n % 2)
                dve.wait_ge(sig("u_ready"), 2 * n + 2)
                dve.wait_ge(sig("u_sig"), n + 1)
                if n < 8:
                    V.tensor_tensor(v[:, n, TAPS - 1:], ps[:, b, :], sgt[:, n % 2, :], ALU.mult).then_inc(sig("u_taken"), 1)
                    conv_taps(21)
                elif n < 16:
                    j = n - 8
                    if j >= 2:
                        dve.wait_ge(sig("ylru"), j - 1)
                    st.go(V.tensor_tensor(lsil[:, j % 2, :], ps[:, b + 1, :], sgt[:, n % 2, :], ALU.mult))
                    V.tensor_copy(lxb[:, j % 2, STAPS - 1:], ps[:, b, :]).then_inc(sig("u_taken"), 1)
                    st.wait()
                    dve.wait_ge(sig("u_taken"), n + 1)
                    x_ = xs[:, j % 2, :]
                    if j == 0:
                        st.wait()
                    st.link(V.tensor_scalar(x_, lxb[:, j % 2, 0:T], ch("sc_w", j * STAPS), ch("sc_b", j), ALU.mult, ALU.add))
                    for q in range(1, STAPS):
                        i = V.scalar_tensor_tensor(x_, lxb[:, j % 2, q:q + T], ch("sc_w", j * STAPS + q), x_, ALU.mult, ALU.add)
                        if q < STAPS - 1:
                            st.link(i)
                    i.then_inc(sig("xs"), 1)
                    conv_taps(6)
                    if j >= 1:
                        lru_vec(j - 1)
                    conv_taps(4)
                else:
                    c = 2 * (n - 16)
                    if n == 16:
                        lru_vec(KD - 1)
                        conv_taps(len(taps))
                    dve.wait_ge(sig("u_sig2"), n - 15)
                    st.go(V.tensor_tensor(scs[:, c, :], ps[:, b, :], lsil[:, n % 2, :], ALU.mult))
                    V.tensor_tensor(scs[:, c + 1, :], ps[:, b + 1, :], sgt[:, n % 2, :], ALU.mult).then_inc(sig("u_taken"), 1)
                    st.wait()
                if n == 18:
                    dve.wait_ge(sig("mean_ps"), 1)
                    for k in range(KD):
                        V.tensor_tensor(vc[:, k, :], vc[:, k, :], ps[:, 4, :], ALU.subtract).then_inc(sig("vcent"), 1)
            dve.wait_ge(sig("rstd"), 2)
            for k in range(KD):
                V.scalar_tensor_tensor(vc[:, k, :], vc[:, k, :], ch("cln_g", k), rep[:, 1, :], ALU.mult, ALU.mult).then_inc(sig("vscaled"), 1)
            for k in range(KD):
                dve.wait_ge(sig("v_sig"), k + 1)
                V.scalar_tensor_tensor(vc[:, k, :], vc[:, k, :], ch("cln_b", k), sgt[:, k % 2, :], ALU.add, ALU.mult).then_inc(sig("vln"), 1)
            dve.wait_ge(sig("gateb_in"), 16)
            dve.wait_ge(sig("gate_used"), N_GATE)
            for q in range(2):
                V.scalar_tensor_tensor(gate1[:, q * 512:(q + 1) * 512], ps[:, 6 + q, :], 1.0, gate1[:, q * 512:(q + 1) * 512],
                                       ALU.add, ALU.add).then_inc(sig("gate1"), 1)
            for m in range(KD):
                dve.wait_ge(sig("pw2_ready"), m + 1)
                V.scalar_tensor_tensor(scs[:, m, :], ps[:, m % 4, :], ch("pw2_b", m), scs[:, m, :], ALU.add, ALU.mult).then_inc(sig("yconv"), 1)
            dve.wait_ge(sig("xtok_in"), 16)
            dve.wait_ge(sig("gate1"), 2)
            def add_y(half, t):
                c_ = slice(half * 512, (half + 1) * 512)
                tmp = rep[:, t % 2, :]
                st.link(V.tensor_tensor(tmp, ps[:, 4 * half + t, :], gate1[:, c_], ALU.mult))
                V.tensor_tensor(x2[:, t, c_], x2[:, t, c_], tmp, ALU.add).then_inc(sig("x2"), 1)

            dve.wait_ge(sig("out_used"), 4)
            for t in range(TC):
                add_y(0, t)
            dve.wait_ge(sig("out_used"), 8)
            dve.wait_ge(sig("rows1_in"), 16)

            def norm_stats(t):
                r = rows_of(t)
                if t < TC:
                    add_y(1, t)
                    dve.wait_ge(sig("x2"), TC + t + 1)
                    st.link(V.tensor_tensor(h[:, t, :], x2[:, t, :], rows1[:, 0, :], ALU.mult))
                else:
                    dve.wait_ge(sig("meta_in"), 16)
                for q in range(2):
                    st.go(V.bn_stats(bn_part[0:r, t, 6 * q:6 * q + 6], h[0:r, t, q * 512:(q + 1) * 512]))
                st.wait()
                st.link(V.bn_aggr(bn_mv[0:r, t, :], bn_part[0:r, t, :]))
                v_ = emb_var[0:r, t:t + 1]
                if t < TC:
                    dve.wait_ge(sig("x2_ss"), t + 1)
                    st.link(V.tensor_scalar(v_, x2_ss[:, t:t + 1], EPS_LN2 / D, EPS_LN2 * EPS_RMS, ALU.mult, ALU.add))
                    V.tensor_tensor(v_, v_, bn_mv[:, t, 1:2], ALU.add).then_inc(sig("emb_var"), 1)
                else:
                    V.tensor_scalar(v_, bn_mv[0:r, t, 1:2], EPS_LN2, None, ALU.add).then_inc(sig("emb_var"), 1)

            def norm_apply(t):
                r = rows_of(t)
                dve.wait_ge(sig("emb_rstd"), t + 1)
                st.link(V.tensor_scalar(h[0:r, t, :], h[0:r, t, :], bn_mv[0:r, t, 0:1], emb_rstd[0:r, t:t + 1], ALU.subtract, ALU.mult))
                V.tensor_tensor(h[0:r, t, :], h[0:r, t, :], rows1[0:r, 1, :], ALU.mult).then_inc(sig("h_scaled"), 1)

            ss = z_ss.rearrange("p (t s) -> p t s", t=LC)
            sq = qnT.rearrange("p a b -> p (a b)")[:, 0:512]
            st.link(V.memset(z_ss, 1.0))
            norm_stats(0)
            for t in range(LC):
                if t + 1 < LC:
                    norm_stats(t + 1)
                norm_apply(t)

            def z_sums(unit):
                g, t = Z_UNITS[unit]
                r = rows_of(t)
                z, n_, at = ((zA, 3, 0), (zB, 4, 3), (zC, 2, 7))[g]
                dve.wait_ge(sig("z"), unit + 1)
                x = z[0:r, t, 0:n_ * P]
                st.link(V.tensor_tensor(sq[0:r, 0:n_ * P], x, x, ALU.mult))
                i = V.tensor_reduce(ss[0:r, t, at:at + n_], sq[0:r, 0:n_ * P].rearrange("p (g n) -> p g n", g=n_), AX.X, ALU.add)
                if g == 0:
                    st.link(i)
                    st.link(V.tensor_tensor(ss[0:r, t, 0:1], ss[0:r, t, 0:1], ss[0:r, t, 1:2], ALU.add))
                    i = V.tensor_scalar(ss[0:r, t, 0:1], ss[0:r, t, 0:1], 0.5, None, ALU.mult)
                i.then_inc(sig("z_ss"), 1)

            rope = rtmp[:, 0, :]
            rope2 = rtmp[:, 1, :]

            def rotate(dst1, dst2, x1, x2_, cos, sin, t1, t2, signal=None):
                st.go(V.tensor_tensor(t1, x1, cos, ALU.mult))
                st.link(V.tensor_tensor(t2, x2_, sin, ALU.mult))
                st.link(V.tensor_tensor(dst1, t1, t2, ALU.subtract))
                st.go(V.tensor_tensor(t1, x1, sin, ALU.mult))
                st.link(V.tensor_tensor(t2, x2_, cos, ALU.mult))
                i = V.tensor_tensor(dst2, t1, t2, ALU.add)
                if signal is None:
                    st.link(i)
                else:
                    i.then_inc(signal, 1)

            def rotate_a(t):
                r = rows_of(t)
                dve.wait_ge(sig("z_rstd"), t + 1)
                if t >= 1:
                    dve.wait_ge(sig("turned_ps"), t)
                if t < TC:
                    st.go(V.tensor_scalar(zA[0:r, t, 0:256], zA[0:r, t, 0:256], ss[0:r, t, 0:1], None, ALU.mult))
                st.go(V.tensor_scalar(zA[0:r, t, 256:384], zA[0:r, t, 256:384], ss[0:r, t, 2:3], None, ALU.mult))
                c1, s1 = tab[0:r, t, 0:32], tab[0:r, t, 32:64]
                kr = pe_rot[0:r, 4 * ROPE:4 * ROPE + P]
                x1, x2_ = zA[0:r, t, 384:416], zA[0:r, t, 416:448]
                rotate(kr[:, 0:32], kr[:, 32:64], x1, x2_, c1, s1, rope[0:r, 0:32], rope2[0:r, 0:32])
                V.tensor_copy(kr[:, 64:128], kr[:, 0:64]).then_inc(sig("rotated"), 1)

            def rotate_heads(unit):
                g, t = Z_UNITS[unit]
                r = rows_of(t)
                z, n_, at, col0, first = ((zB, 4, 0, 0, AT_B), (zC, 2, 4, P, AT_C))[g - 1]
                dve.wait_ge(sig("z_rstd"), unit + 1)
                if t >= 1:
                    dve.wait_ge(sig("turned_ps"), first + t)
                for q in range(n_):
                    st.go(V.scalar_tensor_tensor(z[0:r, t, q * P:(q + 1) * P], z[0:r, t, q * P:(q + 1) * P], ss[0:r, t, 3 + at + q:4 + at + q],
                                                 qk_rows[0:r, col0:col0 + P], ALU.mult, ALU.mult))
                st.wait()
                zz_ = z[0:r, t, 0:n_ * P].rearrange("p (h a b n) -> p h a b n", h=n_, a=2, b=2)
                rr = rot[0:r, at * P:(at + n_) * P].rearrange("p (h a b n) -> p h a b n", h=n_, a=2, b=2)
                t1 = rope[0:r, 0:n_ * 64].rearrange("p (h a n) -> p h a n", h=n_, a=2)
                t2 = rope2[0:r, 0:n_ * 64].rearrange("p (h a n) -> p h a n", h=n_, a=2)
                cc = tab[0:r, t, 64:128].rearrange("p (o a n) -> p o a n", o=1, a=2).to_broadcast([r, n_, 2, 32])
                sn = tab[0:r, t, 128:192].rearrange("p (o a n) -> p o a n", o=1, a=2).to_broadcast([r, n_, 2, 32])
                rotate(rr[:, :, :, 0, :], rr[:, :, :, 1, :], zz_[:, :, :, 0, :], zz_[:, :, :, 1, :], cc, sn, t1, t2, sig("rotated"))

            for t in range(LC):
                z_sums(t)
            dve.wait_ge(sig("tab_in"), 32)
            dve.wait_ge(sig("rows2_in"), 16)
            for t in range(LC):
                rotate_a(t)
                dve.wait_ge(sig("rotated"), AT_A + t + 1)
                if t < TC:
                    z_sums(LC + t)
            for t in range(LC):
                if t < TC:
                    rotate_heads(LC + t)
                    dve.wait_ge(sig("rotated"), AT_B + t + 1)
                z_sums(LC + TC + t)
            for t in range(LC):
                rotate_heads(LC + TC + t)
                dve.wait_ge(sig("rotated"), AT_C + t + 1)
            for t in range(TC):
                dve.wait_ge(sig("qp_ps"), t + 1)
                qv = ps[:, t // 2, t % 2 * 256:(t % 2 + 1) * 256].rearrange("p (h b n) -> p h b n", h=HM, b=2)
                dv = qrot[:, t, :].rearrange("p (h b n) -> p h b n", h=HM, b=2)
                c1 = tab[:, t, 0:32].rearrange("p (o n) -> p o n", o=1).to_broadcast([P, HM, 32])
                s1 = tab[:, t, 32:64].rearrange("p (o n) -> p o n", o=1).to_broadcast([P, HM, 32])
                t1 = rope[:, 0:128].rearrange("p (h n) -> p h n", h=HM)
                t2 = rope2[:, 0:128].rearrange("p (h n) -> p h n", h=HM)
                rotate(dv[:, :, 0, :], dv[:, :, 1, :], qv[:, :, 0, :], qv[:, :, 1, :], c1, s1, t1, t2, sig("rotated"))
                dve.wait_ge(sig("rotated"), AT_QP + t + 1)

            def nmax(u):
                hh, qt = UNITS[u]
                scale = (NOPE + ROPE) ** -0.5 if hh < HM else P ** -0.5
                dve.wait_ge(sig("scores_ps"), u + 1)
                st.link(V.tensor_reduce(nmaxs[:, u:u + 1], ps[:, 2 * (u % 2):2 * (u % 2) + 2, :].rearrange("p a b -> p (a b)")[:, 0:L],
                                        AX.X, ALU.max))
                V.tensor_scalar(nmaxs[:, u:u + 1], nmaxs[:, u:u + 1], -scale, None, ALU.mult).then_inc(sig("nmax"), 1)

            def output(u):
                hh, qt = UNITS[u]
                dve.wait_ge(sig("prob"), u + 1)
                st.link(V.reciprocal(psums[:, u:u + 1], psums[:, u:u + 1]))
                dve.wait_ge(sig("o_ps"), u + 1)
                V.tensor_scalar(o_tok[:, qt, hh * P:(hh + 1) * P], ps[:, 6 + u % 2, 0:P], psums[:, u:u + 1], None, ALU.mult).then_inc(sig("o_taken"), 1)

            nmax(0)
            nmax(1)
            for u in range(len(UNITS)):
                if u + 2 < len(UNITS):
                    nmax(u + 2)
                output(u)
            dve.wait_ge(sig("o_rstd"), 1)
            dve.wait_ge(sig("o_taken"), 32)
            for t in range(TC):
                for g in range(2):
                    V.tensor_scalar(o_tok[:, t, g * 512:(g + 1) * 512], o_tok[:, t, g * 512:(g + 1) * 512],
                                    o_rstd[:, 2 * t + g:2 * t + g + 1], None, ALU.mult).then_inc(sig("o_norm"), 1)
            def mix(half, t):
                c_ = slice(half * 512, (half + 1) * 512)
                V.scalar_tensor_tensor(h1[:, t, c_], h[:, t, c_], ALPHA, ps[:, 4 * half + t, :], ALU.mult, ALU.add).then_inc(sig("mix_taken"), 1)

            def ln1_apply(t):
                dve.wait_ge(sig("ln1_rstd"), t + 1)
                st.link(V.tensor_scalar(h1[:, t, :], h1[:, t, :], bn_mv[:, t, 0:1], ln_rstd[:, t:t + 1], ALU.subtract, ALU.mult))
                V.tensor_tensor(h1[:, t, :], h1[:, t, :], ln_rows[:, 0, :], ALU.mult).then_inc(sig("h_scaled"), 1)

            dve.wait_ge(sig("o_used"), 2)
            for t in range(TC):
                mix(0, t)
            dve.wait_ge(sig("ln1_rows_in"), 32)
            dve.wait_ge(sig("o_used"), 4)
            for t in range(TC):
                mix(1, t)
                dve.wait_ge(sig("mix_taken"), TC + t + 1)
                for q in range(2):
                    st.go(V.bn_stats(bn_part[:, t, 6 * q:6 * q + 6], h1[:, t, q * 512:(q + 1) * 512]))
                st.wait()
                st.link(V.bn_aggr(bn_mv[:, t, :], bn_part[:, t, :]))
                V.tensor_copy(ln_var[:, t:t + 1], bn_mv[:, t, 1:2]).then_inc(sig("ln1_var"), 1)
                if t >= 1:
                    ln1_apply(t - 1)
            ln1_apply(TC - 1)
            dve.wait_ge(sig("logits_ps"), 1)
            st.link(V.tensor_tensor(logit, ps[:, 2, 0:TC * E].rearrange("p (t e) -> p t e", t=TC),
                                    qk_rows[:, 2 * P:2 * P + E].rearrange("p (o e) -> p o e", o=1).to_broadcast([P, TC, E]), ALU.add))
            for t in range(TC):
                st.link(V.max(v8[:, t, :], logit[:, t, :]))
                st.go(V.max_index(i8[:, t, :], v8[:, t, :], logit[:, t, :]))
            st.wait()
            V.tensor_scalar(nv0.rearrange("p (t o) -> p t o", o=1), v8[:, :, 0:1], -1.0, None, ALU.mult).then_inc(sig("best"), 1)
            st.link(V.tensor_copy(if4.rearrange("p (t k) -> p t k", t=TC), i8[:, :, 0:TOPK]))

            def spread(x, n):
                return x.rearrange("p (m o) -> p m o", o=1).to_broadcast([P, x.shape[1], n])

            st.link(V.tensor_tensor(mk, cst("iota", 0, E).rearrange("p (o e) -> p o e", o=1).to_broadcast([P, TC * TOPK, E]),
                                    spread(if4, E), ALU.is_equal))

            def over_k(x):
                return x.rearrange("p (t k) e -> p t e k", t=TC)

            V.tensor_reduce(routed, over_k(mk), AX.X, ALU.add).then_inc(sig("masks"), 1)
            st.link(V.tensor_tensor(mkt, mk, spread(cst("dst"), E), ALU.mult))
            st.link(V.tensor_reduce(dst, over_k(mkt), AX.X, ALU.add))
            dve.wait_ge(sig("gate_exp"), TC)
            st.link(V.reciprocal(gsum, gsum))
            st.link(V.tensor_tensor(gates, gates, spread(gsum, TOPK), ALU.mult))
            st.link(V.tensor_tensor(mkt, mk, spread(gates.rearrange("p t k -> p (t k)"), E), ALU.mult))
            V.tensor_reduce(gmat, over_k(mkt), AX.X, ALU.add).then_inc(sig("masks"), 1)
            dve.wait_ge(sig("lists_ps"), 1)
            dve.wait_ge(sig("masks"), 1)
            st.link(V.scalar_tensor_tensor(posm.rearrange("p t e -> p (t e)"), ps[:, 3, 0:TC * E], 1.0, routed.rearrange("p t e -> p (t e)"), ALU.add, ALU.mult))
            st.go(V.tensor_scalar(posm, posm, -1.0, None, ALU.add))
            for t in range(3):
                st.go(V.tensor_scalar(flags[:, :, t], ps[:, 3, TC * E:(TC + 1) * E], float(P * (t + 1)), None, ALU.is_gt))
            st.link(V.tensor_scalar(dcur[:, :, 0], cst("tok"), -NONE, None, ALU.add))

            class ItemSteps:
                def __init__(self, i, per, before):
                    self.i, self.per, self.before, self.n = i, per, before, 0

                def link(self, ins):
                    self.n += 1
                    ins.then_inc(sig("item_step"), 1)
                    dve.wait_ge(sig("item_step"), self.i * self.per + (self.before + self.n))

            PER = 2

            def slots_of(m, s):
                s.link(V.tensor_copy(cur.rearrange("p (t o) -> p t o", o=1), posm[:, :, m:m + 1]))
                s.link(V.tensor_copy(dcur[:, :, 1:2], dst[:, :, m:m + 1]))
                one_hot()

            def one_hot():
                V.tensor_tensor(oh, cst("iota").rearrange("p (o e) -> p o e", o=1).to_broadcast([P, TC, P]), spread(cur, P),
                                ALU.is_equal).then_inc(sig("oh_ready"), 1)

            def row_numbers(signal):
                V.tensor_scalar(idx_2[:], ps[:, 4, 1:2], NONE, None, ALU.add).then_inc(sig("idx2_ready"), 1)
                V.tensor_scalar(idx_g[:], ps[:, 4, 0:1], NONE, None, ALU.add).then_inc(signal, 1)

            def low(x, q, bank, signal):
                V.tensor_tensor(x[:, 1, 4 * q:4 * q + 4, :], ps[:, bank, :].rearrange("p (k n) -> p k n", k=4),
                                x[:, 0, 4 * q:4 * q + 4, :], ALU.subtract).then_inc(signal, 1)

            s = ItemSteps(0, 0, 0)
            slots_of(0, s)
            fl = flags.rearrange("p e t -> p (e t)")
            st.link(V.tensor_tensor_scan(fsum, cst("ones", 0, 96), fl, 0.0, ALU.mult, ALU.add))
            st.link(V.scalar_tensor_tensor(feq, fsum, cst("part1"), fl, ALU.is_equal, ALU.mult))
            st.link(V.tensor_tensor(ftmp, feq, cst("over_e"), ALU.mult))
            st.link(V.tensor_reduce(ev, ftmp, AX.X, ALU.add))
            st.link(V.tensor_tensor(ftmp, feq, cst("over_t"), ALU.mult))
            st.link(V.tensor_reduce(tv, ftmp, AX.X, ALU.add))
            st.link(V.tensor_scalar(tv, tv, NONE, None, ALU.add))
            for q, x in enumerate((ev, tv)):
                V.tensor_scalar(evb[:, q, :], cst("ones"), x, None, ALU.mult).then_inc(sig("over_ready"), 1)
            dve.wait_ge(sig("idx_ps"), 1)
            row_numbers(sig("idx0_ready"))
            st.go(V.tensor_copy(elist[:, 0:E], cst("iota", 0, E)))
            st.go(V.memset(tlist[:, 0:E], 0.0))
            dve.wait_ge(sig("lists_ps"), 2)
            st.go(V.tensor_copy(elist[:, E:2 * E], ps[:, 3, 0:E]))
            V.tensor_copy(tlist[:, E:2 * E], ps[:, 3, E:2 * E]).then_inc(sig("list_ready"), 1)
            st.wait()
            V.tensor_copy(eint[0:1, :], elist[0:1, :]).then_inc(sig("list_ready"), 1)
            V.tensor_scalar(nint[0:1, :], fsum[0:1, 95:96], float(E), None, ALU.add).then_inc(sig("list_ready"), 1)
            dve.wait_ge(sig("h1_stored"), 16 * TC)
            for c in range(TC):
                for q in range(2):
                    dve.wait_ge(sig("bdown_ps"), 2 * c + q + 1)
                    x = h1[:, c, q * 512:(q + 1) * 512]
                    V.scalar_tensor_tensor(x, x, ALPHA, ps[:, 4 + 2 * (c % 2) + q, :], ALU.mult, ALU.add).then_inc(sig("acc"), 1)
            dve.wait_ge(sig("list_ready"), 3)

            dve.wait_ge(sig("bgu_hi"), 1)
            V.tensor_tensor(bgu[E:2 * E, :], bgu_raw[E:2 * E, :], bgu[E:2 * E, :], ALU.subtract).then_inc(sig("bgu_lo"), 1)
            V.memset(idx_s[:], int(NONE)).then_inc(sig("idxs_ready"), 1)
            V.memset(glu[:, 0, 0:1], 0.0).then_inc(sig("lin_ready"), 2)
            V.memset(glu[:, 1, 0:1], 0.0).then_inc(sig("at_lo"), 2)
            both_rows(V.tensor_tensor, 0)
            slots_of(1, s)
            before = s.n
            for q in range(2):
                dve.wait_ge(sig("xt_hi"), q + 1)
                low(xTs, q, 7 - q, sig("xt_lo"))
            dve.wait_ge(sig("lin_ready"), 2)
            dve.wait_ge(sig("at_lo"), 2)
            n_items = dve.value_load(nint[0:1, 0:1], min_val=E, max_val=E + 16)
            with dve.Fori(0, n_items) as i:
                s = ItemSteps(i, PER, before)

                def split_low(lo, hi):
                    for c in [x for x in range(lo, hi) if x not in BY_POOL]:
                        dve.wait_ge(sig("hi_ready"), i * CHUNKS + (c + 1))
                        low_chunk(V.tensor_tensor, i, c)

                def swiglu(half):
                    dve.wait_ge(sig("split_used"), i * CHUNKS + (8 * (half + 1) + SPLITS))
                    gu = ps[:, 2 * half:2 * half + 2, :].rearrange("p b (n o) -> p (b n) o", o=2)
                    g_, a_ = glu[:, half, :], actv[:, half * 512:(half + 1) * 512]
                    V.tensor_scalar(g_, gu[:, :, 0], LIMIT, None, ALU.min).then_inc(sig("glu_ready"), 1)
                    V.tensor_scalar(a_, gu[:, :, 1], LIMIT, -LIMIT, ALU.min, ALU.max).then_inc(sig("lin_ready"), 1)
                    dve.wait_ge(sig("lin_ready"), i * 2 + (half + 3))
                    dve.wait_ge(sig("glu_ready"), i * 2 + (half + 1))
                    s.link(V.scalar_tensor_tensor(a_, a_, 1.0, g_, ALU.add, ALU.mult))
                    dve.wait_ge(sig("gsig_ready"), i * 2 + (half + 1))
                    V.tensor_tensor(a_, a_, gsig[:, half, :], ALU.mult).then_inc(sig("act_ready"), 1)

                split_low(0, 12)
                dve.wait_ge(sig("scattered"), i * 16 + 16)
                dve.wait_ge(sig("idx2_ready"), i + 1)
                V.tensor_copy(idx_s[:], idx_2[:]).then_inc(sig("idxs_ready"), 1)
                dve.wait_ge(sig("idxs_ready"), i + 2)
                dve.wait_ge(sig("idx_ps"), i + 2)
                dve.wait_ge(sig("gathered"), i * 16 + 16)
                row_numbers(sig("idx_ready"))
                swiglu(0)
                split_low(12, 16)
                dve.wait_ge(sig("at_hi"), i * 2 + 1)
                low(aTs, 0, 6, sig("at_lo"))
                split_low(16, 18)
                swiglu(1)
                split_low(18, 21)
                dve.wait_ge(sig("xt_hi"), i * 2 + 3)
                low(xTs, 0, 7, sig("xt_lo"))
                dve.wait_ge(sig("at_hi"), i * 2 + 2)
                low(aTs, 1, 6, sig("at_lo"))
                split_low(21, 24)
                dve.wait_ge(sig("xt_hi"), i * 2 + 4)
                low(xTs, 1, 6, sig("xt_lo"))
                dve.wait_ge(sig("cur_ready"), i + 1)
                one_hot()
                assert s.n == PER, s.n
            dve.wait_ge(sig("acc"), 2 * TC)
            dve.wait_ge(sig("rows3_in"), 32)
            def last_norm(t):
                dve.wait_ge(sig("ln2_rstd"), t + 1)
                st.link(V.tensor_scalar(h1[:, t, :], h1[:, t, :], bn_mv[:, t, 0:1], ln_rstd[:, t:t + 1], ALU.subtract, ALU.mult))
                i = V.tensor_tensor(h1[:, t, :], h1[:, t, :], ln_rows[:, 0, :], ALU.mult)
                if t < TC - 1:
                    i.then_inc(sig("h_scaled"), 1)
                else:
                    st.link(i)
                    dve.wait_ge(sig("out_ready"), TC - 1)
                    V.tensor_tensor(h1[:, t, :], h1[:, t, :], ln_rows[:, 1, :], ALU.add).then_inc(sig("out_ready"), 1)

            for t in range(TC):
                dve.wait_ge(sig(f"y{t}_in"), 16 * TOPK)
                for k in range(TOPK):
                    st.link(V.scalar_tensor_tensor(h1[:, t, :], ybuf[t * TOPK + k], gates[:, t, k:k + 1], h1[:, t, :], ALU.mult, ALU.add))
                for q in range(2):
                    st.go(V.bn_stats(bn_part[:, t, 6 * q:6 * q + 6], h1[:, t, q * 512:(q + 1) * 512]))
                st.wait()
                st.link(V.bn_aggr(bn_mv[:, t, :], bn_part[:, t, :]))
                V.tensor_copy(ln_var[:, t:t + 1], bn_mv[:, t, 1:2]).then_inc(sig("ln2_var"), 1)
                if t >= 1:
                    last_norm(t - 1)
            last_norm(TC - 1)



def _chunks(v):
    return v.reshape(-1, P).T


def _tables():
    import numpy as np

    f = np.float32
    inv = (f(10000.0) ** (-np.arange(0, 64, 2, dtype=f) / f(64))).astype(f)
    pos = np.concatenate([np.arange(META, L), np.arange(META)])
    row = np.concatenate([np.repeat(np.arange(T // 64), 64), np.full(META, -1)])
    colm = np.concatenate([np.tile(np.arange(64), T // 64), np.arange(META)])
    ang = [(p.astype(f)[:, None] * inv[None, :]).astype(f) for p in (pos, row, colm)]
    cos, sin = [np.cos(x).astype(f) for x in ang], [np.sin(x).astype(f) for x in ang]
    return np.ascontiguousarray(np.concatenate([cos[0], sin[0], cos[1], cos[2], sin[1], sin[2]], axis=1), dtype=f)


def _constants():
    import numpy as np

    c = np.zeros((P, NCONST), np.float32)

    def put(name, value):
        o, n = CONST[name]
        c[:, o:o + n] = value

    p = np.arange(P)
    put("ident", np.eye(P))
    put("ones", 1.0)
    put("mean", 1.0 / D)
    put("before", (p[:, None] < p[None, :]))
    put("iota", p[None, :])
    put("over_e", np.repeat(np.arange(E), 3)[None, :])
    put("over_t", (np.tile([1, 2, 3], E) * P - NONE)[None, :])
    t, k = np.divmod(np.arange(16), TOPK)
    put("dst", k[None, :] * T + t[None, :] * P + p[:, None] - NONE)
    put("part1", p[:, None] + 1)
    put("tok", np.arange(TC)[None, :] * P + p[:, None])
    put("eps6", EPS_RMS)
    put("eps5", EPS_LN2)
    put("hln2", 0.5 * math.log(2.0))
    put("tiny", 1e-37)
    put("one", 1.0)
    return c


def kernel(**inputs):
    import numpy as np
    import concourse.bacc as bacc
    from concourse.bass_utils import run_bass_kernel_spmd

    x = {k: np.asarray(v) for k, v in inputs.items()}
    arrays = {"x": x["x"][0], "xT": x["x"][0].T, "meta_tokens_2": x["meta_tokens_2"], "tab": _tables(), "const": _constants()}
    per_channel = {"c": x["c"][0], "norm_g": x["norm_g"][0], "mod_b": x["mod_b"][0][:2 * D], "lam": x["lam"][0]}
    for k in ("cln_g", "cln_b", "pw2_b", "sc_b", "br", "bi", "dw_b"):
        per_channel[k] = x[k][0]
    per_channel["g_q_a"], per_channel["g_kv_a"] = x["g_q_a_2"][0], x["g_kv_a_2"][0]
    per_channel["g_o"] = np.concatenate([x["g_o_mla_2"][0], x["g_o_gqa_2"][0]])
    chan = np.zeros((P, NCHAN), np.float32)
    for k, (o, n) in CHAN.items():
        if k in ("sc_w", "dw_w"):
            chan[:, o:o + n] = x[k][0].T.reshape(KD, P, -1).transpose(1, 0, 2).reshape(P, n)
        else:
            chan[:, o:o + n] = _chunks(per_channel[k])
    arrays["chan"] = chan
    arrays["rows"] = np.concatenate([x["mod_b"][0][2 * D:], x["final_g"], x["ln_emb_g_2"], x["ln_emb_b_2"], x["ln1_g_2"][0], x["ln1_b_2"][0],
                                     x["g_q_gqa_2"][0], x["g_k_gqa_2"][0], x["b_router_2"][0], x["ln2_g_2"][0], x["ln2_b_2"][0]])[None, :]
    w = x["w_in"][0].reshape(KD, P, 5 * KD, P)
    cv, cg, cs, lx, ls = (np.arange(KD) + KD * i for i in range(5))
    pairs = np.stack([np.concatenate([cv, lx, cs[0::2]]), np.concatenate([cg, ls, cs[1::2]])], 1)
    arrays["w_in"] = w[:, :, pairs, :].transpose(2, 1, 0, 3, 4).reshape(N_IN, P, TILE)
    for k in ("mod_w", "pw2_w", "w_out", "wr", "wi", "w_in_2", "w_q_b_2", "w_kv_b_2", "w_o_2", "w_router_2", "w_gate_up_2", "b_gate_up_2",
              "w_down_2", "b_down_2"):
        arrays[k] = x[k][0]
    nc = bacc.Bacc("TRN2", target_bir_lowering=False, num_devices=1)
    feeds, a = {}, {}
    for k, v in arrays.items():
        feeds[f"in_{k}"] = np.ascontiguousarray(v)
        a[k] = nc.dram_tensor(f"in_{k}", feeds[f"in_{k}"].shape, F32, kind="ExternalInput").ap()
    h1_dram = nc.dram_tensor("h1_rows", (T, D), F32, kind="Internal").ap()
    y_dram = nc.dram_tensor("y_rows", (TOPK * T, D), F32, kind="Internal").ap()
    out = nc.dram_tensor("out_0", (T, D), F32, kind="ExternalOutput").ap()
    program(nc, a, out, h1_dram, y_dram)
    r = run_bass_kernel_spmd(nc, [feeds], core_ids=[0])
    return r.results[0]["out_0"].reshape(1, T, D)
```
